# Optimizing a Trainium2 kernel written in Bass

```python
import math
import jax, jax.numpy as jnp
from jax import lax
import numpy as np

D_MODEL = 1024
BATCH = 1
SEQ = 256
DEPTH = 2

GRID_W = 64
CTX_LEN = 256
EPS = 1e-6
N_HEADS = 8
Q_LORA = 384
KV_LORA = 256
QK_NOPE = 64
QK_ROPE = 32
V_HEAD = 64
ROPE_BASE = 10000.0
Q_BLOCK = 128
ATTN_SCALE = (QK_NOPE + QK_ROPE) ** -0.5
HY_WIDTH = 512
HY_EMB = 17
HY_FILTER_HIDDEN = 64
HY_DECAY_MIN = -math.log(1e-2) / 1.5
HY_DECAY_MAX = -math.log(1e-2) / 0.3
D_FF = 2816
N_EXPERTS = 8
TOP_K = 2
N_DENSE = (DEPTH + 1) // 2
N_MOE = DEPTH // 2
KV_START = Q_LORA
HY_START = KV_START + KV_LORA + QK_ROPE
GATE_START = HY_START + 3 * HY_WIDTH
IN_COLS = GATE_START + 2 * D_MODEL


def rmsnorm(x, g):
    xf = x.astype(jnp.float32)
    xf = xf * lax.rsqrt(jnp.mean(xf * xf, axis=-1, keepdims=True) + EPS)
    return xf.astype(x.dtype) * g

def adaln(cond, w, b, n_chunks):
    return jnp.split(jax.nn.silu(cond) @ w + b, n_chunks, axis=-1)

def axial_rope_tables(rows, dtype):
    n_freq = QK_ROPE // 4
    inv_freq = ROPE_BASE ** (-jnp.arange(n_freq, dtype=jnp.float32) / n_freq)
    r = jnp.repeat(jnp.arange(rows, dtype=jnp.float32), GRID_W)
    col = jnp.tile(jnp.arange(GRID_W, dtype=jnp.float32), rows)
    ang = jnp.concatenate([r[:, None] * inv_freq, col[:, None] * inv_freq], axis=-1)
    return jnp.cos(ang).astype(dtype), jnp.sin(ang).astype(dtype)

def apply_rope(v, cos, sin):
    half = QK_ROPE // 2
    a, b = v[..., :half], v[..., half:]
    return jnp.concatenate([a * cos - b * sin, b * cos + a * sin], axis=-1)

def mla_queries(p_q, q_norm_g, w_uq, rope):
    bsz, n, _ = p_q.shape
    q = (rmsnorm(p_q, q_norm_g) @ w_uq).reshape(bsz, n, N_HEADS, QK_NOPE + QK_ROPE)
    if rope is None:
        return q
    cos, sin = rope
    return jnp.concatenate([q[..., :QK_NOPE], apply_rope(q[..., QK_NOPE:], cos[:, None], sin[:, None])], axis=-1)

def mla_keys_values(p_kv, kv_norm_g, w_uk, w_uv, rope):
    bsz, n, _ = p_kv.shape
    c_kv = rmsnorm(p_kv[..., :KV_LORA], kv_norm_g)
    k_rope = p_kv[..., KV_LORA:]
    if rope is not None:
        k_rope = apply_rope(k_rope, *rope)
    k_nope = (c_kv @ w_uk).reshape(bsz, n, N_HEADS, QK_NOPE)
    v = (c_kv @ w_uv).reshape(bsz, n, N_HEADS, V_HEAD)
    k = jnp.concatenate([k_nope, jnp.broadcast_to(k_rope[:, :, None, :], (bsz, n, N_HEADS, QK_ROPE))], axis=-1)
    return k, v

def attend(q, k, v):
    s = jnp.einsum('bqhd,bkhd->bhqk', q, k).astype(jnp.float32) * ATTN_SCALE
    p = jax.nn.softmax(s, axis=-1).astype(v.dtype)
    return jnp.einsum('bhqk,bkhd->bqhd', p, v)

def attend_blocked(q, k, v):
    bsz, n, h, dk = q.shape
    qb = q.reshape(bsz, n // Q_BLOCK, Q_BLOCK, h, dk).transpose(1, 0, 2, 3, 4)
    o = lax.map(lambda qi: attend(qi, k, v), qb)
    return o.transpose(1, 0, 2, 3, 4).reshape(bsz, n, h * V_HEAD)

def hyena_filter(n, w1, b1, w2, b2, w3, freq, decay):
    f32 = jnp.float32
    w1, b1, w2, b2, w3, freq, decay = (a.astype(f32) for a in (w1, b1, w2, b2, w3, freq, decay))
    bands = (HY_EMB - 1) // 2
    t = jnp.linspace(0.0, 1.0, n, dtype=f32)[:, None]
    phase = (2.0 * math.pi / n) * jnp.arange(n, dtype=f32)[:, None] * jnp.linspace(1e-4, bands - 1, bands, dtype=f32)
    z = jnp.concatenate([t, jnp.cos(phase), -jnp.sin(phase)], axis=-1)
    h = jnp.sin(freq * (z @ w1 + b1))
    h = jnp.sin(freq * (h @ w2 + b2))
    h = (h @ w3).reshape(n, 2, HY_WIDTH) * jnp.exp(-t[:, :, None] * jnp.abs(decay))
    k = jnp.concatenate([h[:, 0], jnp.zeros((1, HY_WIDTH), f32), h[:0:-1, 1]], axis=0)
    return k / jnp.sum(jnp.abs(k), axis=0, keepdims=True)

def hyena(p, short_w, short_b, w1, b1, w2, b2, w3, freq, decay, bias):
    n = p.shape[1]
    pp = jnp.pad(p, ((0, 0), (1, 1), (0, 0)))
    u = pp[:, :-2] * short_w[0] + pp[:, 1:-1] * short_w[1] + pp[:, 2:] * short_w[2] + short_b
    v, x1, x0 = jnp.split(u, 3, axis=-1)
    z = v * x1
    k = hyena_filter(n, w1, b1, w2, b2, w3, freq, decay)
    zf = z.astype(jnp.float32)
    y = jnp.fft.irfft(jnp.fft.rfft(zf, n=2 * n, axis=1) * jnp.fft.rfft(k, axis=0)[None], n=2 * n, axis=1)[:, :n]
    y = (y + zf * bias.astype(jnp.float32)).astype(z.dtype)
    return y * x0

def token_mixer(p, k_all, v_all, rope, q_norm_g, w_uq, hy, w_br_attn, w_br_hy, w_out):
    bsz, n, _ = p.shape
    q = mla_queries(p[..., :Q_LORA], q_norm_g, w_uq, rope)
    if rope is None:
        o_attn = attend(q, k_all, v_all).reshape(bsz, n, N_HEADS * V_HEAD)
    else:
        o_attn = attend_blocked(q, k_all, v_all)
    o_hy = hyena(p[..., HY_START:GATE_START], *hy)
    g_attn, g_hy = jnp.split(jax.nn.sigmoid(p[..., GATE_START:]), 2, axis=-1)
    merged = g_attn * (o_attn @ w_br_attn) + g_hy * (o_hy @ w_br_hy)
    return merged @ w_out

def swiglu(h, w_gate, w_up, w_down):
    return (jax.nn.silu(h @ w_gate) * (h @ w_up)) @ w_down

def moe_swiglu(h, router, w_gate, w_up, w_down):
    bsz, n, d = h.shape
    t = h.reshape(-1, d)
    logits = (t @ router).astype(jnp.float32)
    top_val, top_idx = lax.top_k(logits, TOP_K)
    top_w = jax.nn.softmax(top_val, axis=-1)
    combine = jnp.sum(jax.nn.one_hot(top_idx, N_EXPERTS, dtype=jnp.float32) * top_w[..., None], axis=1).astype(h.dtype)
    out = jnp.zeros_like(t)
    for e in range(N_EXPERTS):
        out = out + combine[:, e:e + 1] * swiglu(t, w_gate[e], w_up[e], w_down[e])
    return out.reshape(bsz, n, d)

def channel_mixer(h, layer, ffn_w_gate, ffn_w_up, ffn_w_down, moe_router, moe_w_gate, moe_w_up, moe_w_down):
    i = layer // 2
    if layer % 2 == 0:
        return swiglu(h, ffn_w_gate[i], ffn_w_up[i], ffn_w_down[i])
    return moe_swiglu(h, moe_router[i], moe_w_gate[i], moe_w_up[i], moe_w_down[i])

def first_inputs(seed: int = 0) -> dict:
    key = jax.random.key(seed)
    ks = iter(jax.random.split(key, 48))
    f32 = jnp.float32
    D, L = D_MODEL, DEPTH

    def nrm(shape, fan_in, gain=1.0):
        return jax.random.normal(next(ks), shape, f32) * (gain * fan_in ** -0.5)

    def gain_vec(shape):
        return 1.0 + 0.02 * jax.random.normal(next(ks), shape, f32)

    def small(shape, scale):
        return scale * jax.random.normal(next(ks), shape, f32)

    return {
        'x': jax.random.normal(next(ks), (BATCH, SEQ, D), f32),
        'c': jax.random.normal(next(ks), (BATCH, D), f32),
        'ctx': jax.random.normal(next(ks), (BATCH, CTX_LEN, D), f32),
        'c_ctx': jax.random.normal(next(ks), (D,), f32),
        'w_mod': nrm((L, D, 6 * D), D, 0.5),
        'b_mod': small((L, 6 * D), 0.02),
        'norm1_g': gain_vec((L, D)),
        'norm2_g': gain_vec((L, D)),
        'w_in': nrm((L, D, IN_COLS), D),
        'q_norm_g': gain_vec((L, Q_LORA)),
        'kv_norm_g': gain_vec((L, KV_LORA)),
        'w_uq': nrm((L, Q_LORA, N_HEADS * (QK_NOPE + QK_ROPE)), Q_LORA),
        'w_uk': nrm((L, KV_LORA, N_HEADS * QK_NOPE), KV_LORA),
        'w_uv': nrm((L, KV_LORA, N_HEADS * V_HEAD), KV_LORA),
        'hy_short_w': nrm((L, 3, 3 * HY_WIDTH), 3),
        'hy_short_b': small((L, 3 * HY_WIDTH), 0.02),
        'hy_w1': nrm((L, HY_EMB, HY_FILTER_HIDDEN), HY_EMB),
        'hy_b1': small((L, HY_FILTER_HIDDEN), 0.1),
        'hy_w2': nrm((L, HY_FILTER_HIDDEN, HY_FILTER_HIDDEN), HY_FILTER_HIDDEN),
        'hy_b2': small((L, HY_FILTER_HIDDEN), 0.1),
        'hy_w3': nrm((L, HY_FILTER_HIDDEN, 2 * HY_WIDTH), HY_FILTER_HIDDEN),
        'hy_freq': gain_vec((L, HY_FILTER_HIDDEN)),
        'hy_decay': jax.random.uniform(next(ks), (L, 2, HY_WIDTH), f32, minval=HY_DECAY_MIN, maxval=HY_DECAY_MAX),
        'hy_bias': jax.random.normal(next(ks), (L, HY_WIDTH), f32),
        'w_br_attn': nrm((L, N_HEADS * V_HEAD, D), N_HEADS * V_HEAD),
        'w_br_hy': nrm((L, HY_WIDTH, D), HY_WIDTH),
        'w_out': nrm((L, D, D), D),
        'ffn_w_gate': nrm((N_DENSE, D, D_FF), D),
        'ffn_w_up': nrm((N_DENSE, D, D_FF), D),
        'ffn_w_down': nrm((N_DENSE, D_FF, D), D_FF),
        'moe_router': nrm((N_MOE, D, N_EXPERTS), D),
        'moe_w_gate': nrm((N_MOE, N_EXPERTS, D, D_FF), D),
        'moe_w_up': nrm((N_MOE, N_EXPERTS, D, D_FF), D),
        'moe_w_down': nrm((N_MOE, N_EXPERTS, D_FF, D), D_FF),
        'final_g': gain_vec((D,)),
    }

def first_block(x, c, ctx, c_ctx, w_mod, b_mod, norm1_g, norm2_g, w_in, q_norm_g, kv_norm_g, w_uq, w_uk, w_uv,
              hy_short_w, hy_short_b, hy_w1, hy_b1, hy_w2, hy_b2, hy_w3, hy_freq, hy_decay, hy_bias,
              w_br_attn, w_br_hy, w_out, ffn_w_gate, ffn_w_up, ffn_w_down,
              moe_router, moe_w_gate, moe_w_up, moe_w_down, final_g):
    rows = x.shape[1] // GRID_W
    rope = axial_rope_tables(rows, x.dtype)
    for layer in range(DEPTH):
        last = layer == DEPTH - 1
        sh1, sc1, g1, sh2, sc2, g2 = (m[:, None, :] for m in adaln(c, w_mod[layer], b_mod[layer], 6))
        hy = (hy_short_w[layer], hy_short_b[layer], hy_w1[layer], hy_b1[layer], hy_w2[layer], hy_b2[layer],
              hy_w3[layer], hy_freq[layer], hy_decay[layer], hy_bias[layer])

        h_lat = rmsnorm(x, norm1_g[layer]) * (1 + sc1) + sh1
        p_lat = h_lat @ w_in[layer]
        k_lat, v_lat = mla_keys_values(p_lat[..., KV_START:HY_START], kv_norm_g[layer], w_uk[layer], w_uv[layer], rope)

        if last:
            csh1, csc1 = adaln(c_ctx, w_mod[layer][:, :2 * D_MODEL], b_mod[layer][:2 * D_MODEL], 2)
            h_ctx = rmsnorm(ctx, norm1_g[layer]) * (1 + csc1) + csh1
            p_ctx_kv = h_ctx @ w_in[layer][:, KV_START:HY_START]
            k_ctx, v_ctx = mla_keys_values(p_ctx_kv, kv_norm_g[layer], w_uk[layer], w_uv[layer], None)
        else:
            csh1, csc1, cg1, csh2, csc2, cg2 = adaln(c_ctx, w_mod[layer], b_mod[layer], 6)
            h_ctx = rmsnorm(ctx, norm1_g[layer]) * (1 + csc1) + csh1
            p_ctx = h_ctx @ w_in[layer]
            k_ctx, v_ctx = mla_keys_values(p_ctx[..., KV_START:HY_START], kv_norm_g[layer], w_uk[layer], w_uv[layer], None)
            mix_ctx = token_mixer(p_ctx, k_ctx, v_ctx, None, q_norm_g[layer], w_uq[layer], hy,
                                  w_br_attn[layer], w_br_hy[layer], w_out[layer])

        k_all = jnp.concatenate([k_ctx, k_lat], axis=1)
        v_all = jnp.concatenate([v_ctx, v_lat], axis=1)
        mix_lat = token_mixer(p_lat, k_all, v_all, rope, q_norm_g[layer], w_uq[layer], hy,
                              w_br_attn[layer], w_br_hy[layer], w_out[layer])
        x = x + g1 * mix_lat
        x = x + g2 * channel_mixer(rmsnorm(x, norm2_g[layer]) * (1 + sc2) + sh2, layer,
                                   ffn_w_gate, ffn_w_up, ffn_w_down, moe_router, moe_w_gate, moe_w_up, moe_w_down)
        if not last:
            ctx = ctx + cg1 * mix_ctx
            ctx = ctx + cg2 * channel_mixer(rmsnorm(ctx, norm2_g[layer]) * (1 + csc2) + csh2, layer,
                                            ffn_w_gate, ffn_w_up, ffn_w_down, moe_router, moe_w_gate, moe_w_up, moe_w_down)
    return rmsnorm(x, final_g)


DEPTH_2 = 1

CHUNK = 64
LEFT_CHUNKS = 8
BAND = (LEFT_CHUNKS + 1) * CHUNK
ATT_HEADS = 8
ATT_HEAD_DIM = 64
ATT_WIDTH = ATT_HEADS * ATT_HEAD_DIM
MAX_REL = 128
LRU_WIDTH = D_MODEL
LRU_BLOCKS = 16
LRU_BLOCK = LRU_WIDTH // LRU_BLOCKS
CONV_WIDTH = 4
LRU_C = 8.0
N_SUB = 3
PROJ_SIZES = (ATT_WIDTH, ATT_WIDTH, ATT_WIDTH, LRU_WIDTH, LRU_WIDTH, D_MODEL, D_MODEL)
PROJ_WIDTH = sum(PROJ_SIZES)


def rmsnorm_2(x, g):
    xf = x.astype(jnp.float32)
    y = xf * lax.rsqrt(jnp.mean(xf * xf, axis=-1, keepdims=True) + EPS)
    return (y * g.astype(jnp.float32)).astype(x.dtype)

def modulate(h, shift, scale):
    return h * (1 + scale[:, None, :]) + shift[:, None, :]

def swiglu_2(h, w_gu, w_down):
    g, u = jnp.split(h @ w_gu, 2, axis=-1)
    return (jax.nn.silu(g) * u) @ w_down

def chunked_attention(q, k, v, rel_bias):
    b, s, _ = q.shape
    nc = s // CHUNK
    q = q.reshape(b, nc, CHUNK, ATT_HEADS, ATT_HEAD_DIM)
    k = k.reshape(b, nc, CHUNK, ATT_HEADS, ATT_HEAD_DIM)
    v = v.reshape(b, nc, CHUNK, ATT_HEADS, ATT_HEAD_DIM)
    pad = ((0, 0), (LEFT_CHUNKS, 0), (0, 0), (0, 0), (0, 0))
    kp, vp = jnp.pad(k, pad), jnp.pad(v, pad)
    kb = jnp.concatenate([kp[:, j:j + nc] for j in range(LEFT_CHUNKS + 1)], axis=2)
    vb = jnp.concatenate([vp[:, j:j + nc] for j in range(LEFT_CHUNKS + 1)], axis=2)
    scores = jnp.einsum('bnqhd,bnkhd->bhnqk', q, kb).astype(jnp.float32) * (ATT_HEAD_DIM ** -0.5)
    qi = jnp.arange(CHUNK)[:, None]
    kj = jnp.arange(BAND)[None, :]
    rel = jnp.clip(qi - kj + LEFT_CHUNKS * CHUNK, -MAX_REL, MAX_REL) + MAX_REL
    bias = rel_bias.astype(jnp.float32)[:, rel]
    scores = scores + bias[None, :, None, :, :]
    valid = (jnp.arange(nc)[:, None] - LEFT_CHUNKS + jnp.arange(BAND)[None, :] // CHUNK) >= 0
    scores = jnp.where(valid[None, None, :, None, :], scores, jnp.finfo(jnp.float32).min)
    p = jax.nn.softmax(scores, axis=-1).astype(v.dtype)
    out = jnp.einsum('bhnqk,bnkhd->bnqhd', p, vb)
    return out.reshape(b, s, ATT_WIDTH)

def causal_depthwise_conv(x, w, bias):
    rhs = w[:, None, :]
    y = lax.conv_general_dilated(x, rhs, window_strides=(1,), padding=[(CONV_WIDTH - 1, 0)],
                                 dimension_numbers=('NWC', 'WIO', 'NWC'),
                                 feature_group_count=x.shape[-1])
    return y + bias

def block_diag_linear(x, w, bias):
    b, s, _ = x.shape
    xb = x.reshape(b, s, LRU_BLOCKS, LRU_BLOCK)
    return jnp.einsum('bsnk,nkj->bsnj', xb, w).reshape(b, s, LRU_WIDTH) + bias

def rg_lru(x, w_a, b_a, w_x, b_x, lam):
    r = jax.nn.sigmoid(block_diag_linear(x, w_a, b_a).astype(jnp.float32))
    i = jax.nn.sigmoid(block_diag_linear(x, w_x, b_x).astype(jnp.float32))
    log_a = -LRU_C * r * jax.nn.softplus(-lam.astype(jnp.float32))
    a = jnp.exp(log_a)
    mult = jnp.sqrt(-jnp.expm1(2.0 * log_a))
    u = mult * (i * x.astype(jnp.float32))

    def combine(left, right):
        a1, b1 = left
        a2, b2 = right
        return a1 * a2, a2 * b1 + b2

    _, h = lax.associative_scan(combine, (a, u), axis=1)
    return h.astype(x.dtype)

def mixer(h, w_in, rel_bias, conv_w, conv_b, lru_wa, lru_ba, lru_wx, lru_bx, lru_lambda,
          w_att_o, w_rec_o, w_out):
    proj = h @ w_in
    idx = [int(v) for v in np.cumsum(PROJ_SIZES)[:-1]]
    q, k, v, xr, yr, g_att, g_rec = jnp.split(proj, idx, axis=-1)
    att = chunked_attention(q, k, v, rel_bias) @ w_att_o
    xr = causal_depthwise_conv(xr, conv_w, conv_b)
    rec = (rg_lru(xr, lru_wa, lru_ba, lru_wx, lru_bx, lru_lambda) * jax.nn.gelu(yr)) @ w_rec_o
    merged = jax.nn.sigmoid(g_att) * att + jax.nn.sigmoid(g_rec) * rec
    return merged @ w_out

def sandwich(x, fn, g_pre, g_post, shift, scale, gate, res_w):
    h = modulate(rmsnorm_2(x, g_pre), shift, scale)
    y = rmsnorm_2(fn(h), g_post)
    return x + res_w * gate[:, None, :] * y

def second_inputs(seed: int = 0) -> dict:
    key = jax.random.key(seed)
    ks = jax.random.split(key, 24)
    L, D, F, W = DEPTH_2, D_MODEL, D_FF, LRU_WIDTH
    nrm = lambda k, shape, fan_in: jax.random.normal(k, shape, jnp.float32) * (fan_in ** -0.5)
    u = jax.random.uniform(ks[20], (L, W), jnp.float32, 0.9, 0.999)
    p = u ** (1.0 / LRU_C)
    lam = jnp.log(p) - jnp.log1p(-p)
    return {
        "x": jax.random.normal(ks[0], (BATCH, SEQ, D), jnp.float32),
        "c": jax.random.normal(ks[1], (BATCH, D), jnp.float32),
        "w_ada": nrm(ks[2], (L, D, N_SUB * 3 * D), D) * 0.5,
        "b_ada": 0.02 * jax.random.normal(ks[3], (L, N_SUB * 3 * D), jnp.float32),
        "norm_pre": 1.0 + 0.05 * jax.random.normal(ks[4], (L, N_SUB, D), jnp.float32),
        "norm_post": 1.0 + 0.05 * jax.random.normal(ks[5], (L, N_SUB, D), jnp.float32),
        "ffn1_w_gu": nrm(ks[6], (L, D, 2 * F), D),
        "ffn1_w_down": nrm(ks[7], (L, F, D), F),
        "w_in": nrm(ks[8], (L, D, PROJ_WIDTH), D),
        "rel_bias": 0.5 * jax.random.normal(ks[9], (L, ATT_HEADS, 2 * MAX_REL + 1), jnp.float32),
        "conv_w": nrm(ks[10], (L, CONV_WIDTH, W), CONV_WIDTH),
        "conv_b": 0.02 * jax.random.normal(ks[11], (L, W), jnp.float32),
        "lru_wa": nrm(ks[12], (L, LRU_BLOCKS, LRU_BLOCK, LRU_BLOCK), LRU_BLOCK),
        "lru_ba": 0.02 * jax.random.normal(ks[13], (L, W), jnp.float32),
        "lru_wx": nrm(ks[14], (L, LRU_BLOCKS, LRU_BLOCK, LRU_BLOCK), LRU_BLOCK),
        "lru_bx": 0.02 * jax.random.normal(ks[15], (L, W), jnp.float32),
        "lru_lambda": lam,
        "w_att_o": nrm(ks[16], (L, ATT_WIDTH, D), ATT_WIDTH),
        "w_rec_o": nrm(ks[17], (L, W, D), W),
        "w_out": nrm(ks[18], (L, D, D), D),
        "ffn2_w_gu": nrm(ks[19], (L, D, 2 * F), D),
        "ffn2_w_down": nrm(ks[21], (L, F, D), F),
    }

def second_block(x, c, w_ada, b_ada, norm_pre, norm_post, ffn1_w_gu, ffn1_w_down, w_in, rel_bias,
              conv_w, conv_b, lru_wa, lru_ba, lru_wx, lru_bx, lru_lambda, w_att_o, w_rec_o,
              w_out, ffn2_w_gu, ffn2_w_down):
    b = x.shape[0]
    c_act = jax.nn.silu(c)
    for l in range(DEPTH_2):
        mod = (c_act @ w_ada[l] + b_ada[l]).reshape(b, N_SUB, 3, D_MODEL)
        ffn1 = lambda h: swiglu_2(h, ffn1_w_gu[l], ffn1_w_down[l])
        mix = lambda h: mixer(h, w_in[l], rel_bias[l], conv_w[l], conv_b[l], lru_wa[l], lru_ba[l],
                              lru_wx[l], lru_bx[l], lru_lambda[l], w_att_o[l], w_rec_o[l], w_out[l])
        ffn2 = lambda h: swiglu_2(h, ffn2_w_gu[l], ffn2_w_down[l])
        x = sandwich(x, ffn1, norm_pre[l, 0], norm_post[l, 0], mod[:, 0, 0], mod[:, 0, 1], mod[:, 0, 2], 0.5)
        x = sandwich(x, mix, norm_pre[l, 1], norm_post[l, 1], mod[:, 1, 0], mod[:, 1, 1], mod[:, 1, 2], 1.0)
        x = sandwich(x, ffn2, norm_pre[l, 2], norm_post[l, 2], mod[:, 2, 0], mod[:, 2, 1], mod[:, 2, 2], 0.5)
    return x


def setup_inputs(seed=0):
    out = dict(first_inputs(seed))
    for name, value in second_inputs(seed + 1).items():
        if name != "x":
            out[name + "_2"] = value
    return out


def reference(
    x, c, ctx, c_ctx, w_mod, b_mod, norm1_g, norm2_g, w_in, q_norm_g, kv_norm_g, w_uq, w_uk,
    w_uv, hy_short_w, hy_short_b, hy_w1, hy_b1, hy_w2, hy_b2, hy_w3, hy_freq, hy_decay, hy_bias,
    w_br_attn, w_br_hy, w_out, ffn_w_gate, ffn_w_up, ffn_w_down, moe_router, moe_w_gate,
    moe_w_up, moe_w_down, final_g, c_2, w_ada_2, b_ada_2, norm_pre_2, norm_post_2, ffn1_w_gu_2,
    ffn1_w_down_2, w_in_2, rel_bias_2, conv_w_2, conv_b_2, lru_wa_2, lru_ba_2, lru_wx_2,
    lru_bx_2, lru_lambda_2, w_att_o_2, w_rec_o_2, w_out_2, ffn2_w_gu_2, ffn2_w_down_2,
):
    x = first_block(
        x, c, ctx, c_ctx, w_mod, b_mod, norm1_g, norm2_g, w_in, q_norm_g, kv_norm_g, w_uq, w_uk,
        w_uv, hy_short_w, hy_short_b, hy_w1, hy_b1, hy_w2, hy_b2, hy_w3, hy_freq, hy_decay,
        hy_bias, w_br_attn, w_br_hy, w_out, ffn_w_gate, ffn_w_up, ffn_w_down, moe_router,
        moe_w_gate, moe_w_up, moe_w_down, final_g,
    )
    return second_block(
        x, c_2, w_ada_2, b_ada_2, norm_pre_2, norm_post_2, ffn1_w_gu_2, ffn1_w_down_2, w_in_2,
        rel_bias_2, conv_w_2, conv_b_2, lru_wa_2, lru_ba_2, lru_wx_2, lru_bx_2, lru_lambda_2,
        w_att_o_2, w_rec_o_2, w_out_2, ffn2_w_gu_2, ffn2_w_down_2,
    )


_drawn_inputs = setup_inputs


def setup_inputs(seed=0):
    import zlib

    import numpy as np

    out = dict(_drawn_inputs(seed))
    spreads = {}
    factors = {'ctx': 3.884,
     'norm1_g': 4.102,
     'norm2_g': 16.256,
     'q_norm_g': 8.0,
     'kv_norm_g': 8.0,
     'hy_short_b': 5.704,
     'hy_b1': 5.701,
     'hy_b2': 4.954,
     'hy_freq': 8.0,
     'hy_decay': 5.527,
     'final_g': 7.539,
     'norm_post_2': 8.615,
     'conv_b_2': 3.459,
     'lru_ba_2': 59.457,
     'lru_bx_2': 26.516}
    for name, (base, spread) in spreads.items():
        noise = np.random.default_rng([zlib.crc32(name.encode()), seed]).standard_normal(out[name].shape)
        drawn = base * np.exp(spread * noise) if base else spread * noise
        out[name] = __import__('jax').numpy.asarray(drawn.astype(out[name].dtype))
    for name, factor in factors.items():
        out[name] = (out[name] * factor).astype(out[name].dtype)
    return out
```

```python
import math
from contextlib import ExitStack

import numpy as np

import concourse.bass as bass
from concourse import mybir

ALU = mybir.AluOpType
ACT = mybir.ActivationFunctionType
AX = mybir.AxisListType
F32 = mybir.dt.float32
F32R = mybir.dt.float32r
U32 = mybir.dt.uint32

P = 128
D = 1024
S = 256
NC = D // P
NH = 8
Q_LORA, KV_LORA, NOPE, ROPE, VH = 384, 256, 64, 32, 64
QD = NOPE + ROPE
QC, KVC = Q_LORA // P, KV_LORA // P
HY = 512
HYC = HY // P
EMB, FH = 17, 64
DFF = 2816
HALF = DFF // P // 2
NE = 8
KV_START = Q_LORA
HY_START = KV_START + KV_LORA + ROPE
GATE_START = HY_START + 3 * HY
EPS = 1e-6
SCALE = QD ** -0.5
SCALE2 = 64 ** -0.5
MAXREL = 128
AW = 512
TPS = 8
SLOT = TPS * P
RAW = 11
SPL = 3
NMODB = (2 * 6 + 9) * D // 512
NMOD = NMODB * NC // 2
BANKS = 6
HSLOTS = 3 * HALF
HCHUNKS = 2 * HALF + NC
HA, HD = HALF, HALF + NC

VEC = {}
_n = 0
for _name, _w in ([(f"{v}{l}", w) for l in range(2) for v, w in
                   (("n1", 8), ("n2", 8), ("qn", QC), ("kvn", KVC), ("sw", 36), ("sb", 12), ("hb", 4),
                    ("bm", 48), ("fb1", 1), ("fb2", 1), ("freq", 1))] +
                  [("fg", 8), ("bm2", 72), ("pre", 24), ("post", 24), ("cw", 32), ("cb", 8), ("ba", 8),
                   ("bx", 8), ("lam", 8), ("router", 64), ("c3", 256)]):
    VEC[_name] = (_n, _w)
    _n += _w
NVEC = _n
CST = {}
_n = 0
for _name, _w in (("ident", 128), ("ones", 128), ("F", 1024), ("G", 1024), ("cos", 512), ("sin", 512),
                  ("iota", 8), ("negt", 2), ("mask", 2), ("negm", 2), ("h1m", 2), ("alt2", 128)):
    CST[_name] = (_n, _w)
    _n += _w
NCST = _n


class Plan:

    def __init__(self):
        self.c, self.name = [], {}
        self.tiles = 0
        self.steps = 0
        self.slot_end = {}
        self.rank = {"A": 0, "D": 0}
        self.complete = []
        self.mod_end = []
        self.loops = {}
        self.caps = []

    def chunk(self, name, owner, tiles=0, mod=False):
        if mod:
            self.mod_end += [self.steps + j + 1 for j in range(NC // 2)]
            self.steps += NC // 2 - 1
        t0 = self.tiles
        t1 = t0 + tiles
        for t in range(t0, t1):
            if t % TPS == TPS - 1 and t != t1 - 1:
                self.steps += 1
                self.slot_end[t // TPS] = self.steps
        self.steps += 1
        if tiles and t1 % TPS == 0:
            self.slot_end[t1 // TPS - 1] = self.steps
        self.tiles = t1
        self.rank[owner] += 1
        self.name[name] = len(self.c)
        self.c.append(dict(name=name, owner=owner, t0=t0, t1=t1, end=self.steps, rank=self.rank[owner]))
        self.complete.append(t1 // TPS)

    def loop(self, name, times):
        assert self.tiles % TPS == 0
        s0 = self.tiles // TPS
        for i in range(SPL if s0 >= SPL else 0):
            assert self.slot_end[s0 - SPL + i] <= self.steps - (3, 1, 0)[i]
        self.caps.append(s0)
        self.loops[name] = dict(slot=s0, chunk=len(self.c), step=self.steps, A=self.rank["A"],
                                D=self.rank["D"], half=sum(v["times"] for v in self.loops.values()), times=times)
        for q in range(times):
            for f in range(HALF):
                self.chunk(f"{name}.{q}.g{f}", "A", TPS)
                self.chunk(f"{name}.{q}.u{f}", "D", TPS)
            for n in range(NC):
                self.chunk(f"{name}.{q}.d{n}", "D", HALF)

    def __getitem__(self, name):
        return self.c[self.name[name]]


def attention_order(label, tiles):
    items = [(hp, qt, hh) for hp in range(NH // 2) for qt in range(tiles) for hh in range(2)]
    return items


def make_plan():
    p = Plan()

    def attn(l, tiles):
        n = len(attention_order(l, tiles))
        p.chunk(f"{l}.S0", "D" if l == "B" else "A")
        for i in range(n + 1):
            if i + 1 < n:
                p.chunk(f"{l}.S{i+1}", "D" if l == "B" else "A")
            if i < n:
                p.chunk(f"{l}.PT{i}", "D")
            if i >= 1 and (i - 1) % 2 == 1:
                p.chunk(f"{l}.O{(i-1)//2}", "D")

    for b in range(NMODB + 1):
        if b < NMODB:
            p.chunk(f"mod{b}", "A", mod=True)
        if b:
            p.chunk(f"modT{b-1}", "D")
    for l in range(2):
        L = f"L{l}"
        p.chunk(f"{L}.n1", "D")
        for i in range(KVC):
            p.chunk(f"{L}.kv{i}", "D", NC)
        p.chunk(f"{L}.kr", "D", NC)
        for i in range(QC):
            p.chunk(f"{L}.q{i}", "D", NC)
        p.chunk(f"{L}.nkv", "D")
        p.chunk(f"{L}.nq", "D")
        for i in range(4):
            p.chunk(f"{L}.uk{i}", "A", KVC)
        for i in range(4):
            p.chunk(f"{L}.uv{i}", "A", 2 * 4 if i == 3 else 0)
        for h in range(NH):
            p.chunk(f"{L}.uq{h}", "D", QC)
        attn(L, 4 if l == 0 else 2)
        p.chunk(f"f{l}.a", "D")
        p.chunk(f"f{l}.b", "D")
        for t in range(4):
            p.chunk(f"f{l}.h{t}", "D")
        p.chunk(f"f{l}.sum", "D")
        for t in range(4):
            p.chunk(f"f{l}.K{t}", "D")
        for c in range(HYC):
            for v in range(3):
                p.chunk(f"{L}.hy{c}{v}", "D", NC)
        for s in range(2 if l == 0 else 1):
            for t in range(2):
                p.chunk(f"{L}.z{s}{t}", "D")
            for f in range(4):
                p.chunk(f"{L}.Z{s}{f}", "D")
            for c in range(HYC):
                p.chunk(f"{L}.y{s}{c}", "D")
        for n in range(NC):
            p.chunk(f"{L}.ga{n}", "A", NC)
            p.chunk(f"{L}.ba{n}", "D", 4)
            p.chunk(f"{L}.gh{n}", "A", NC)
            p.chunk(f"{L}.bh{n}", "D", 4)
        for n in range(NC):
            p.chunk(f"{L}.o{n}", "D", NC)
        p.chunk(f"{L}.n2", "D")
        if l == 1:
            for t in range(2):
                p.chunk(f"route{t}", "D")
            for e in range(NE // 2):
                p.chunk(f"cb{e}", "D")
        p.loop(f"{L}.ff", 2 if l == 0 else 2 * NE)
    p.chunk("final", "D")
    for j in range(3):
        p.chunk(f"B.pre{j}", "D")
        if j != 1:
            p.loop(f"B.ff{j}", 2)
        else:
            for n in range(8):
                p.chunk(f"B.qk{n}", "A", NC)
            for t in range(2):
                p.chunk(f"B.v{t}", "A", 1 if t == 1 else 31)
            attn("B", 2)
            for n in range(NC):
                p.chunk(f"B.xr{n}", "D", NC)
            for n in range(NC):
                p.chunk(f"B.ra{n}", "A")
                p.chunk(f"B.rx{n}", "A")
            for n in range(NC):
                p.chunk(f"B.yr{n}", "A", NC)
            for n in range(NC):
                p.chunk(f"B.ga{n}", "A", NC)
                p.chunk(f"B.ba{n}", "D", 4)
                p.chunk(f"B.gh{n}", "A", NC)
                p.chunk(f"B.bh{n}", "D", NC)
            for n in range(NC):
                p.chunk(f"B.o{n}", "D", NC)
        p.chunk(f"B.post{j}", "D")
    assert p.tiles % TPS == 0
    return p


ARENA = 17408
FF_AT = 4096


def build(nc, io):
    plan = make_plan()
    NSPLIT = plan.tiles // TPS
    caps = plan.caps + [NSPLIT]
    with ExitStack() as ctx:
        def sb(name, shape, dt=F32):
            return ctx.enter_context(nc.sbuf_tensor(name, shape, dt))

        def sem(name):
            return ctx.enter_context(nc.semaphore(name))

        raw = sb("raw", [P, RAW, SLOT])
        whi = sb("whi", [P, SPL, SLOT], F32R)
        wlo = sb("wlo", [P, SPL, SLOT], F32R)
        xs = sb("xs", [P, NC, 2 * S])
        hH = sb("hH", [P, NC, 2 * S], F32R)
        hL = sb("hL", [P, NC, 2 * S], F32R)
        arena_at = -(-nc.sbuf_base // 32) * 32
        arena = sb("arena", [P, ARENA])
        rounded = nc.alloc_sbuf_tensor_at("rounded", [P, ARENA], F32R, offset=arena_at)
        vec = sb("vec", [P, NVEC])
        cst = sb("cst", [P, NCST])
        modT = sb("modT", [P, (12 + 12 + 18) * 4, 3])
        dv = sb("dv", [P, 14, NC])
        small = sb("small", [P, 96])
        idx = sb("idx", [P, 8], U32)
        ps = ctx.enter_context(nc.psum_tensor("ps", [P, BANKS, 512], F32))

        def view(at, n, width, dt=F32):
            v = (arena if dt is F32 else rounded)[:, at:at + n * width]
            return v.rearrange("p (n w) -> p n w", n=n)

        def C(name, a=0, b=None):
            at, w = CST[name]
            return cst[:, at + a:at + (w if b is None else b)]

        def Vv(name, a=0, b=None):
            at, w = VEC[name]
            return vec[:, at + a:at + (w if b is None else b)]

        ident, ones = C("ident"), C("ones")

        raw_in = [sem(f"raw_in{i}") for i in range(RAW)]
        hi_ready = sem("hi_ready")
        lo_ready = sem("lo_ready")
        pe_step = sem("pe_step")
        act_free = sem("act_free")
        dve_free = sem("dve_free")
        free_of = {"A": act_free, "D": dve_free}
        consts_in = sem("consts_in")
        cact_ready = sem("cact_ready")
        sq_ready = sem("sq_ready")
        std_ready = sem("std_ready")
        norm_ready = sem("norm_ready")
        nhi_ready = sem("nhi_ready")
        nlo_ready = sem("nlo_ready")
        rope_ready = sem("rope_ready")
        nmax_ready = sem("nmax_ready")
        exp_ready = sem("exp_ready")
        prob_ready = sem("prob_ready")
        ohi_ready = sem("ohi_ready")
        filt_in = sem("filt_in")
        filt_d = sem("filt_d")
        filt_a = sem("filt_a")
        z_ready = sem("z_ready")
        Y_ready = sem("Y_ready")
        o_ready = sem("o_ready")
        hyhi_ready = sem("hyhi_ready")
        hylo_ready = sem("hylo_ready")
        m_ready = sem("m_ready")
        mhi_ready = sem("mhi_ready")
        mlo_ready = sem("mlo_ready")
        hidhi_ready = sem("hidhi_ready")
        hidlo_ready = sem("hidlo_ready")
        comb_ready = sem("comb_ready")
        gates_ready = sem("gates_ready")
        blk_in = sem("blk_in")
        lru_d = sem("lru_d")
        lru_a = sem("lru_a")
        lam_abs = sem("lam_abs")
        lam_exp = sem("lam_exp")
        out_ready = sem("out_ready")
        out_done = sem("out_done")
        d_link = sem("d_link")
        a_link = sem("a_link")
        p_link = sem("p_link")

        NORMS = ["L0.n1", "L0.nkv", "L0.nq", "L0.n2", "L1.n1", "L1.nkv", "L1.nq", "L1.n2", "final",
                 "B.pre0", "B.post0", "B.pre1", "B.post1", "B.pre2", "B.post2"]
        NORM_CHUNKS = {n: KVC if "nkv" in n else QC if "nq" in n else NC for n in NORMS}

        def norm_at(label, n=0):
            return sum(NORM_CHUNKS[m] for m in NORMS[:NORMS.index(label)]) + n

        SPLIT = [n for n in NORMS if n != "final" and "post" not in n]

        def split_at(label, n=0):
            return sum(NORM_CHUNKS[m] for m in SPLIT[:SPLIT.index(label)]) + n

        ATTN = {"L0": 0, "L1": 32, "B": 48}
        LAYERS = ((0, 0, 2 * S), (1, S, S))

        block = ctx.enter_context(nc.Block())

        def wait_chunk(eng, name):
            eng.wait_ge(pe_step, plan[name]["end"])

        def wait_free(eng, name):
            eng.wait_ge(free_of[plan[name]["owner"]], plan[name]["rank"])

        def bank(name):
            return ps[:, plan.name[name] % BANKS, :]

        @block.sync
        def _(sp):
            sp.dma_start(vec[:, :], io["vec"]).then_inc(consts_in, 16)
            for g in range(NMOD):
                if g >= RAW:
                    sp.wait_ge(pe_step, plan.mod_end[g - RAW])
                sp.dma_start(raw[:, g % RAW, :], io["wmod"][g]).then_inc(raw_in[g % RAW], 16)
            for s in range(RAW):
                g = s + NMOD
                sp.wait_ge(pe_step, plan.mod_end[g - RAW])
                sp.dma_start(raw[:, g % RAW, :], io["wsplit"][s]).then_inc(raw_in[g % RAW], 16)
            turns = NSPLIT // RAW - 1
            with sp.Fori(0, turns) as k:
                for j in range(RAW):
                    sp.wait_ge(lo_ready, k * RAW + (j + 1))
                    sp.dma_start(raw[:, (NMOD + j) % RAW, :],
                                 io["wsplit"][bass.ds(k * RAW + (RAW + j), 1)].rearrange("o p w -> p (o w)"))\
                      .then_inc(raw_in[(NMOD + j) % RAW], 16)
            for s in range((turns + 1) * RAW, NSPLIT):
                sp.wait_ge(lo_ready, s - RAW + 1)
                sp.dma_start(raw[:, (NMOD + s) % RAW, :], io["wsplit"][s]).then_inc(raw_in[(NMOD + s) % RAW], 16)
            sp.wait_ge(out_ready, 1)
            sp.dma_start(io["out"].rearrange("(c p) t -> p c t", p=P), xs[:, :, S:2 * S]).then_inc(out_done, 16)
            sp.wait_ge(out_done, 16)

        @block.tensor
        def _(pe):
            st = {"step": 0}

            def step(mm):
                mm.then_inc(pe_step, 1)
                st["step"] += 1

            def begin(name):
                c = plan.name[name]
                if c >= BANKS:
                    wait_free(pe, plan.c[c - BANKS]["name"])

            def lin(name, mov, T, ktiles=None):
                begin(name)
                c = plan[name]
                for i, t in enumerate(range(c["t0"], c["t1"])):
                    s, r = divmod(t, TPS)
                    if i == 0 or r == 0:
                        pe.wait_ge(lo_ready, s + 1)
                    wh = whi[:, s % SPL, r * P:(r + 1) * P]
                    wl = wlo[:, s % SPL, r * P:(r + 1) * P]
                    xh, xl = mov(i)
                    o = bank(name)[:, 0:T]
                    last = t == c["t1"] - 1
                    pe.matmul(o, wh, xh, start=(i == 0), stop=False)
                    pe.matmul(o, wh, xl, start=False, stop=False)
                    mm = pe.matmul(o, wl, xh, start=False, stop=last)
                    if r == TPS - 1 or last:
                        step(mm)
                assert st["step"] == c["end"], name

            def mean_square(label, sq, n, T):
                begin(label)
                pe.wait_ge(sq_ready, NORMS.index(label) + 1)
                for k in range(n):
                    mm = pe.matmul(bank(label)[:, 0:T], ones, sq[:, k, :], start=(k == 0), stop=(k == n - 1))
                step(mm)

            def mod_block(b):
                begin(f"mod{b}")
                cact = view(0, NC, 32)
                for k in range(NC):
                    g = b * (NC // 2) + k // 2
                    if k % 2 == 0:
                        pe.wait_ge(raw_in[g % RAW], 16 * (g // RAW + 1))
                    j = k % 4
                    mm = pe.matmul(bank(f"mod{b}")[32 * j:32 * j + 32, :], cact[:, k, :],
                                   raw[:, g % RAW, (k % 2) * 512:(k % 2 + 1) * 512],
                                   start=(k < 4), stop=(k >= 4), skip_group_check=True, tile_position=(0, 32 * j))
                    if k % 2:
                        step(mm)

            def mod_turn(b):
                begin(f"modT{b}")
                wait_free(pe, f"mod{b}")
                rows = view(256, 2, 512)
                for q in range(4):
                    mm = pe.transpose(bank(f"modT{b}")[:, q * P:(q + 1) * P], rows[:, b % 2, q * P:(q + 1) * P], ident)
                step(mm)

            def attention(l, tiles, qk, vt, pT, pv_rows):
                items = attention_order(l, tiles)
                n = len(items)

                def scores(i):
                    begin(f"{l}.S{i}")
                    qa, ka, nk = qk(*items[i])
                    step(pe.matmul(bank(f"{l}.S{i}")[:, 0:nk], qa, ka, start=True, stop=True))

                def turn(i):
                    begin(f"{l}.PT{i}")
                    pe.wait_ge(prob_ready, ATTN[l] + i + 1)
                    nk = qk(*items[i])[2]
                    for c in range(nk // P):
                        mm = pe.transpose(bank(f"{l}.PT{i}")[:, c * P:(c + 1) * P], pv_rows[:, i % 2, c * P:(c + 1) * P],
                                          ident)
                    step(mm)

                def out(i):
                    hp, qt, hh = items[i]
                    o = f"{l}.O{i//2}"
                    if hh == 0:
                        begin(o)
                    wait_free(pe, f"{l}.PT{i}")
                    nk = qk(*items[i])[2]
                    h = 2 * hp + hh
                    for c in range(nk // P):
                        mm = pe.matmul(bank(o)[64 * hh:64 * hh + 64, 0:P], vt[:, c, h * VH:(h + 1) * VH],
                                       pT[:, i % 2, c * P:(c + 1) * P], start=(c == 0), stop=(c == nk // P - 1),
                                       skip_group_check=True, tile_position=(0, 64 * hh))
                    if hh == 1:
                        step(mm)

                scores(0)
                for i in range(n + 1):
                    if i + 1 < n:
                        scores(i + 1)
                    if i < n:
                        turn(i)
                    if i >= 1:
                        out(i - 1)

            def feed_forward(name, T, t0):
                L = plan.loops[name]
                for sem_, key in ((act_free, "A"), (dve_free, "D")):
                    pe.wait_ge(sem_, L[key])
                hid_h = view(FF_AT, HALF, T, F32R)
                hid_l = view(FF_AT + HALF * T, HALF, T, F32R)
                with pe.Fori(0, L["times"]) as q:
                    for c in range(HCHUNKS):
                        owner, rank = ("A", c // 2) if c < 2 * HALF and c % 2 == 0 else \
                            ("D", c // 2 if c < 2 * HALF else c - HALF)
                        b = c - BANKS
                        if b < 0:
                            pe.wait_ge(dve_free, q * HD + (L["D"] + 1 + b))
                        elif b < 2 * HALF and b % 2 == 0:
                            pe.wait_ge(act_free, q * HA + (L["A"] + b // 2 + 1))
                        else:
                            pe.wait_ge(dve_free, q * HD + (L["D"] + (b // 2 if b < 2 * HALF else b - HALF) + 1))
                        o = ps[:, (L["chunk"] + c) % BANKS, 0:T]
                        down = c >= 2 * HALF
                        t0_ = c * TPS if not down else 2 * HALF * TPS + (c - 2 * HALF) * HALF
                        nk = HALF if down else NC
                        for i in range(nk):
                            s, r = divmod(t0_ + i, TPS)
                            if i == 0 or r == 0:
                                pe.wait_ge(lo_ready, q * HSLOTS + (L["slot"] + s + 1))
                            if c == 2 * HALF:
                                pe.wait_ge(hidlo_ready, q * HALF + (L["half"] * HALF + i + 1))
                            wh = whi[:, (L["slot"] + s) % SPL, r * P:(r + 1) * P]
                            wl = wlo[:, (L["slot"] + s) % SPL, r * P:(r + 1) * P]
                            xh, xl = (hid_h[:, i, :], hid_l[:, i, :]) if down else \
                                (hH[:, i, t0:t0 + T], hL[:, i, t0:t0 + T])
                            pe.matmul(o, wh, xh, start=(i == 0), stop=False)
                            pe.matmul(o, wh, xl, start=False, stop=False)
                            mm = pe.matmul(o, wl, xh, start=False, stop=(i == nk - 1))
                            if r == TPS - 1 or i == nk - 1:
                                mm.then_inc(pe_step, 1)
                st["step"] = plan[f"{name}.{L['times']-1}.d{NC-1}"]["end"]

            pe.wait_ge(consts_in, 64)
            pe.wait_ge(cact_ready, 1)
            for b in range(NMODB + 1):
                if b < NMODB:
                    mod_block(b)
                if b:
                    mod_turn(b - 1)

            for l, q0, T in LAYERS:
                L = f"L{l}"
                allk = lambda k: (hH[:, k, :], hL[:, k, :])
                qk_ = lambda k: (hH[:, k, q0:q0 + T], hL[:, k, q0:q0 + T])
                mean_square(f"{L}.n1", view(0, NC, 512), NC, 512)
                pe.wait_ge(nlo_ready, split_at(f"{L}.n1", NC))
                for i in range(KVC):
                    lin(f"{L}.kv{i}", allk, 512)
                lin(f"{L}.kr", allk, 512)
                for i in range(QC):
                    lin(f"{L}.q{i}", qk_, T)
                mean_square(f"{L}.nkv", view(4096, KVC, 512), KVC, 512)
                mean_square(f"{L}.nq", view(5120, QC, T), QC, T)
                ckvh, ckvl = view(10240, KVC, 512, F32R), view(11264, KVC, 512, F32R)
                cqh, cql = view(12288, QC, T, F32R), view(12288 + 1536, QC, T, F32R)
                pe.wait_ge(nlo_ready, split_at(f"{L}.nkv", KVC))
                for i in range(4):
                    lin(f"{L}.uk{i}", lambda k: (ckvh[:, k, :], ckvl[:, k, :]), 512)
                s = plan[f"{L}.uv3"]["t0"] // TPS
                for i in range(4):
                    begin(f"{L}.uv{i}")
                    pe.wait_ge(lo_ready, s + 1)
                    o = bank(f"{L}.uv{i}")
                    for k in range(KVC):
                        wh, wl = (w[:, s % SPL, k * 512:(k + 1) * 512] for w in (whi, wlo))
                        xh, xl = (x[:, k, i * P:(i + 1) * P] for x in (ckvh, ckvl))
                        pe.matmul(o, xh, wh, start=(k == 0), stop=False)
                        pe.matmul(o, xl, wh, start=False, stop=False)
                        mm = pe.matmul(o, xh, wl, start=False, stop=(k == KVC - 1))
                    step(mm)
                pe.wait_ge(nlo_ready, split_at(f"{L}.nq", QC))
                for h in range(NH):
                    lin(f"{L}.uq{h}", lambda k: (cqh[:, k, :], cql[:, k, :]), T)
                kT, qT = view(0, NH, 512), view(4096, NH, T)
                pe.wait_ge(rope_ready, (l + 1) * (NH + 1))
                for i in range(4):
                    wait_free(pe, f"{L}.uv{i}")

                def qk(hp, qt, hh):
                    h = 2 * hp + hh
                    nk = S if l == 0 and qt < 2 else 2 * S
                    return qT[0:QD, h, qt * P:(qt + 1) * P], kT[0:QD, h, 0:nk], nk
                attention(L, T // P, qk, view(8192, 4, 512), view(15360, 2, 512), view(14336, 2, 512))

                pe.wait_ge(filt_in, 16 * 5 * (l + 1))
                fw = 16384
                begin(f"f{l}.a")
                step(pe.matmul(bank(f"f{l}.a")[0:FH, 0:S], arena[0:EMB, fw:fw + 64], arena[0:EMB, fw + 128:fw + 384],
                               start=True, stop=True))
                begin(f"f{l}.b")
                pe.wait_ge(filt_a, 3 * l + 2)
                step(pe.matmul(bank(f"f{l}.b")[0:FH, 0:S], arena[0:FH, fw + 64:fw + 128],
                               arena[0:FH, fw + 384:fw + 640], start=True, stop=True))
                pe.wait_ge(filt_a, 3 * l + 3)
                for t in range(4):
                    begin(f"f{l}.h{t}")
                    step(pe.matmul(bank(f"f{l}.h{t}"), arena[0:FH, fw + 640 + (t // 2) * P:fw + 640 + (t // 2 + 1) * P],
                                   arena[0:FH, 14336 + (t % 2) * 512:14336 + (t % 2 + 1) * 512], start=True, stop=True))
                begin(f"f{l}.sum")
                pe.wait_ge(filt_d, 5 * l + 4)
                ab = view(14336, 4, 512)
                for c in range(HYC):
                    for t in range(4):
                        mm = pe.matmul(bank(f"f{l}.sum")[:, c:c + 1], ab[:, t, c * P:(c + 1) * P], ones[:, 0:1],
                                       start=(t == 0), stop=(t == 3))
                step(mm)
                pe.wait_ge(filt_d, 5 * l + 5)
                Fm = C("F").rearrange("p (t f) -> p t f", t=2)
                hsum, hdif, h1 = view(14336, 2, 512), view(15360, 2, 512), view(4096, 4, 512)
                for f in range(4):
                    begin(f"f{l}.K{f}")
                    o = bank(f"f{l}.K{f}")
                    src = hsum if f < 2 else hdif
                    for t in range(2):
                        mm = pe.matmul(o, Fm[:, t, f * P:(f + 1) * P], src[:, t, :], start=(t == 0),
                                       stop=(t == 1 and f != 2))
                    if f == 2:
                        for t in range(2):
                            mm = pe.matmul(o, C("alt2"), h1[:, 2 * t + 1, :], start=False, stop=(t == 1))
                    step(mm)

                for c in range(HYC):
                    for v in range(3):
                        lin(f"{L}.hy{c}{v}", qk_, T)
                zT, zrow, Z, Y = view(0, HYC, T), view(8192, 2, 512), view(14336, 4, 512), view(4096, 4, 512)
                G = C("G").rearrange("p (f t) -> p f t", f=4)
                for s in range(T // S):
                    u = (0 if l == 0 else 2) + s
                    pe.wait_ge(z_ready, l + 1)
                    for t in range(2):
                        begin(f"{L}.z{s}{t}")
                        for c in range(HYC):
                            mm = pe.transpose(bank(f"{L}.z{s}{t}")[:, c * P:(c + 1) * P],
                                              zT[:, c, s * S + t * P:s * S + (t + 1) * P], ident)
                        step(mm)
                    wait_free(pe, f"{L}.z{s}1")
                    for f in range(4):
                        begin(f"{L}.Z{s}{f}")
                        for t in range(2):
                            mm = pe.matmul(bank(f"{L}.Z{s}{f}"), Fm[:, t, f * P:(f + 1) * P], zrow[:, t, :],
                                           start=(t == 0), stop=(t == 1))
                        step(mm)
                    pe.wait_ge(Y_ready, u + 1)
                    for c in range(HYC):
                        begin(f"{L}.y{s}{c}")
                        for f in range(4):
                            mm = pe.matmul(bank(f"{L}.y{s}{c}")[:, 0:S], Y[:, f, c * P:(c + 1) * P], G[:, f, :],
                                           start=(f == 0), stop=(f == 3))
                        step(mm)
                pe.wait_ge(hylo_ready, (2, 3)[l])
                oh, ol = view(10240, 4, T, F32R), view(12288, 4, T, F32R)
                yh, yl = view(0, 4, T, F32R), view(2048, 4, T, F32R)
                wait_free(pe, f"{L}.O{len(attention_order(L, T // P)) // 2 - 1}")
                for n in range(NC):
                    lin(f"{L}.ga{n}", qk_, T)
                    lin(f"{L}.ba{n}", lambda k: (oh[:, k, :], ol[:, k, :]), T)
                    lin(f"{L}.gh{n}", qk_, T)
                    lin(f"{L}.bh{n}", lambda k: (yh[:, k, :], yl[:, k, :]), T)
                pe.wait_ge(mlo_ready, l + 1)
                for n in range(NC):
                    lin(f"{L}.o{n}", qk_, T)
                mean_square(f"{L}.n2", view(0, NC, T), NC, T)
                pe.wait_ge(nlo_ready, split_at(f"{L}.n2", NC))
                if l == 1:
                    h32 = view(0, NC, S)
                    router = Vv("router").rearrange("p (k e) -> p k e", k=NC)
                    for t in range(2):
                        begin(f"route{t}")
                        for k in range(NC):
                            mm = pe.matmul(bank(f"route{t}")[:, 0:NE], h32[:, k, t * P:(t + 1) * P], router[:, k, :],
                                           start=(k == 0), stop=(k == NC - 1))
                        step(mm)
                    cbE = view(2048, 16, P)
                    pe.wait_ge(comb_ready, 2)
                    for e2 in range(NE // 2):
                        begin(f"cb{e2}")
                        for j in range(2):
                            for t in range(2):
                                mm = pe.matmul(bank(f"cb{e2}")[:, j * S + t * P:j * S + (t + 1) * P],
                                               cbE[:, (2 * e2 + j) * 2 + t, :], ident, start=True, stop=True,
                                               skip_group_check=True)
                        step(mm)
                feed_forward(f"{L}.ff", T, q0)

            mean_square("final", view(0, NC, S), NC, S)
            hx = lambda k: (hH[:, k, S:2 * S], hL[:, k, S:2 * S])
            for j in range(3):
                mean_square(f"B.pre{j}", view(0, NC, S), NC, S)
                pe.wait_ge(nlo_ready, split_at(f"B.pre{j}", NC))
                if j != 1:
                    feed_forward(f"B.ff{j}", S, S)
                else:
                    for n in range(8):
                        lin(f"B.qk{n}", hx, S)
                    for i in range(2):
                        begin(f"B.v{i}")
                    for k in range(NC):
                        s = plan["B.v0"]["t0"] // TPS + k // 2
                        pe.wait_ge(lo_ready, s + 1)
                        for i in range(2):
                            o = bank(f"B.v{i}")
                            wh, wl = (w[:, s % SPL, (k % 2) * 512:(k % 2 + 1) * 512] for w in (whi, wlo))
                            xh, xl = (x[:, k, S + i * P:S + (i + 1) * P] for x in (hH, hL))
                            pe.matmul(o, xh, wh, start=(k == 0), stop=False)
                            pe.matmul(o, xl, wh, start=False, stop=False)
                            mm = pe.matmul(o, xh, wl, start=False, stop=(k == NC - 1))
                            if (k % 2 == 1 and i == 1) or k == NC - 1:
                                step(mm)
                    qkT = view(2048, 8, S)
                    for n in range(8):
                        wait_free(pe, f"B.qk{n}")
                    for i in range(2):
                        wait_free(pe, f"B.v{i}")

                    def qk(hp, qt, hh):
                        nk = (qt + 1) * P
                        r = slice(64 * hh, 64 * hh + 64)
                        return qkT[r, hp, qt * P:(qt + 1) * P], qkT[r, 4 + hp, 0:nk], nk
                    attention("B", 2, qk, view(4096, 2, 512), view(8192, 2, S), view(7168, 2, S))
                    for n in range(NC):
                        lin(f"B.xr{n}", hx, S)
                    xc = view(2048, NC, S)
                    lw = view(13312, 2 * NC, P)
                    pe.wait_ge(lru_d, 1)
                    pe.wait_ge(blk_in, 32)
                    for n in range(NC):
                        for i, nm in enumerate(("ra", "rx")):
                            begin(f"B.{nm}{n}")
                            step(pe.matmul(bank(f"B.{nm}{n}")[:, 0:S], lw[:, 2 * n + i, :], xc[:, n, :],
                                           start=True, stop=True))
                    for n in range(NC):
                        lin(f"B.yr{n}", hx, S)
                    oh, ol = view(5120, 4, S, F32R), view(6144, 4, S, F32R)
                    yh, yl = view(2048, NC, S, F32R), view(7168, NC, S, F32R)
                    wait_free(pe, "B.O7")
                    pe.wait_ge(lru_d, 6)
                    for n in range(NC):
                        lin(f"B.ga{n}", hx, S)
                        lin(f"B.ba{n}", lambda k: (oh[:, k, :], ol[:, k, :]), S)
                        lin(f"B.gh{n}", hx, S)
                        lin(f"B.bh{n}", lambda k: (yh[:, k, :], yl[:, k, :]), S)
                    pe.wait_ge(mlo_ready, 3)
                    for n in range(NC):
                        lin(f"B.o{n}", hx, S)
                mean_square(f"B.post{j}", view(2048, NC, S), NC, S)

        def splitter(one):
            st = {"s": 0}

            def ahead(name):
                c = plan.name[name]
                done = plan.complete[c - 1] if c else 0
                cap = min(x for x in caps if x >= st["s"])
                for s in range(st["s"], min(cap, max(done + SPL, -(-plan.c[c]["t1"] // TPS)))):
                    one(s)
                    st["s"] = s + 1
            return ahead, st

        def mod_at(col, r):
            return modT[:, col, r:r + 1]

        def x_scale(L, which, r, n):
            l = int(L[1])
            i = {(0, 0): 0, (0, 1): 2, (1, 0): 4, (1, 1): 5}[(l, which)]
            return dv[:, i + r, n:n + 1], mod_at(48 * l + 24 * which + n, r)

        @block.scalar
        def _(act):
            for name in ("cst",):
                act.dma_start(cst[:, :], io[name]).then_inc(consts_in, 16)
            act.dma_start(xs[:, :, 0:S], io["ctxT"].rearrange("(c p) t -> p c t", p=P)).then_inc(consts_in, 16)
            act.dma_start(xs[:, :, S:2 * S], io["xT"].rearrange("(c p) t -> p c t", p=P)).then_inc(consts_in, 16)

            def split_hi(s):
                g = s + NMOD
                act.wait_ge(raw_in[g % RAW], 16 * (g // RAW + 1))
                if s >= SPL:
                    act.wait_ge(pe_step, plan.slot_end[s - SPL])
                act.activation(whi[:, s % SPL, :], raw[:, g % RAW, :], ACT.Copy).then_inc(hi_ready, 1)

            ahead, st = splitter(split_hi)

            def evac(name, *ops):
                ahead(name)
                wait_chunk(act, name)
                for op in ops:
                    ins = op(bank(name))
                ins.then_inc(act_free, 1)

            def squares(label, src, dst):
                act.activation(dst, src, ACT.Square).then_inc(sq_ready, 1)

            def root(label, rst):
                ahead(label)
                wait_free(act, label)
                act.activation(rst, rst, ACT.Sqrt).then_inc(std_ready, 1)

            def his(label, n_of, src, dst):
                for n in range(n_of):
                    act.wait_ge(norm_ready, norm_at(label, n + 1))
                    act.activation(dst(n), src(n), ACT.Copy).then_inc(nhi_ready, 1)

            def attention(l, tiles, scale, oh):
                items = attention_order(l, tiles)
                n = len(items)
                pb = view(7168, 2, S) if l == "B" else view(14336, 2, 512)

                def exps(i):
                    nk = (items[i][1] + 1) * P if l == "B" else S if l == "L0" and items[i][1] < 2 else 2 * S
                    j = i % 2
                    act.wait_ge(nmax_ready, ATTN[l] + i + 1)
                    if l == "B":
                        act.activation(pb[:, j, 0:nk], pb[:, j, 0:nk], ACT.Exp, bias=small[:, j:j + 1],
                                       accum_out=small[:, 2 + j:3 + j]).then_inc(exp_ready, 1)
                        return
                    if i >= 2:
                        wait_chunk(act, f"{l}.PT{i-2}")
                    act.activation(pb[:, j, 0:nk], bank(f"{l}.S{i}")[:, 0:nk], ACT.Exp, bias=small[:, j:j + 1],
                                   scale=scale, accum_out=small[:, 2 + j:3 + j]).then_inc(act_free, 1)

                exps(0)
                for i in range(n + 1):
                    if i + 1 < n:
                        exps(i + 1)
                    if i >= 1 and (i - 1) % 2 == 1:
                        hp, qt, _ = items[i - 1]
                        o = f"{l}.O{(i-1)//2}"
                        wait_chunk(act, o)
                        act.activation(oh[:, hp, qt * P:(qt + 1) * P], bank(o)[:, 0:P], ACT.Copy).then_inc(ohi_ready, 1)

            def merge(l, n, T, sga, sgh):
                if n >= 2:
                    wait_free(act, f"{l}.ba{n-2}")
                evac(f"{l}.ga{n}", lambda o: act.activation(sga[:, n % 2, :], o[:, 0:T], ACT.Sigmoid))
                ahead(f"{l}.ba{n}")
                if n >= 2:
                    wait_free(act, f"{l}.bh{n-2}")
                evac(f"{l}.gh{n}", lambda o: act.activation(sgh[:, n % 2, :], o[:, 0:T], ACT.Sigmoid))
                ahead(f"{l}.bh{n}")

            def feed_forward(name, T):
                L = plan.loops[name]
                assert st["s"] == L["slot"]
                hid_h = view(FF_AT, HALF, T, F32R)
                sg = view(FF_AT + 2 * HALF * T, 2, T)
                h32 = view(FF_AT + 2 * HALF * T + 2 * T, 2, T)
                ends = [plan.slot_end[L["slot"] + s] - L["step"] for s in range(HSLOTS)]
                per = ends[-1]

                with act.Fori(0, L["times"]) as q:
                    def hi(s):
                        g = NMOD + L["slot"] + s
                        act.wait_ge(raw_in[g % RAW], q * (16 * HSLOTS // RAW) + 16 * (g // RAW + 1))
                        e = ends[s - SPL] if s >= SPL else ends[HSLOTS + s - SPL] - per
                        act.wait_ge(pe_step, q * per + (L["step"] + e))
                        act.activation(whi[:, (L["slot"] + s) % SPL, :], raw[:, g % RAW, :], ACT.Copy)\
                           .then_inc(hi_ready, 1)

                    def silu(f):
                        c = plan.c[L["chunk"] + 2 * f]
                        act.wait_ge(pe_step, q * per + c["end"])
                        if f >= 2:
                            act.wait_ge(dve_free, q * HD + (L["D"] + f - 1))
                        act.activation(sg[:, f % 2, :], ps[:, (L["chunk"] + 2 * f) % BANKS, 0:T], ACT.Silu)\
                           .then_inc(act_free, 1)

                    def hid_hi(f):
                        act.wait_ge(dve_free, q * HD + (L["D"] + f + 1))
                        act.activation(hid_h[:, f, :], h32[:, f % 2, :], ACT.Copy).then_inc(hidhi_ready, 1)

                    for f in range(HALF):
                        hi(2 * f)
                        hi(2 * f + 1)
                        if f >= 1:
                            silu(f - 1)
                        if f >= 2:
                            hid_hi(f - 2)
                    hi(2 * HALF)
                    silu(HALF - 1)
                    hid_hi(HALF - 2)
                    hi(2 * HALF + 1)
                    hid_hi(HALF - 1)
                    for s in range(2 * HALF + 2, HSLOTS):
                        hi(s)
                st["s"] = L["slot"] + HSLOTS * L["times"]

            act.wait_ge(consts_in, 64)
            act.activation(view(0, NC, 32), Vv("c3").rearrange("p (k r) -> p k r", k=NC), ACT.Silu)\
               .then_inc(cact_ready, 1)
            rows = view(256, 2, 512)
            for b in range(NMODB):
                if b >= 2:
                    wait_chunk(act, f"modT{b-2}")
                wait_chunk(act, f"mod{b}")
                act.activation(rows[:, b % 2, :], bank(f"mod{b}"), ACT.Copy).then_inc(act_free, 1)
            wait_chunk(act, f"modT{NMODB-1}")
            act.wait_ge(lam_abs, 1)
            e_lam = arena[:, 8256:8264]
            act.activation(e_lam, e_lam, ACT.Exp).then_inc(lam_exp, 1)

            for l, q0, T in LAYERS:
                L = f"L{l}"
                if l == 1:
                    wait_free(act, f"L0.ff.1.d{NC-1}")
                squares(f"{L}.n1", xs[:, :, :], view(0, NC, 512))
                root(f"{L}.n1", arena[:, 4096:4608])
                his(f"{L}.n1", NC, lambda n: view(0, NC, 512)[:, n, :], lambda n: hH[:, n, :])
                for i in range(KVC):
                    ahead(f"{L}.kv{i}")
                wait_free(act, f"{L}.kv{KVC-1}")
                squares(f"{L}.nkv", view(15360, KVC, 512), view(4096, KVC, 512))
                ahead(f"{L}.kr")
                for i in range(QC):
                    ahead(f"{L}.q{i}")
                wait_free(act, f"{L}.q{QC-1}")
                squares(f"{L}.nq", view(8192, QC, T), view(5120, QC, T))
                root(f"{L}.nkv", arena[:, 6656:7168])
                root(f"{L}.nq", arena[:, 7168:7168 + T])
                his(f"{L}.nkv", KVC, lambda n: view(15360, KVC, 512)[:, n, :],
                    lambda n: view(10240, KVC, 512, F32R)[:, n, :])
                his(f"{L}.nq", QC, lambda n: view(8192, QC, T)[:, n, :],
                    lambda n: view(12288, QC, T, F32R)[:, n, :])
                kT = view(0, NH, 512)
                for i in range(4):
                    evac(f"{L}.uk{i}",
                         lambda o: act.activation(kT[0:64, 2 * i, :], o[0:64, :], ACT.Copy),
                         lambda o: act.activation(kT[0:64, 2 * i + 1, :], o[64:128, :], ACT.Copy))
                act.wait_ge(nlo_ready, split_at(f"{L}.nq", QC))
                for i in range(4):
                    evac(f"{L}.uv{i}", lambda o: act.activation(view(8192, 4, 512)[:, i, :], o, ACT.Copy))
                for h in range(NH):
                    ahead(f"{L}.uq{h}")
                attention(L, T // P, SCALE, view(10240, 4, T, F32R))

                ahead(f"f{l}.a")
                act.wait_ge(filt_d, 5 * l + 1)
                for t in range(2):
                    ins = act.activation(view(8192, 2, 1024)[:, t, :], arena[:, 15360:16384], ACT.Exp,
                                         scale=C("negt", t, t + 1))
                ins.then_inc(filt_a, 1)
                for i, at in enumerate((384, 640)):
                    act.wait_ge(filt_d, 5 * l + 2 + i)
                    r = arena[0:FH, 16384 + at:16384 + at + S]
                    act.activation(r, r, ACT.Sin).then_inc(filt_a, 1)
                for c in range(HYC):
                    for v in range(3):
                        ahead(f"{L}.hy{c}{v}")
                        wait_chunk(act, f"{L}.hy{c}{v}")
                ahead(f"{L}.z00")
                for s in range(T // S):
                    u = (0 if l == 0 else 2) + s
                    act.wait_ge(o_ready, u + 1)
                    act.activation(view(0, HYC, T, F32R)[:, :, s * S:(s + 1) * S], view(9216, HYC, S), ACT.Copy)\
                       .then_inc(hyhi_ready, 1)
                for n in range(NC):
                    merge(L, n, T, view(8192, 2, T), view(9216, 2, T))
                act.wait_ge(m_ready, l + 1)
                act.activation(hH[:, :, q0:q0 + T], view(4096, NC, T), ACT.Copy).then_inc(mhi_ready, 1)
                for n in range(NC):
                    ahead(f"{L}.o{n}")
                    wait_chunk(act, f"{L}.o{n}")
                wait_free(act, f"{L}.o{NC-1}")
                squares(f"{L}.n2", xs[:, :, q0:q0 + T], view(0, NC, T))
                root(f"{L}.n2", arena[:, 4096:4096 + T])
                his(f"{L}.n2", NC, lambda n: view(0, NC, T)[:, n, :], lambda n: hH[:, n, q0:q0 + T])
                if l == 1:
                    act.wait_ge(comb_ready, 1)
                    act.activation(small[:, 54:56], small[:, 52:54], ACT.Sigmoid)
                    act.activation(small[:, 56:58], small[:, 52:54], ACT.Sigmoid, scale=-1.0).then_inc(gates_ready, 1)
                feed_forward(f"{L}.ff", T)

            wait_free(act, f"L1.ff.{2*NE-1}.d{NC-1}")
            squares("final", xs[:, :, S:2 * S], view(0, NC, S))
            root("final", arena[:, 4096:4096 + S])
            for j in range(3):
                act.wait_ge(norm_ready, norm_at("final" if j == 0 else f"B.post{j-1}", NC))
                squares(f"B.pre{j}", xs[:, :, S:2 * S], view(0, NC, S))
                root(f"B.pre{j}", arena[:, 4096:4096 + S])
                his(f"B.pre{j}", NC, lambda n: view(0, NC, S)[:, n, :], lambda n: hH[:, n, S:2 * S])
                if j != 1:
                    feed_forward(f"B.ff{j}", S)
                    last = f"B.ff{j}.1.d{NC-1}"
                else:
                    for n in range(8):
                        evac(f"B.qk{n}", lambda o: act.activation(view(2048, 8, S)[:, n, :], o[:, 0:S], ACT.Copy))
                    for i in range(2):
                        evac(f"B.v{i}", lambda o: act.activation(view(4096, 2, 512)[:, i, :], o, ACT.Copy))
                    attention("B", 2, SCALE2, view(5120, 4, S, F32R))
                    for n in range(NC):
                        ahead(f"B.xr{n}")
                        wait_chunk(act, f"B.xr{n}")
                    for n in range(NC):
                        for at, nm, bn in ((7168, "ra", "ba"), (9216, "rx", "bx")):
                            evac(f"B.{nm}{n}", lambda o: act.activation(
                                view(at, NC, S)[:, n, :], o[:, 0:S], ACT.Sigmoid, bias=Vv(bn, n, n + 1)))
                    act.wait_ge(lru_d, 2)
                    act.activation(view(11264, NC, S), view(7168, NC, S), ACT.Exp)
                    act.activation(view(15360, NC, S), view(7168, NC, S), ACT.Tanh).then_inc(lru_a, 1)
                    act.wait_ge(lru_d, 3)
                    act.activation(view(7168, NC, S), view(7168, NC, S), ACT.Sqrt).then_inc(lru_a, 1)
                    for n in range(NC):
                        evac(f"B.yr{n}", lambda o: act.activation(view(15360, NC, S)[:, n, :], o[:, 0:S],
                                                                  ACT.Gelu_apprx_tanh))
                    act.wait_ge(lru_d, 5)
                    act.activation(view(2048, NC, S, F32R), view(11264, NC, S), ACT.Copy).then_inc(lru_a, 1)
                    for n in range(NC):
                        merge("B", n, S, view(15360, 2, S), view(15872, 2, S))
                    act.wait_ge(m_ready, 3)
                    act.activation(hH[:, :, S:2 * S], view(13312, NC, S), ACT.Copy).then_inc(mhi_ready, 1)
                    for n in range(NC):
                        ahead(f"B.o{n}")
                        wait_chunk(act, f"B.o{n}")
                    last = f"B.o{NC-1}"
                wait_free(act, last)
                squares(f"B.post{j}", view(0, NC, S), view(2048, NC, S))
                root(f"B.post{j}", arena[:, 4096:4096 + S])

        @block.vector
        def _(dve):
            chain = [0]

            def link(ins):
                chain[0] += 1
                ins.then_inc(d_link, 1)
                dve.wait_ge(d_link, chain[0])

            def split_lo(s):
                dve.wait_ge(hi_ready, s + 1)
                dve.tensor_tensor(wlo[:, s % SPL, :], raw[:, (NMOD + s) % RAW, :], whi[:, s % SPL, :].bitcast(F32),
                                  ALU.subtract).then_inc(lo_ready, 1)

            ahead, st = splitter(split_lo)

            def evac(name, *ops):
                ahead(name)
                wait_chunk(dve, name)
                for i, op in enumerate(ops):
                    ins = op(bank(name))
                    if i < len(ops) - 1:
                        link(ins)
                ins.then_inc(dve_free, 1)

            def norm(label, dim, T, rst, n_of, src, gain, shift, h32, lo, hi):
                variance(label, dim, T, rst)
                normalise(label, T, rst, n_of, src, gain, shift, h32, lo, hi)

            def variance(label, dim, T, rst):
                evac(label, lambda o: dve.tensor_scalar(rst, o[:, 0:T], 1.0 / dim, EPS, ALU.mult, ALU.add))

            def normalise(label, T, rst, n_of, src, gain, shift, h32, lo, hi):
                dve.wait_ge(std_ready, NORMS.index(label) + 1)
                link(dve.reciprocal(rst, rst))
                streams = 1 if shift is None else T // S

                def low(n):
                    dve.wait_ge(nhi_ready, split_at(label, n + 1))
                    dve.tensor_tensor(lo(n), h32(n), hi(n).bitcast(F32), ALU.subtract).then_inc(nlo_ready, 1)

                for n in range(n_of):
                    w = T // streams
                    for r in range(streams):
                        c = slice(r * w, (r + 1) * w)
                        ins = dve.scalar_tensor_tensor(out=h32(n)[:, c], in0=src(n)[:, c], scalar=gain(r, n),
                                                       in1=rst[:, c], op0=ALU.mult, op1=ALU.mult)
                    if shift is not None:
                        link(ins)
                        for r in range(streams):
                            c = slice(r * w, (r + 1) * w)
                            ins = dve.tensor_scalar(h32(n)[:, c], h32(n)[:, c], shift(r, n), None, ALU.add)
                    ins.then_inc(norm_ready, 1)
                    if lo is not None and n:
                        low(n - 1)
                if lo is not None:
                    low(n_of - 1)

            def rope(name, T, at, dst, head, rest):
                ta, tb = arena[64:96, 16384:16384 + T], arena[64:96, 16896:16896 + T]
                w = slice(512 - T, 512) if T < 512 else slice(0, 512)
                ops = [lambda o: dve.tensor_copy(dst[0:64, head, :], o[0:64, 0:T])] if rest else []
                ahead(name)
                wait_chunk(dve, name)
                o = bank(name)
                if rest:
                    dve.tensor_copy(dst[0:64, head, :], o[0:64, 0:T])
                dve.tensor_tensor(ta, o[64:96, 0:T], C("cos")[64:96, w], ALU.mult)
                dve.tensor_tensor(tb, o[96:128, 0:T], C("sin")[96:128, w], ALU.mult).then_inc(dve_free, 1)
                wait_free(dve, name)
                dve.tensor_tensor(dst[64:96, head, :], ta, tb, ALU.add).then_inc(rope_ready, 1)
                dve.wait_ge(rope_ready, at)

            def attention(l, tiles, scale, oh, ol):
                items = attention_order(l, tiles)
                n = len(items)
                B = l == "B"
                pb = view(7168, 2, S) if B else view(14336, 2, 512)
                pT = view(8192, 2, S) if B else view(15360, 2, 512)
                bias = view(9216, 16, S)

                def keys(i):
                    return (items[i][1] + 1) * P if B else S if l == "L0" and items[i][1] < 2 else 2 * S

                def maxima(i):
                    hp, qt, hh = items[i]
                    nk, j = keys(i), i % 2
                    wait_chunk(dve, f"{l}.S{i}")
                    s = bank(f"{l}.S{i}")[:, 0:nk]
                    if B:
                        if i >= 2:
                            wait_chunk(dve, f"B.PT{i-2}")
                        dve.scalar_tensor_tensor(out=pb[:, j, 0:nk], in0=s, scalar=scale,
                                                 in1=bias[:, qt * NH + 2 * hp + hh, 0:nk], op0=ALU.mult, op1=ALU.add)\
                           .then_inc(dve_free, 1)
                        wait_free(dve, f"B.S{i}")
                        link(dve.memset(pb[0:64, j, nk - 64:nk], -3.4028234663852886e38))
                        s = pb[:, j, 0:nk]
                    link(dve.tensor_reduce(small[:, 4 + j:5 + j], s, AX.X, ALU.max))
                    dve.tensor_scalar(small[:, j:j + 1], small[:, 4 + j:5 + j], -1.0 if B else -scale, None, ALU.mult)\
                       .then_inc(nmax_ready, 1)

                def probs(i):
                    j = i % 2
                    if B:
                        dve.wait_ge(exp_ready, i + 1)
                    else:
                        wait_free(dve, f"{l}.S{i}")
                    link(dve.reciprocal(small[:, 6 + j:7 + j], small[:, 2 + j:3 + j]))
                    dve.tensor_scalar(pb[:, j, 0:keys(i)], pb[:, j, 0:keys(i)], small[:, 6 + j:7 + j], None, ALU.mult)\
                       .then_inc(prob_ready, 1)

                maxima(0)
                for i in range(n + 1):
                    if i < n:
                        probs(i)
                    if i + 1 < n:
                        maxima(i + 1)
                    if i < n:
                        wait_chunk(dve, f"{l}.PT{i}")
                        if i >= 2:
                            wait_chunk(dve, f"{l}.O{(i-2)//2}")
                        dve.tensor_copy(pT[:, i % 2, 0:keys(i)], bank(f"{l}.PT{i}")[:, 0:keys(i)]).then_inc(dve_free, 1)
                    if i >= 1 and (i - 1) % 2 == 1:
                        hp, qt, _ = items[i - 1]
                        o = f"{l}.O{(i-1)//2}"
                        dve.wait_ge(ohi_ready, (ATTN[l] + i) // 2)
                        c = slice(qt * P, (qt + 1) * P)
                        dve.tensor_tensor(ol[:, hp, c], bank(o)[:, 0:P], oh[:, hp, c].bitcast(F32), ALU.subtract)\
                           .then_inc(dve_free, 1)

            def sine_argument(name, l, i, at, tmp):
                x, k = arena[0:FH, 16384 + at:16384 + at + S], arena[0:FH, 16384 + tmp:16384 + tmp + S]
                evac(name, lambda o: dve.tensor_scalar(x, o[0:FH, 0:S], Vv(f"fb{i}{l}")[0:FH, :], Vv(f"freq{l}")[0:FH, :],
                                                       ALU.add, ALU.mult))
                wait_free(dve, name)
                big = 1.5 * 2 ** 23
                link(dve.tensor_scalar(k, x, 1 / (2 * math.pi), big, ALU.mult, ALU.add))
                link(dve.tensor_scalar(k, k, big, None, ALU.subtract))
                link(dve.scalar_tensor_tensor(out=x, in0=k, scalar=-6.28125, in1=x, op0=ALU.mult, op1=ALU.add))
                link(dve.scalar_tensor_tensor(out=x, in0=k, scalar=-(2 * math.pi - 6.28125), in1=x, op0=ALU.mult,
                                              op1=ALU.add))
                dve.tensor_scalar(x, x, 3.1415925, -3.1415925, ALU.min, ALU.max).then_inc(filt_d, 1)

            def merge(l, n, T, sga, sgh, M, tmp, last):
                ahead(f"{l}.ga{n}")
                wait_free(dve, f"{l}.ga{n}")
                evac(f"{l}.ba{n}", lambda o: dve.tensor_tensor(M[:, n, :], sga[:, n % 2, :], o[:, 0:T], ALU.mult))
                ahead(f"{l}.gh{n}")
                wait_free(dve, f"{l}.gh{n}")
                evac(f"{l}.bh{n}", lambda o: dve.tensor_tensor(tmp, sgh[:, n % 2, :], o[:, 0:T], ALU.mult))
                wait_free(dve, f"{l}.bh{n}")
                ins = dve.tensor_tensor(M[:, n, :], M[:, n, :], tmp, ALU.add)
                if last:
                    ins.then_inc(m_ready, 1)
                else:
                    link(ins)

            def merged_low(k, hi, lo, M):
                dve.wait_ge(mhi_ready, k)
                dve.tensor_tensor(lo, M, hi.bitcast(F32), ALU.subtract).then_inc(mlo_ready, 1)

            def feed_forward(name, T, gate, acc, streams, experts=None):
                L = plan.loops[name]
                assert st["s"] == L["slot"]
                sg = view(FF_AT + 2 * HALF * T, 2, T)
                h32 = view(FF_AT + 2 * HALF * T + 2 * T, 2, T)
                per = plan.slot_end[L["slot"] + HSLOTS - 1] - L["step"]

                def turn(q, cb, e0):
                    def lo(s):
                        g = NMOD + L["slot"] + s
                        dve.wait_ge(hi_ready, q * HSLOTS + (L["slot"] + s + 1))
                        dve.tensor_tensor(wlo[:, (L["slot"] + s) % SPL, :], raw[:, g % RAW, :],
                                          whi[:, (L["slot"] + s) % SPL, :].bitcast(F32), ALU.subtract)\
                           .then_inc(lo_ready, 1)

                    def mul(f):
                        c = plan.c[L["chunk"] + 2 * f + 1]
                        dve.wait_ge(act_free, q * HA + (L["A"] + f + 1))
                        if cb is not None:
                            dve.tensor_tensor(sg[:, f % 2, :], sg[:, f % 2, :], cb, ALU.mult).then_inc(comb_ready, 1)
                            dve.wait_ge(comb_ready, q * HALF + (f + 3))
                        dve.wait_ge(pe_step, q * per + c["end"])
                        if f >= 2:
                            dve.wait_ge(hidlo_ready, q * HALF + (L["half"] * HALF + f - 1))
                        dve.tensor_tensor(h32[:, f % 2, :], sg[:, f % 2, :],
                                          ps[:, (L["chunk"] + 2 * f + 1) % BANKS, 0:T], ALU.mult).then_inc(dve_free, 1)

                    for f in range(HALF):
                        lo(2 * f)
                        lo(2 * f + 1)
                        if f >= 1:
                            mul(f - 1)
                    lo(2 * HALF)
                    mul(HALF - 1)
                    nxt = 2 * HALF + 1
                    for n in range(NC):
                        while nxt < min(HSLOTS, 2 * HALF + (HALF * n) // TPS + SPL):
                            lo(nxt)
                            nxt += 1
                        c = plan.c[L["chunk"] + 2 * HALF + n]
                        dve.wait_ge(pe_step, q * per + c["end"])
                        for r in range(streams):
                            cs = slice(r * S, (r + 1) * S)
                            ins = dve.scalar_tensor_tensor(
                                out=acc(n)[:, cs], in0=ps[:, (L["chunk"] + 2 * HALF + n) % BANKS, cs],
                                scalar=gate(r, n), in1=acc(n)[:, cs], op0=ALU.mult, op1=ALU.add)
                        ins.then_inc(dve_free, 1)
                        dve.wait_ge(dve_free, q * HD + (L["D"] + HALF + n + 1))

                with dve.Fori(0, L["times"]) as q:
                    cb = None
                    if experts is not None:
                        cb = experts(q)
                    turn(q, cb, 0)
                st["s"] = L["slot"] + HSLOTS * L["times"]

            for b in range(NMODB):
                wait_chunk(dve, f"modT{b}")
                o = bank(f"modT{b}").rearrange("p (q j r) -> p q r j", q=4, j=4)
                dve.tensor_reduce(modT[:, 4 * b:4 * b + 4, :], o[:, :, 0:3, :], AX.X, ALU.add).then_inc(dve_free, 1)
            wait_free(dve, f"modT{NMODB-1}")
            dve.wait_ge(consts_in, 64)
            for l in range(2):
                for r in range(2):
                    m = modT[:, 48 * l:48 * l + 48, r]
                    dve.tensor_tensor(m, m, Vv(f"bm{l}"), ALU.add)
            m = modT[:, 96:168, 2]
            link(dve.tensor_tensor(m, m, Vv("bm2"), ALU.add))

            def scale_vector(i, col, r, g):
                dve.scalar_tensor_tensor(out=dv[:, i, :], in0=modT[:, col:col + NC, r], scalar=1.0, in1=g,
                                         op0=ALU.add, op1=ALU.mult)
            for l in range(2):
                for which in range(2):
                    for r in range(2):
                        i = {(0, 0): 0, (0, 1): 2, (1, 0): 4}.get((l, which))
                        if (l, which) == (1, 1):
                            if r == 0:
                                continue
                            i = 5
                        scale_vector(i + r, 48 * l + 24 * which + 8, r, Vv(f"n{which+1}{l}"))
            for j in range(3):
                scale_vector(7 + j, 96 + 24 * j + 8, 2, Vv("pre", 8 * j, 8 * j + 8))
                dve.scalar_tensor_tensor(out=dv[:, 10 + j, :], in0=modT[:, 96 + 24 * j + 16:96 + 24 * j + 24, 2],
                                         scalar=(0.5, 1.0, 0.5)[j], in1=Vv("post", 8 * j, 8 * j + 8),
                                         op0=ALU.mult, op1=ALU.mult)
            a, e, s2, acc_ = (arena[:, 8192 + 64 * i:8200 + 64 * i] for i in range(4))
            dve.tensor_scalar(dv[:, 13, :], Vv("lam"), -1.0, 0.0, ALU.mult, ALU.max)
            link(dve.scalar_tensor_tensor(out=a, in0=Vv("lam"), scalar=-1.0, in1=Vv("lam"), op0=ALU.mult, op1=ALU.max))
            dve.tensor_scalar(e, a, -1.0, None, ALU.mult).then_inc(lam_abs, 1)
            dve.wait_ge(lam_exp, 1)
            link(dve.tensor_scalar(a, e, 2.0, None, ALU.add))
            link(dve.reciprocal(a, a))
            link(dve.tensor_tensor(a, a, e, ALU.mult))
            link(dve.tensor_tensor(s2, a, a, ALU.mult))
            link(dve.tensor_scalar(acc_, s2, 1 / 15, 1 / 13, ALU.mult, ALU.add))
            for c in (1 / 11, 1 / 9, 1 / 7, 1 / 5, 1 / 3, 1.0):
                link(dve.tensor_tensor(acc_, acc_, s2, ALU.mult))
                link(dve.tensor_scalar(acc_, acc_, c, None, ALU.add))
            link(dve.tensor_tensor(acc_, acc_, a, ALU.mult))
            link(dve.scalar_tensor_tensor(out=acc_, in0=acc_, scalar=2.0, in1=dv[:, 13, :], op0=ALU.mult, op1=ALU.add))
            link(dve.tensor_scalar(dv[:, 13, :], acc_, -8.0, None, ALU.mult))

            for l, q0, T in LAYERS:
                L = f"L{l}"
                hf = view(0, NC, 512)
                norm(f"{L}.n1", D, 512, arena[:, 4096:4608], NC, lambda n: xs[:, n, :],
                     lambda r, n: x_scale(L, 0, r, n)[0], lambda r, n: x_scale(L, 0, r, n)[1],
                     lambda n: hf[:, n, :], lambda n: hL[:, n, :], lambda n: hH[:, n, :])
                pkv, pq = view(15360, KVC, 512), view(8192, QC, T)
                for i in range(KVC):
                    evac(f"{L}.kv{i}", lambda o: dve.tensor_copy(pkv[:, i, :], o))
                kT, qT = view(0, NH, 512), view(4096, NH, T)
                for_l = l * (NH + 1)
                rope(f"{L}.kr", 512, for_l + 1, kT, 0, False)
                for h in range(1, NH):
                    ins = dve.tensor_copy(kT[64:96, h, :], kT[64:96, 0, :])
                link(ins)
                for i in range(QC):
                    evac(f"{L}.q{i}", lambda o: dve.tensor_copy(pq[:, i, :], o[:, 0:T]))
                rkv, rq = arena[:, 6656:7168], arena[:, 7168:7168 + T]
                variance(f"{L}.nkv", KV_LORA, 512, rkv)
                variance(f"{L}.nq", Q_LORA, T, rq)
                normalise(f"{L}.nkv", 512, rkv, KVC, lambda n: pkv[:, n, :], lambda r, n: Vv(f"kvn{l}", n, n + 1), None,
                          lambda n: pkv[:, n, :], lambda n: view(11264, KVC, 512, F32R)[:, n, :],
                          lambda n: view(10240, KVC, 512, F32R)[:, n, :])
                normalise(f"{L}.nq", T, rq, QC, lambda n: pq[:, n, :], lambda r, n: Vv(f"qn{l}", n, n + 1), None,
                          lambda n: pq[:, n, :], lambda n: view(12288 + 1536, QC, T, F32R)[:, n, :],
                          lambda n: view(12288, QC, T, F32R)[:, n, :])
                for i in range(4):
                    ahead(f"{L}.uk{i}")
                for i in range(4):
                    ahead(f"{L}.uv{i}")
                for h in range(NH):
                    rope(f"{L}.uq{h}", T, for_l + 2 + h, qT, h, True)
                oh, ol = view(10240, 4, T, F32R), view(12288, 4, T, F32R)
                attention(L, T // P, SCALE, oh, ol)

                dve.wait_ge(filt_in, 16 * 5 * (l + 1))
                dec = arena[:, 15360:16384]
                dve.scalar_tensor_tensor(out=dec, in0=dec, scalar=-1.0, in1=dec, op0=ALU.mult, op1=ALU.max).then_inc(filt_d, 1)
                sine_argument(f"f{l}.a", l, 1, 384, 640)
                sine_argument(f"f{l}.b", l, 2, 640, 384)
                hh, E = view(4096, 4, 512), view(8192, 4, 512)
                dve.wait_ge(filt_a, 3 * l + 1)
                for t in range(4):
                    evac(f"f{l}.h{t}", lambda o: dve.scalar_tensor_tensor(
                        out=hh[:, t, :], in0=o, scalar=C("h1m", t // 2, t // 2 + 1) if t % 2 else 1.0, in1=E[:, t, :],
                        op0=ALU.mult, op1=ALU.mult))
                wait_free(dve, f"f{l}.h3")
                dve.scalar_tensor_tensor(out=view(14336, 4, 512), in0=hh, scalar=-1.0, in1=hh, op0=ALU.mult, op1=ALU.max).then_inc(filt_d, 1)
                evac(f"f{l}.sum", lambda o: dve.reciprocal(small[:, 8:12], o[:, 0:HYC]))
                h4 = arena[:, 4096:6144].rearrange("p (t w c) -> p t w c", t=2, w=2)
                dve.tensor_tensor(view(14336, 2, 512), h4[:, :, 0, :], h4[:, :, 1, :], ALU.add)
                dve.tensor_tensor(view(15360, 2, 512), h4[:, :, 0, :], h4[:, :, 1, :], ALU.subtract).then_inc(filt_d, 1)
                KF = view(6144, 4, 512)
                for f in range(4):
                    evac(f"f{l}.K{f}", lambda o: dve.tensor_copy(KF[:, f, :], o))

                zT, x0 = view(0, HYC, T), view(2048, HYC, T)
                U = view(16384, 2, T)
                for c in range(HYC):
                    for v in range(3):
                        dst = x0[:, c, :] if v == 2 else U[:, v, :]
                        d3 = dst.rearrange("p (s t) -> p s t", t=S)
                        w = [Vv(f"sw{l}", 12 * j + 4 * v + c, 12 * j + 4 * v + c + 1) for j in range(3)]
                        bb = Vv(f"sb{l}", 4 * v + c, 4 * v + c + 1)

                        def o3(o):
                            return o[:, 0:T].rearrange("p (s t) -> p s t", t=S)
                        evac(f"{L}.hy{c}{v}",
                             lambda o: dve.tensor_scalar(dst, o[:, 0:T], w[1], bb, ALU.mult, ALU.add),
                             lambda o: dve.scalar_tensor_tensor(out=d3[:, :, 1:S], in0=o3(o)[:, :, 0:S - 1], scalar=w[0],
                                                                in1=d3[:, :, 1:S], op0=ALU.mult, op1=ALU.add),
                             lambda o: dve.scalar_tensor_tensor(out=d3[:, :, 0:S - 1], in0=o3(o)[:, :, 1:S], scalar=w[2],
                                                                in1=d3[:, :, 0:S - 1], op0=ALU.mult, op1=ALU.add))
                        if v == 1:
                            wait_free(dve, f"{L}.hy{c}1")
                            ins = dve.tensor_tensor(zT[:, c, :], U[:, 0, :], U[:, 1, :], ALU.mult)
                            if c == HYC - 1:
                                ins.then_inc(z_ready, 1)
                            else:
                                link(ins)
                dve.wait_ge(z_ready, l + 1)
                wait_free(dve, f"{L}.hy{HYC-1}2")
                zrow, Z, Y, T1 = view(8192, 2, 512), view(14336, 4, 512), view(4096, 4, 512), view(9216, 2, 512)
                for s in range(T // S):
                    u = (0 if l == 0 else 2) + s
                    for t in range(2):
                        evac(f"{L}.z{s}{t}", lambda o: dve.tensor_copy(zrow[:, t, :], o))
                    for f in range(4):
                        evac(f"{L}.Z{s}{f}", lambda o: dve.tensor_copy(Z[:, f, :], o))
                    wait_free(dve, f"{L}.Z{s}3")
                    dve.tensor_tensor(T1, Z[:, 2:4, :], KF[:, 2:4, :], ALU.mult)
                    dve.tensor_tensor(Y[:, 2:4, :], Z[:, 0:2, :], KF[:, 2:4, :], ALU.mult)
                    link(dve.tensor_tensor(Y[:, 0:2, :], Z[:, 0:2, :], KF[:, 0:2, :], ALU.mult))
                    link(dve.tensor_tensor(Z[:, 0:2, :], Z[:, 2:4, :], KF[:, 0:2, :], ALU.mult))
                    for t in range(2):
                        dve.scalar_tensor_tensor(out=Y[:, t, :], in0=T1[:, t, :], scalar=C("negm", t, t + 1),
                                                 in1=Y[:, t, :], op0=ALU.mult, op1=ALU.add)
                    link(dve.tensor_tensor(Y[:, 2:4, :], Y[:, 2:4, :], Z[:, 0:2, :], ALU.add))
                    dve.tensor_copy(Y[0:1, 2, :], T1[0:1, 0, :]).then_inc(Y_ready, 1)
                    dve.wait_ge(Y_ready, u + 1)
                    o32, tmp = view(9216, HYC, S), view(14336, 2, S)
                    for c in range(HYC):
                        zc, xc = zT[:, c, s * S:(s + 1) * S], x0[:, c, s * S:(s + 1) * S]
                        link(dve.tensor_scalar(tmp[:, 0, :], zc, Vv(f"hb{l}", c, c + 1), None, ALU.mult))
                        evac(f"{L}.y{s}{c}", lambda o: dve.scalar_tensor_tensor(
                            out=tmp[:, 1, :], in0=o[:, 0:S], scalar=small[:, 8 + c:9 + c], in1=tmp[:, 0, :],
                            op0=ALU.mult, op1=ALU.add))
                        wait_free(dve, f"{L}.y{s}{c}")
                        ins = dve.tensor_tensor(o32[:, c, :], tmp[:, 1, :], xc, ALU.mult)
                        if c == HYC - 1:
                            ins.then_inc(o_ready, 1)
                        else:
                            link(ins)
                    dve.wait_ge(hyhi_ready, u + 1)
                    dve.tensor_tensor(view(2048, HYC, T, F32R)[:, :, s * S:(s + 1) * S], o32,
                                      view(0, HYC, T, F32R)[:, :, s * S:(s + 1) * S].bitcast(F32), ALU.subtract)\
                        .then_inc(hylo_ready, 1)
                    dve.wait_ge(hylo_ready, u + 1)
                M = view(4096, NC, T)
                for n in range(NC):
                    merge(L, n, T, view(8192, 2, T), view(9216, 2, T), M, arena[:, 14336:14336 + T], n == NC - 1)
                merged_low(l + 1, hH[:, :, q0:q0 + T], hL[:, :, q0:q0 + T], M)
                for n in range(NC):
                    ops = []
                    ahead(f"{L}.o{n}")
                    wait_chunk(dve, f"{L}.o{n}")
                    for s in range(T // S):
                        r = 1 if l == 1 else s
                        xv = xs[:, n, q0 + s * S:q0 + (s + 1) * S]
                        ins = dve.scalar_tensor_tensor(out=xv, in0=bank(f"{L}.o{n}")[:, s * S:(s + 1) * S],
                                                       scalar=mod_at(48 * l + 16 + n, r), in1=xv, op0=ALU.mult,
                                                       op1=ALU.add)
                    ins.then_inc(dve_free, 1)
                hf = view(0, NC, T)
                norm(f"{L}.n2", D, T, arena[:, 4096:4096 + T], NC, lambda n: xs[:, n, q0:q0 + T],
                     lambda r, n: x_scale(L, 1, r + l, n)[0], lambda r, n: x_scale(L, 1, r + l, n)[1],
                     lambda n: hf[:, n, :], lambda n: hL[:, n, q0:q0 + T], lambda n: hH[:, n, q0:q0 + T])
                experts = None
                if l == 1:
                    lg, top, cmb = small[:, 24:32], small[:, 32:40], small[:, 64:80]
                    for t in range(2):
                        evac(f"route{t}", lambda o: dve.tensor_copy(lg, o[:, 0:NE]))
                        wait_free(dve, f"route{t}")
                        link(dve.max(top, lg))
                        link(dve.max_index(idx[:, :], top, lg))
                        link(dve.tensor_copy(small[:, 58 + 2 * t:60 + 2 * t], idx[:, 0:2]))
                        ins = dve.tensor_tensor(small[:, 52 + t:53 + t], top[:, 0:1], top[:, 1:2], ALU.subtract)
                        if t == 1:
                            ins.then_inc(comb_ready, 1)
                        else:
                            link(ins)
                    dve.wait_ge(gates_ready, 1)
                    for t in range(2):
                        i0, i1 = small[:, 58 + 2 * t:59 + 2 * t], small[:, 59 + 2 * t:60 + 2 * t]
                        dve.tensor_scalar(lg, C("iota"), i0, small[:, 54 + t:55 + t], ALU.is_equal, ALU.mult)
                        link(dve.tensor_scalar(top, C("iota"), i1, small[:, 56 + t:57 + t], ALU.is_equal, ALU.mult))
                        link(dve.tensor_tensor(cmb[:, 8 * t:8 * t + 8], lg, top, ALU.add))
                    cbE = view(2048, 16, P)
                    for e in range(NE):
                        for t in range(2):
                            ins = dve.tensor_scalar(cbE[:, 2 * e + t, :], ones, cmb[:, 8 * t + e:8 * t + e + 1], None,
                                                    ALU.mult)
                    ins.then_inc(comb_ready, 1)
                    cb = arena[:, 11264:13312]
                    for e2 in range(NE // 2):
                        evac(f"cb{e2}", lambda o: dve.tensor_copy(cb[:, e2 * 512:(e2 + 1) * 512], o))
                    cb2 = arena[:, 13312:17408].rearrange("p (e j t) -> p e j t", e=NE, j=2)
                    wait_free(dve, f"cb{NE//2-1}")
                    for j in range(2):
                        ins = dve.tensor_copy(cb2[:, :, j, :], cb.rearrange("p (e t) -> p e t", e=NE))
                    link(ins)
                    experts = lambda q: arena[:, bass.ds(q * S + 13312, S)]
                feed_forward(f"{L}.ff", T, lambda r, n: mod_at(48 * l + 40 + n, r + l),
                             lambda n: xs[:, n, q0:q0 + T], T // S, experts)

            xl = lambda n: xs[:, n, S:2 * S]
            norm("final", D, S, arena[:, 4096:4096 + S], NC, xl, lambda r, n: Vv("fg", n, n + 1), None, xl, None, None)
            fh = view(0, NC, S)
            for j in range(3):
                norm(f"B.pre{j}", D, S, arena[:, 4096:4096 + S], NC, xl, lambda r, n: dv[:, 7 + j, n:n + 1],
                     lambda r, n: mod_at(96 + 24 * j + n, 2), lambda n: fh[:, n, :], lambda n: hL[:, n, S:2 * S],
                     lambda n: hH[:, n, S:2 * S])
                if j != 1:
                    dve.wait_ge(nlo_ready, split_at(f"B.pre{j}", NC))
                    link(dve.memset(fh, 0.0))
                    feed_forward(f"B.ff{j}", S, lambda r, n: 1.0, lambda n: fh[:, n, :], 1)
                else:
                    for n in range(8):
                        ahead(f"B.qk{n}")
                    for i in range(2):
                        ahead(f"B.v{i}")
                    dve.wait_ge(blk_in, 32)
                    attention("B", 2, SCALE2, view(5120, 4, S, F32R), view(6144, 4, S, F32R))
                    xc = view(2048, NC, S)
                    for n in range(NC):
                        w = [Vv("cw", 8 * i + n, 8 * i + n + 1) for i in range(4)]

                        def tap(i):
                            return lambda o: dve.scalar_tensor_tensor(
                                out=xc[:, n, i:S], in0=o[:, 0:S - i], scalar=w[3 - i], in1=xc[:, n, i:S],
                                op0=ALU.mult, op1=ALU.add)
                        evac(f"B.xr{n}",
                             lambda o: dve.tensor_scalar(xc[:, n, :], o[:, 0:S], w[3], Vv("cb", n, n + 1), ALU.mult,
                                                         ALU.add), tap(1), tap(2), tap(3))
                    wait_free(dve, f"B.xr{NC-1}")
                    link(dve.tensor_copy(small[:, 90:91], small[:, 8:9]))
                    dve.tensor_copy(small[:, 91:92], small[:, 8:9]).then_inc(lru_d, 1)
                    for n in range(NC):
                        ahead(f"B.ra{n}")
                        ahead(f"B.rx{n}")
                    rr, ii, aa, th = view(7168, NC, S), view(9216, NC, S), view(11264, NC, S), view(15360, NC, S)
                    wait_free(dve, f"B.rx{NC-1}")
                    for n in range(NC):
                        ins = dve.tensor_scalar(rr[:, n, :], rr[:, n, :], dv[:, 13, n:n + 1], None, ALU.mult)
                    ins.then_inc(lru_d, 1)
                    link(dve.tensor_tensor(ii, ii, xc, ALU.mult))
                    dve.wait_ge(lru_a, 1)
                    link(dve.tensor_scalar(rr, th, -1.0, 1.0, ALU.mult, ALU.add))
                    link(dve.reciprocal(rr, rr))
                    link(dve.tensor_tensor(rr, rr, th, ALU.mult))
                    dve.tensor_scalar(rr, rr, -2.0, 0.0, ALU.mult, ALU.max).then_inc(lru_d, 1)
                    dve.wait_ge(lru_a, 2)
                    link(dve.tensor_tensor(rr, rr, ii, ALU.mult))
                    for n in range(NC):
                        ins = dve.tensor_tensor_scan(ii[:, n, :], aa[:, n, :], rr[:, n, :], 0.0, ALU.mult, ALU.add)
                    ins.then_inc(lru_d, 1)
                    dve.wait_ge(lru_d, 4)
                    for n in range(NC):
                        ahead(f"B.yr{n}")
                        wait_free(dve, f"B.yr{n}")
                    dve.tensor_tensor(aa, ii, th, ALU.mult).then_inc(lru_d, 1)
                    dve.wait_ge(lru_a, 3)
                    dve.tensor_tensor(view(7168, NC, S, F32R), aa, view(2048, NC, S, F32R).bitcast(F32),
                                      ALU.subtract).then_inc(lru_d, 1)
                    M = view(13312, NC, S)
                    for n in range(NC):
                        merge("B", n, S, view(15360, 2, S), view(15872, 2, S), M, arena[:, 16384:16384 + S],
                              n == NC - 1)
                    merged_low(3, hH[:, :, S:2 * S], hL[:, :, S:2 * S], M)
                    for n in range(NC):
                        evac(f"B.o{n}", lambda o: dve.tensor_copy(fh[:, n, :], o[:, 0:S]))
                rst, t32 = arena[:, 4096:4096 + S], view(2048, NC, S)
                variance(f"B.post{j}", D, S, rst)
                dve.wait_ge(std_ready, NORMS.index(f"B.post{j}") + 1)
                link(dve.reciprocal(rst, rst))
                for n in range(NC):
                    link(dve.scalar_tensor_tensor(out=t32[:, n, :], in0=fh[:, n, :], scalar=dv[:, 10 + j, n:n + 1],
                                                  in1=rst, op0=ALU.mult, op1=ALU.mult))
                    dve.tensor_tensor(xl(n), xl(n), t32[:, n, :], ALU.add).then_inc(norm_ready, 1)
            dve.wait_ge(norm_ready, norm_at("B.post2", NC))
            dve.tensor_copy(small[:, 92:93], small[:, 8:9]).then_inc(out_ready, 1)

        @block.gpsimd
        def _(pool):
            def hidden_low(name, T):
                L = plan.loops[name]
                hid_h, hid_l = view(FF_AT, HALF, T, F32R).bitcast(F32), view(FF_AT + HALF * T, HALF, T, F32R)
                h32 = view(FF_AT + 2 * HALF * T + 2 * T, 2, T)
                with pool.Fori(0, L["times"]) as q:
                    for f in range(HALF):
                        pool.wait_ge(hidhi_ready, q * HALF + (L["half"] * HALF + f + 1))
                        pool.tensor_tensor(hid_l[:, f, :], h32[:, f % 2, :], hid_h[:, f, :], ALU.subtract)\
                            .then_inc(hidlo_ready, 1)

            for l, q0, T in LAYERS:
                wait_free(pool, f"L{l}.O{len(attention_order('', T // P)) // 2 - 1}")
                fw = 16384
                pool.dma_start(arena[0:EMB, fw:fw + 64], io["fw1"][l]).then_inc(filt_in, 16)
                pool.dma_start(arena[0:FH, fw + 64:fw + 128], io["fw2"][l]).then_inc(filt_in, 16)
                pool.dma_start(arena[0:EMB, fw + 128:fw + 384], io["emb"]).then_inc(filt_in, 16)
                pool.dma_start(arena[0:FH, 14336:15360], io["fw3"][l]).then_inc(filt_in, 16)
                pool.dma_start(arena[:, 15360:16384], io["decay"][l:l + 1, :].broadcast_to([P, 1024]))\
                    .then_inc(filt_in, 16)
                hidden_low(f"L{l}.ff", T)
            hidden_low("B.ff0", S)
            wait_free(pool, f"B.ff0.1.d{NC-1}")
            pool.dma_start(arena[:, 9216:13312], io["bias"]).then_inc(blk_in, 16)
            pool.dma_start(arena[:, 13312:15360], io["lru"]).then_inc(blk_in, 16)
            hidden_low("B.ff2", S)


def _tiles(w):
    k, n = w.shape
    return w.reshape(k // P, P, n // P, P).transpose(2, 0, 1, 3).reshape(-1, P, P)


def _rows(w):
    k, n = w.shape
    return w.reshape(k // P, P, n // P, P).transpose(0, 2, 1, 3).reshape(-1, P, P)


def _cols(v):
    return v.reshape(-1, P).T


def _constants():
    c = np.zeros((P, NCST), np.float32)

    def put(name, a, rows=slice(0, P)):
        at, w = CST[name]
        c[rows, at:at + w] = a
    put("ident", np.eye(P))
    put("ones", 1.0)
    t = np.arange(S)
    f = np.arange(S)
    ang = 2 * np.pi * ((t[:, None] * f[None, :]) % (2 * S)) / (2 * S)
    Fr, Fi = np.cos(ang), -np.sin(ang)
    Fi[:, 0] = (-1.0) ** t
    F = np.concatenate([Fr, Fi], 1)
    put("F", F.reshape(2, P, 2 * S).transpose(1, 0, 2).reshape(P, -1))
    Gr, Gi = 2 * np.cos(ang).T / (2 * S), -2 * np.sin(ang).T / (2 * S)
    Gr[0] = 1 / (2 * S)
    Gi[0] = (-1.0) ** t / (2 * S)
    G = np.concatenate([Gr, Gi], 0)
    put("G", G.reshape(4, P, S).transpose(1, 0, 2).reshape(P, -1))
    alt = np.zeros((P, P))
    alt[:, 0] = 2 * (-1.0) ** np.arange(P)
    put("alt2", alt)
    nf = ROPE // 4
    inv = (np.float32(10000.0) ** (-np.arange(nf, dtype=np.float32) / np.float32(nf))).astype(np.float32)
    r = np.repeat(np.arange(S // 64, dtype=np.float32), 64)
    col = np.tile(np.arange(64, dtype=np.float32), S // 64)
    a = np.concatenate([r[:, None] * inv, col[:, None] * inv], -1)
    cos, sin = np.cos(a).T, np.sin(a).T
    put("cos", np.concatenate([np.ones((ROPE, S)), np.concatenate([cos, cos], 0)], 1), slice(64, 96))
    put("sin", np.concatenate([np.zeros((ROPE, S)), np.concatenate([-sin, sin], 0)], 1), slice(96, 128))
    put("iota", np.arange(NE)[None, :])
    lin = np.linspace(0.0, 1.0, S, dtype=np.float32)
    put("negt", -lin.reshape(2, P).T)
    m = np.ones((P, 2))
    m[0, 0] = 0
    put("mask", m)
    put("negm", -m)
    put("h1m", m)
    bands = (EMB - 1) // 2
    phase = np.float32(2.0 * math.pi / S) * np.arange(S, dtype=np.float32)[:, None] * \
        np.linspace(1e-4, bands - 1, bands, dtype=np.float32)
    emb = np.concatenate([lin[:, None], np.cos(phase), -np.sin(phase)], -1).T
    return c, np.ascontiguousarray(emb, np.float32)


def _lay_out(i):
    f = lambda n: np.asarray(i[n], np.float32)
    tiles = []
    z = lambda k, n: np.zeros((k, n), np.float32)
    half = ROPE // 2

    def swap(w):
        return np.concatenate([w[:, half:], w[:, :half]], 1)

    def ffn(g, u, d):
        out = []
        for h in range(2):
            cs = slice(h * HALF * P, (h + 1) * HALF * P)
            gt, ut = (_tiles(w[:, cs]).reshape(HALF, NC, P, P) for w in (g, u))
            out += [np.stack([gt, ut], 1).reshape(-1, P, P), _tiles(d[cs])]
        return out

    for l in range(2):
        w = f("w_in")[l]
        tiles.append(_tiles(w[:, KV_START:KV_START + KV_LORA]))
        kr = w[:, KV_START + KV_LORA:HY_START]
        tiles.append(_tiles(np.concatenate([z(D, 64), kr, swap(kr)], 1)))
        tiles.append(_tiles(w[:, :Q_LORA]))
        tiles.append(_tiles(f("w_uk")[l]))
        tiles.append(_rows(f("w_uv")[l]))
        uq = f("w_uq")[l].reshape(Q_LORA, NH, QD)
        for h in range(NH):
            tiles.append(_tiles(np.concatenate([uq[:, h], swap(uq[:, h, NOPE:])], 1)))
        hy = _tiles(w[:, HY_START:GATE_START]).reshape(3, HYC, NC, P, P)
        tiles.append(hy.transpose(1, 0, 2, 3, 4).reshape(-1, P, P))
        ga = _tiles(w[:, GATE_START:GATE_START + D]).reshape(NC, NC, P, P)
        gh = _tiles(w[:, GATE_START + D:]).reshape(NC, NC, P, P)
        ba, bh = (_tiles(f(n)[l]).reshape(NC, 4, P, P) for n in ("w_br_attn", "w_br_hy"))
        tiles.append(np.concatenate([ga, ba, gh, bh], 1).reshape(-1, P, P))
        tiles.append(_tiles(f("w_out")[l]))
        if l == 0:
            tiles += ffn(f("ffn_w_gate")[0], f("ffn_w_up")[0], f("ffn_w_down")[0])
        else:
            g, u, d = f("moe_w_gate")[0], f("moe_w_up")[0], f("moe_w_down")[0]
            for e in range(NE):
                tiles += ffn(g[e], u[e], d[e])
    gu = f("ffn1_w_gu_2")[0]
    tiles += ffn(gu[:, :DFF], gu[:, DFF:], f("ffn1_w_down_2")[0])
    w = f("w_in_2")[0]
    tiles.append(_tiles(w[:, :2 * AW]))
    tiles.append(_rows(w[:, 2 * AW:3 * AW]))
    tiles.append(_tiles(w[:, 3 * AW:3 * AW + 2 * D]))
    w = w[:, 3 * AW + 2 * D:]
    ga, gh, bh = (_tiles(m).reshape(NC, NC, P, P) for m in (w[:, :D], w[:, D:], f("w_rec_o_2")[0]))
    ba = _tiles(f("w_att_o_2")[0]).reshape(NC, 4, P, P)
    tiles.append(np.concatenate([ga, ba, gh, bh], 1).reshape(-1, P, P))
    tiles.append(_tiles(f("w_out_2")[0]))
    gu = f("ffn2_w_gu_2")[0]
    tiles += ffn(gu[:, :DFF], gu[:, DFF:], f("ffn2_w_down_2")[0])
    total = sum(t.shape[0] for t in tiles)
    wsplit = np.empty((total // TPS, P, TPS, P), np.float32)
    at = 0
    for t in tiles:
        for s in range(t.shape[0]):
            wsplit[(at + s) // TPS, :, (at + s) % TPS] = t[s]
        at += t.shape[0]

    wm = np.concatenate([f("w_mod")[0], f("w_mod")[1], f("w_ada_2")[0]], 1)
    wmod = np.ascontiguousarray(wm.reshape(NC // 2, 2, P, NMODB, 512).transpose(3, 0, 2, 1, 4)).reshape(NMOD, P, SLOT)

    v = np.zeros((P, NVEC), np.float32)

    def put(name, a, rows=P):
        at, w = VEC[name]
        v[0:rows, at:at + w] = a
    for l in range(2):
        put(f"n1{l}", _cols(f("norm1_g")[l]))
        put(f"n2{l}", _cols(f("norm2_g")[l]))
        put(f"qn{l}", _cols(f("q_norm_g")[l]))
        put(f"kvn{l}", _cols(f("kv_norm_g")[l]))
        put(f"sw{l}", _cols(f("hy_short_w")[l].reshape(-1)))
        put(f"sb{l}", _cols(f("hy_short_b")[l]))
        put(f"hb{l}", _cols(f("hy_bias")[l]))
        put(f"bm{l}", _cols(f("b_mod")[l]))
        put(f"fb1{l}", f("hy_b1")[l][:, None], FH)
        put(f"fb2{l}", f("hy_b2")[l][:, None], FH)
        put(f"freq{l}", f("hy_freq")[l][:, None], FH)
    put("fg", _cols(f("final_g")))
    put("bm2", _cols(f("b_ada_2")[0]))
    put("pre", _cols(f("norm_pre_2")[0].reshape(-1)))
    put("post", _cols(f("norm_post_2")[0].reshape(-1)))
    put("cw", _cols(f("conv_w_2")[0].reshape(-1)))
    put("cb", _cols(f("conv_b_2")[0]))
    put("ba", _cols(f("lru_ba_2")[0]))
    put("bx", _cols(f("lru_bx_2")[0]))
    put("lam", _cols(f("lru_lambda_2")[0]))
    put("router", f("moe_router")[0].reshape(NC, P, NE).transpose(1, 0, 2).reshape(P, -1))
    c3 = np.zeros((P, NC, 32), np.float32)
    for r, n in enumerate(("c_ctx", "c", "c_2")):
        c3[:, :, r] = _cols(f(n).reshape(-1))
    put("c3", c3.reshape(P, -1))
    cst, emb = _constants()
    q = np.arange(S)[:, None] - np.arange(S)[None, :]
    bias = f("rel_bias_2")[0][:, np.clip(q, -MAXREL, MAXREL) + MAXREL]
    bias = bias.reshape(NH, 2, P, S).transpose(2, 1, 0, 3).reshape(P, -1)
    lru = np.zeros((P, NC, 2, P), np.float32)
    for j, n in enumerate(("lru_wa_2", "lru_wx_2")):
        w = f(n)[0]
        for b in range(2 * NC):
            r = slice(64 * (b % 2), 64 * (b % 2) + 64)
            lru[r, b // 2, j, r] = w[b]
    return {
        "wsplit": wsplit.reshape(total // TPS, P, SLOT), "wmod": wmod, "vec": v, "cst": cst, "emb": emb,
        "xT": np.ascontiguousarray(f("x")[0].T), "ctxT": np.ascontiguousarray(f("ctx")[0].T),
        "fw1": f("hy_w1"), "fw2": f("hy_w2"), "fw3": f("hy_w3"), "decay": f("hy_decay").reshape(2, 2 * HY),
        "bias": np.ascontiguousarray(bias), "lru": lru.reshape(P, -1),
    }


def kernel(**inputs):
    import concourse.bacc as _bacc
    from concourse.bass_utils import run_bass_kernel_spmd as _run

    nc = _bacc.Bacc("TRN2", target_bir_lowering=False, num_devices=1)
    arrays = {f"in_{k}": np.ascontiguousarray(v) for k, v in _lay_out(inputs).items()}
    io = {k[3:]: nc.dram_tensor(k, a.shape, F32, kind="ExternalInput").ap() for k, a in arrays.items()}
    io["out"] = nc.dram_tensor("out_xT", (D, S), F32, kind="ExternalOutput").ap()
    build(nc, io)
    r = _run(nc, [arrays], core_ids=[0])
    return np.ascontiguousarray(r.results[0]["out_xT"].T)[None]
```

```python
import math
from contextlib import ExitStack

import numpy as np

import concourse.bass as bass
from concourse import mybir

ALU = mybir.AluOpType
ACT = mybir.ActivationFunctionType
AX = mybir.AxisListType
F32 = mybir.dt.float32
F32R = mybir.dt.float32r
U32 = mybir.dt.uint32

P = 128
D = 1024
S = 256
NC = D // P
NH = 8
Q_LORA, KV_LORA, NOPE, ROPE, VH = 384, 256, 64, 32, 64
QD = NOPE + ROPE
QC, KVC = Q_LORA // P, KV_LORA // P
HY = 512
HYC = HY // P
EMB, FH = 17, 64
DFF = 2816
HALF = DFF // P // 2
NE = 8
KV_START = Q_LORA
HY_START = KV_START + KV_LORA + ROPE
GATE_START = HY_START + 3 * HY
EPS = 1e-6
SCALE = QD ** -0.5
SCALE2 = 64 ** -0.5
MAXREL = 128
AW = 512
TPS = 8
SLOT = TPS * P
RAW = 11
SPL = 3
NMODB = (2 * 6 + 9) * D // 512
NMOD = NMODB * NC // 2
BANKS = 6
FIRST_MOD = 4
HSLOTS = 3 * HALF
HCHUNKS = 2 * HALF + NC
HA, HD = HALF, HALF + NC
CAP = P
GB = DFF // 256
PSLOTS = GB * 4 + 2 * GB
EXTRA = 2 * S // (CAP + 1)
PASSES = NE + EXTRA


def pass_table():
    order = [("X0", 3, "D"), ("X1", 4, "D"), ("S", 5, "A")]
    for b in range(GB):
        order.append((f"GU{b}", b % 3, "D"))
        if b:
            order.append((f"HT{b-1}", 3 + (b - 1) % 2, "D"))
    order += [(f"HT{GB-1}", 3 + (GB - 1) % 2, "D"), ("DA", 6, "A"), ("DB", 7, "D")]
    order += [(f"O{j}", (5, 0, 1, 2)[j], "D") for j in range(4)]
    chunks, ends, step, rank, slot = {}, [], 0, {"A": 0, "D": 0}, 0
    last = {}
    for name, bank, owner in order:
        if name.startswith("GU"):
            for _ in range(3):
                step += 1
                ends.append(step)
        if name == "DA":
            for _ in range(2 * GB - 1):
                step += 1
                ends.append(step)
        step += 1
        if name.startswith("GU") or name == "DB":
            ends.append(step)
        rank[owner] += 1
        chunks[name] = dict(bank=bank, owner=owner, end=step, rank=rank[owner], before=last.get(bank))
        last[bank] = name
    for c in chunks.values():
        c["wraps"] = c["before"] is None
        if c["wraps"]:
            c["before"] = last[c["bank"]]
    assert len(ends) == PSLOTS
    return chunks, ends, step, rank

VEC = {}
_n = 0
for _name, _w in ([(f"{v}{l}", w) for l in range(2) for v, w in
                   (("n1", 8), ("n2", 8), ("qn", QC), ("kvn", KVC), ("sw", 36), ("sb", 12), ("hb", 4),
                    ("bm", 48), ("fb1", 1), ("fb2", 1), ("freq", 1))] +
                  [("fg", 8), ("bm2", 72), ("pre", 24), ("post", 24), ("cw", 32), ("cb", 8), ("ba", 8),
                   ("bx", 8), ("lam", 8), ("router", 64), ("c3", 256)]):
    VEC[_name] = (_n, _w)
    _n += _w
NVEC = _n
CST = {}
_n = 0
for _name, _w in (("ident", 128), ("ones", 128), ("F", 1024), ("G", 1024), ("cos", 512), ("sin", 512),
                  ("iota", 8), ("negt", 2), ("mask", 2), ("negm", 2), ("h1m", 2), ("alt2", 128)):
    CST[_name] = (_n, _w)
    _n += _w
NCST = _n


class Plan:

    def __init__(self):
        self.c, self.name = [], {}
        self.tiles = 0
        self.steps = 0
        self.slot_end = {}
        self.rank = {"A": 0, "D": 0}
        self.complete = []
        self.mod_end = []
        self.loops = {}
        self.caps = []
        self.mods = 0
        self.order = []

    def chunk(self, name, owner, tiles=0, mod=False):
        if mod:
            self.mod_end += [self.steps + j + 1 for j in range(NC // 2)]
            self.steps += NC // 2 - 1
        t0 = self.tiles
        t1 = t0 + tiles
        for t in range(t0, t1):
            if t % TPS == TPS - 1 and t != t1 - 1:
                self.steps += 1
                self.slot_end[t // TPS] = self.steps
        self.steps += 1
        if tiles and t1 % TPS == 0:
            self.slot_end[t1 // TPS - 1] = self.steps
        self.order += [("split", s) for s in range(-(-t0 // TPS), -(-t1 // TPS))]
        self.tiles = t1
        self.rank[owner] += 1
        self.name[name] = len(self.c)
        self.c.append(dict(name=name, owner=owner, t0=t0, t1=t1, end=self.steps, rank=self.rank[owner]))
        self.complete.append(t1 // TPS)

    def loop(self, name, times):
        assert self.tiles % TPS == 0
        s0 = self.tiles // TPS
        for i in range(SPL if s0 >= SPL else 0):
            assert self.slot_end[s0 - SPL + i] <= self.steps - (3, 1, 0)[i]
        self.caps.append(s0)
        self.loops[name] = dict(slot=s0, chunk=len(self.c), step=self.steps, A=self.rank["A"],
                                D=self.rank["D"], half=2 + sum(v["times"] for v in self.loops.values()), times=times)
        for q in range(times):
            for f in range(HALF):
                self.chunk(f"{name}.{q}.g{f}", "A", TPS)
                self.chunk(f"{name}.{q}.u{f}", "D", TPS)
            for n in range(NC):
                self.chunk(f"{name}.{q}.d{n}", "D", HALF)

    def passes(self):
        chunks, ends, steps, rank = pass_table()
        assert self.tiles % TPS == 0
        s0 = self.tiles // TPS
        for i in range(SPL):
            assert self.slot_end[s0 - SPL + i] <= self.steps - steps + ends[PSLOTS - SPL + i]
        assert min(self.rank["A"] - rank["A"], self.rank["D"] - rank["D"]) >= 0
        self.caps.append(s0)
        self.moe = dict(slot=s0, step=self.steps, A=self.rank["A"], D=self.rank["D"], chunks=chunks, ends=ends,
                        per=dict(step=steps, **rank))
        self.steps += steps * PASSES
        for k in "AD":
            self.rank[k] += rank[k] * PASSES
        for i in range(SPL):
            self.slot_end[s0 + PSLOTS * PASSES - SPL + i] = self.steps - steps + ends[PSLOTS - SPL + i]
        self.tiles += PSLOTS * PASSES * TPS
        for i in range(BANKS):
            self.c.append(dict(name=f"drained{i}", owner="D", t0=self.tiles, t1=self.tiles, end=self.steps,
                               rank=self.rank["D"]))
            self.name[f"drained{i}"] = len(self.c) - 1
            self.complete.append(self.tiles // TPS)

    def side(self):
        b = self.mods
        if b > NMODB:
            return
        self.order += [("mod", 4 * b + j) for j in range(4)] if b < NMODB else []
        if b:
            self.chunk(f"modT{b-1}", "D")
        if b < NMODB:
            self.chunk(f"mod{b}", "A", mod=True)
        self.mods = b + 1

    def __getitem__(self, name):
        return self.c[self.name[name]]


def attention_order(label, tiles):
    items = [(hp, qt, hh) for hp in range(NH // 2) for qt in range(tiles) for hh in range(2)]
    return items


def make_plan():
    p = Plan()

    def attn(l, tiles):
        n = len(attention_order(l, tiles))
        p.chunk(f"{l}.S0", "D" if l == "B" else "A")
        for i in range(n + 1):
            if i + 1 < n:
                p.chunk(f"{l}.S{i+1}", "D" if l == "B" else "A")
            if i < n:
                p.chunk(f"{l}.PT{i}", "D")
            if i >= 1 and (i - 1) % 2 == 1:
                p.chunk(f"{l}.O{(i-1)//2}", "D")

    for b in range(FIRST_MOD):
        p.side()
    p.side()
    for l in range(2):
        L = f"L{l}"
        p.chunk(f"{L}.n1", "D")
        for i in range(KVC):
            p.chunk(f"{L}.kv{i}", "D", NC)
        p.chunk(f"{L}.kr", "D", NC)
        for i in range(QC):
            p.chunk(f"{L}.q{i}", "D", NC)
        p.chunk(f"{L}.nkv", "D")
        p.chunk(f"{L}.nq", "D")
        for i in range(4):
            p.chunk(f"{L}.uk{i}", "A", KVC)
        for i in range(4):
            p.chunk(f"{L}.uv{i}", "A", 2 * 4 if i == 3 else 0)
        for h in range(NH):
            p.chunk(f"{L}.uq{h}", "D", QC)
        attn(L, 4 if l == 0 else 2)
        p.chunk(f"f{l}.a", "D")
        p.chunk(f"f{l}.b", "D")
        for t in range(4):
            p.chunk(f"f{l}.h{t}", "D")
        p.chunk(f"f{l}.sum", "D")
        for t in range(4):
            p.chunk(f"f{l}.K{t}", "D")
        for c in range(HYC):
            for v in range(3):
                p.chunk(f"{L}.hy{c}{v}", "D", NC)
            p.side()
        for s in range(2 if l == 0 else 1):
            for t in range(2):
                p.chunk(f"{L}.z{s}{t}", "D")
            for f in range(4):
                p.chunk(f"{L}.Z{s}{f}", "D")
            for c in range(HYC):
                p.chunk(f"{L}.y{s}{c}", "D")
        for n in range(NC):
            p.chunk(f"{L}.ga{n}", "A", NC)
            p.chunk(f"{L}.ba{n}", "D", 4)
            p.chunk(f"{L}.gh{n}", "A", NC)
            p.chunk(f"{L}.bh{n}", "D", 4)
            p.side()
        for n in range(NC):
            p.chunk(f"{L}.o{n}", "D", NC)
        p.chunk(f"{L}.n2", "D")
        if l == 1:
            for t in range(2):
                p.chunk(f"route{t}", "D")
            for t in range(4):
                p.chunk(f"hr{t}", "D")
            p.chunk("pos", "D")
            p.passes()
        else:
            for q in range(2):
                for f in range(HALF):
                    p.chunk(f"{L}.ff.{q}.g{f}", "A", NC)
                    p.chunk(f"{L}.ff.{q}.u{f}", "D", NC)
                    p.side()
                for n in range(NC):
                    p.chunk(f"{L}.ff.{q}.d{n}", "D", HALF)
                    if n % 2:
                        p.side()
            while p.mods <= NMODB:
                p.side()
    p.chunk("final", "D")
    for j in range(3):
        p.chunk(f"B.pre{j}", "D")
        if j != 1:
            p.loop(f"B.ff{j}", 2)
        else:
            for n in range(8):
                p.chunk(f"B.qk{n}", "A", NC)
            for t in range(2):
                p.chunk(f"B.v{t}", "A", 1 if t == 1 else 31)
            attn("B", 2)
            for n in range(NC):
                p.chunk(f"B.xr{n}", "D", NC)
            for n in range(NC):
                p.chunk(f"B.ra{n}", "A")
                p.chunk(f"B.rx{n}", "A")
            for n in range(NC):
                p.chunk(f"B.yr{n}", "A", NC)
            for n in range(NC):
                p.chunk(f"B.ga{n}", "A", NC)
                p.chunk(f"B.ba{n}", "D", 4)
                p.chunk(f"B.gh{n}", "A", NC)
                p.chunk(f"B.bh{n}", "D", NC)
            for n in range(NC):
                p.chunk(f"B.o{n}", "D", NC)
        p.chunk(f"B.post{j}", "D")
    assert p.tiles % TPS == 0 and p.mods == NMODB + 1
    p.load_at = {key: g for g, key in enumerate(p.order) if key[0] == "mod" or key[1] < p.moe["slot"]}
    assert all(p.load_at[("split", s)] == s + NMOD for s in range(p.moe["slot"] - 3, p.moe["slot"]))
    return p


ARENA = 17408
FF_AT = 4096


def build(nc, io):
    plan = make_plan()
    NSPLIT = plan.tiles // TPS
    caps = plan.caps + [NSPLIT]
    with ExitStack() as ctx:
        def sb(name, shape, dt=F32):
            return ctx.enter_context(nc.sbuf_tensor(name, shape, dt))

        def sem(name):
            return ctx.enter_context(nc.semaphore(name))

        raw = sb("raw", [P, RAW, SLOT])
        whi = sb("whi", [P, SPL, SLOT], F32R)
        wlo = sb("wlo", [P, SPL, SLOT], F32R)
        xs = sb("xs", [P, NC, 2 * S])
        hH = sb("hH", [P, NC, 2 * S], F32R)
        hL = sb("hL", [P, NC, 2 * S], F32R)
        arena_at = -(-nc.sbuf_base // 32) * 32
        arena = sb("arena", [P, ARENA])
        rounded = nc.alloc_sbuf_tensor_at("rounded", [P, ARENA], F32R, offset=arena_at)
        vec = sb("vec", [P, NVEC])
        cst = sb("cst", [P, NCST])
        modT = sb("modT", [P, (12 + 12 + 18) * 4, 3])
        dv = sb("dv", [P, 14, NC])
        modrow = sb("modrow", [P, 2, 512])
        passes_i = sb("passes_i", [1, 8], mybir.dt.int32)
        small = sb("small", [P, 96])
        idx = sb("idx", [P, 8], U32)
        ps = ctx.enter_context(nc.psum_tensor("ps", [P, 8, 512], F32))
        M = plan.moe
        per = M["per"]
        PC = M["chunks"]

        def view(at, n, width, dt=F32):
            v = (arena if dt is F32 else rounded)[:, at:at + n * width]
            return v.rearrange("p (n w) -> p n w", n=n)

        def C(name, a=0, b=None):
            at, w = CST[name]
            return cst[:, at + a:at + (w if b is None else b)]

        def Vv(name, a=0, b=None):
            at, w = VEC[name]
            return vec[:, at + a:at + (w if b is None else b)]

        ident, ones = C("ident"), C("ones")

        raw_in = [sem(f"raw_in{i}") for i in range(RAW)]
        hi_ready = sem("hi_ready")
        lo_ready = sem("lo_ready")
        pe_step = sem("pe_step")
        act_free = sem("act_free")
        dve_free = sem("dve_free")
        free_of = {"A": act_free, "D": dve_free}
        consts_in = sem("consts_in")
        cact_ready = sem("cact_ready")
        sq_ready = sem("sq_ready")
        std_ready = sem("std_ready")
        norm_ready = sem("norm_ready")
        nhi_ready = sem("nhi_ready")
        nlo_ready = sem("nlo_ready")
        rope_ready = sem("rope_ready")
        nmax_ready = sem("nmax_ready")
        exp_ready = sem("exp_ready")
        prob_ready = sem("prob_ready")
        ohi_ready = sem("ohi_ready")
        sel_ready = sem("sel_ready")
        xhi_ready = sem("xhi_ready")
        silu_ready = sem("silu_ready")
        hthi_ready = sem("hthi_ready")
        table_ready = sem("table_ready")
        rt_in = sem("rt_in")
        filt_in = sem("filt_in")
        filt_d = sem("filt_d")
        filt_a = sem("filt_a")
        z_ready = sem("z_ready")
        Y_ready = sem("Y_ready")
        o_ready = sem("o_ready")
        hyhi_ready = sem("hyhi_ready")
        hylo_ready = sem("hylo_ready")
        m_ready = sem("m_ready")
        mhi_ready = sem("mhi_ready")
        mlo_ready = sem("mlo_ready")
        hidhi_ready = sem("hidhi_ready")
        hidlo_ready = sem("hidlo_ready")
        comb_ready = sem("comb_ready")
        gates_ready = sem("gates_ready")
        blk_in = sem("blk_in")
        lru_d = sem("lru_d")
        lru_a = sem("lru_a")
        lam_abs = sem("lam_abs")
        lam_exp = sem("lam_exp")
        out_ready = sem("out_ready")
        out_done = sem("out_done")
        d_link = sem("d_link")
        a_link = sem("a_link")
        p_link = sem("p_link")

        NORMS = ["L0.n1", "L0.nkv", "L0.nq", "L0.n2", "L1.n1", "L1.nkv", "L1.nq", "L1.n2", "final",
                 "B.pre0", "B.post0", "B.pre1", "B.post1", "B.pre2", "B.post2"]
        NORM_CHUNKS = {n: KVC if "nkv" in n else QC if "nq" in n else NC for n in NORMS}

        def norm_at(label, n=0):
            return sum(NORM_CHUNKS[m] for m in NORMS[:NORMS.index(label)]) + n

        SPLIT = [n for n in NORMS if n != "final" and "post" not in n]

        def split_at(label, n=0):
            return sum(NORM_CHUNKS[m] for m in SPLIT[:SPLIT.index(label)]) + n

        ATTN = {"L0": 0, "L1": 32, "B": 48}
        LAYERS = ((0, 0, 2 * S), (1, S, S))

        block = ctx.enter_context(nc.Block())

        def wait_chunk(eng, name):
            eng.wait_ge(pe_step, plan[name]["end"])

        def wait_free(eng, name):
            eng.wait_ge(free_of[plan[name]["owner"]], plan[name]["rank"])

        def bank(name):
            return ps[:, plan.name[name] % BANKS, :]

        def load_no(s):
            return plan.load_at.get(("split", s), NMOD + s)

        def rank_of(eng, name, q, prior=False):
            c = PC[name]
            o = c["owner"]
            eng.wait_ge(free_of[o], q * per[o] + (M[o] + c["rank"] - (per[o] if prior else 0)))

        def pass_chunk(eng, name, q):
            eng.wait_ge(pe_step, q * per["step"] + (M["step"] + PC[name]["end"]))

        def pass_bank(name):
            return ps[:, PC[name]["bank"], :]

        def all_passes(eng, body, skip, table=True):
            with eng.Fori(0, NE) as q:
                body(q, q)
            eng.wait_ge(table_ready, 1)
            with eng.Fori(0, EXTRA) as j:
                expert = eng.value_load(passes_i[0:1, bass.ds(j, 1)], min_val=0, max_val=NE - 1)
                runs = eng.value_load(passes_i[0:1, bass.ds(j + 4, 1)], min_val=0, max_val=1)
                with eng.If(runs != 0):
                    body(j + NE, expert)
                with eng.Else():
                    skip(j + NE)

        @block.sync
        def _(sp):
            sp.dma_start(vec[:, :], io["vec"]).then_inc(consts_in, 16)

            def emptied(key):
                if key[0] == "mod":
                    sp.wait_ge(pe_step, plan.mod_end[key[1]])
                else:
                    sp.wait_ge(lo_ready, key[1] + 1)

            first = [k for k in plan.order if k in plan.load_at]
            for g, (kind, i) in enumerate(first):
                if g >= RAW:
                    emptied(first[g - RAW])
                sp.dma_start(raw[:, g % RAW, :], io["wmod" if kind == "mod" else "wsplit"][i])\
                  .then_inc(raw_in[g % RAW], 16)
            s0 = M["slot"]

            def load_pass(q, expert):
                with sp.Fori(0, PSLOTS // RAW) as k:
                    for j in range(RAW):
                        sp.wait_ge(lo_ready, q * PSLOTS + k * RAW + (s0 - RAW + j + 1))
                        sp.dma_start(raw[:, (NMOD + s0 + j) % RAW, :],
                                     io["wsplit"][bass.ds(expert * PSLOTS + k * RAW + (s0 + j), 1)]
                                     .rearrange("o p w -> p (o w)")).then_inc(raw_in[(NMOD + s0 + j) % RAW], 16)

            def skip(q):
                for j in range(RAW):
                    r = (NMOD + s0 + j) % RAW
                    sp.wait_ge(raw_in[r], q * (16 * PSLOTS // RAW) + 16 * ((NMOD + s0 + j) // RAW))
                    sp.sem_inc(raw_in[r], 16 * PSLOTS // RAW)

            all_passes(sp, load_pass, skip)
            s1 = s0 + PASSES * PSLOTS
            gone = EXTRA * PSLOTS
            turns = (NSPLIT - s1) // RAW
            with sp.Fori(0, turns) as k:
                for j in range(RAW):
                    sp.wait_ge(lo_ready, k * RAW + (s1 - RAW + j + 1))
                    sp.dma_start(raw[:, (NMOD + s1 + j) % RAW, :],
                                 io["wsplit"][bass.ds(k * RAW + (s1 - gone + j), 1)].rearrange("o p w -> p (o w)"))\
                      .then_inc(raw_in[(NMOD + s1 + j) % RAW], 16)
            for s in range(s1 + turns * RAW, NSPLIT):
                sp.wait_ge(lo_ready, s - RAW + 1)
                sp.dma_start(raw[:, (NMOD + s) % RAW, :], io["wsplit"][s - gone]).then_inc(raw_in[(NMOD + s) % RAW], 16)
            sp.wait_ge(out_ready, 1)
            sp.dma_start(io["out"].rearrange("(c p) t -> p c t", p=P), xs[:, :, S:2 * S]).then_inc(out_done, 16)
            sp.wait_ge(out_done, 16)

        @block.tensor
        def _(pe):
            st = {"step": 0}

            def step(mm):
                mm.then_inc(pe_step, 1)
                st["step"] += 1

            def begin(name):
                c = plan.name[name]
                if c >= BANKS:
                    wait_free(pe, plan.c[c - BANKS]["name"])

            def lin(name, mov, T, ktiles=None):
                begin(name)
                c = plan[name]
                for i, t in enumerate(range(c["t0"], c["t1"])):
                    s, r = divmod(t, TPS)
                    if i == 0 or r == 0:
                        pe.wait_ge(lo_ready, s + 1)
                    wh = whi[:, s % SPL, r * P:(r + 1) * P]
                    wl = wlo[:, s % SPL, r * P:(r + 1) * P]
                    xh, xl = mov(i)
                    o = bank(name)[:, 0:T]
                    last = t == c["t1"] - 1
                    pe.matmul(o, wh, xh, start=(i == 0), stop=False)
                    pe.matmul(o, wh, xl, start=False, stop=False)
                    mm = pe.matmul(o, wl, xh, start=False, stop=last)
                    if r == TPS - 1 or last:
                        step(mm)
                assert st["step"] == c["end"], name

            def mean_square(label, sq, n, T):
                begin(label)
                pe.wait_ge(sq_ready, NORMS.index(label) + 1)
                for k in range(n):
                    mm = pe.matmul(bank(label)[:, 0:T], ones, sq[:, k, :], start=(k == 0), stop=(k == n - 1))
                step(mm)

            def mod_block(b):
                begin(f"mod{b}")
                cact = Vv("c3").rearrange("p (k r) -> p k r", k=NC)
                for k in range(NC):
                    g = plan.load_at[("mod", b * (NC // 2) + k // 2)]
                    if k % 2 == 0:
                        pe.wait_ge(raw_in[g % RAW], 16 * (g // RAW + 1))
                    j = k % 4
                    mm = pe.matmul(bank(f"mod{b}")[32 * j:32 * j + 32, :], cact[:, k, :],
                                   raw[:, g % RAW, (k % 2) * 512:(k % 2 + 1) * 512],
                                   start=(k < 4), stop=(k >= 4), skip_group_check=True, tile_position=(0, 32 * j))
                    if k % 2:
                        step(mm)

            def mod_turn(b):
                begin(f"modT{b}")
                wait_free(pe, f"mod{b}")
                for q in range(4):
                    mm = pe.transpose(bank(f"modT{b}")[:, q * P:(q + 1) * P], modrow[:, b % 2, q * P:(q + 1) * P],
                                      ident)
                step(mm)

            mods = [0]

            def side():
                b = mods[0]
                if b > NMODB:
                    return
                if b:
                    mod_turn(b - 1)
                if b < NMODB:
                    mod_block(b)
                mods[0] += 1

            def attention(l, tiles, qk, vt, pT, pv_rows):
                items = attention_order(l, tiles)
                n = len(items)

                def scores(i):
                    begin(f"{l}.S{i}")
                    qa, ka, nk = qk(*items[i])
                    step(pe.matmul(bank(f"{l}.S{i}")[:, 0:nk], qa, ka, start=True, stop=True))

                def turn(i):
                    begin(f"{l}.PT{i}")
                    pe.wait_ge(prob_ready, ATTN[l] + i + 1)
                    nk = qk(*items[i])[2]
                    for c in range(nk // P):
                        mm = pe.transpose(bank(f"{l}.PT{i}")[:, c * P:(c + 1) * P], pv_rows[:, i % 2, c * P:(c + 1) * P],
                                          ident)
                    step(mm)

                def out(i):
                    hp, qt, hh = items[i]
                    o = f"{l}.O{i//2}"
                    if hh == 0:
                        begin(o)
                    wait_free(pe, f"{l}.PT{i}")
                    nk = qk(*items[i])[2]
                    h = 2 * hp + hh
                    for c in range(nk // P):
                        mm = pe.matmul(bank(o)[64 * hh:64 * hh + 64, 0:P], vt[:, c, h * VH:(h + 1) * VH],
                                       pT[:, i % 2, c * P:(c + 1) * P], start=(c == 0), stop=(c == nk // P - 1),
                                       skip_group_check=True, tile_position=(0, 64 * hh))
                    if hh == 1:
                        step(mm)

                scores(0)
                for i in range(n + 1):
                    if i + 1 < n:
                        scores(i + 1)
                    if i < n:
                        turn(i)
                    if i >= 1:
                        out(i - 1)

            def feed_forward(name, T, t0):
                L = plan.loops[name]
                for sem_, key in ((act_free, "A"), (dve_free, "D")):
                    pe.wait_ge(sem_, L[key])
                hid_h = view(FF_AT, HALF, T, F32R)
                hid_l = view(FF_AT + HALF * T, HALF, T, F32R)
                with pe.Fori(0, L["times"]) as q:
                    for c in range(HCHUNKS):
                        owner, rank = ("A", c // 2) if c < 2 * HALF and c % 2 == 0 else \
                            ("D", c // 2 if c < 2 * HALF else c - HALF)
                        b = c - BANKS
                        if b < 0:
                            pe.wait_ge(dve_free, q * HD + (L["D"] + 1 + b))
                        elif b < 2 * HALF and b % 2 == 0:
                            pe.wait_ge(act_free, q * HA + (L["A"] + b // 2 + 1))
                        else:
                            pe.wait_ge(dve_free, q * HD + (L["D"] + (b // 2 if b < 2 * HALF else b - HALF) + 1))
                        o = ps[:, (L["chunk"] + c) % BANKS, 0:T]
                        down = c >= 2 * HALF
                        t0_ = c * TPS if not down else 2 * HALF * TPS + (c - 2 * HALF) * HALF
                        nk = HALF if down else NC
                        for i in range(nk):
                            s, r = divmod(t0_ + i, TPS)
                            if i == 0 or r == 0:
                                pe.wait_ge(lo_ready, q * HSLOTS + (L["slot"] + s + 1))
                            if c == 2 * HALF:
                                pe.wait_ge(hidlo_ready, q * HALF + (L["half"] * HALF + i + 1))
                            wh = whi[:, (L["slot"] + s) % SPL, r * P:(r + 1) * P]
                            wl = wlo[:, (L["slot"] + s) % SPL, r * P:(r + 1) * P]
                            xh, xl = (hid_h[:, i, :], hid_l[:, i, :]) if down else \
                                (hH[:, i, t0:t0 + T], hL[:, i, t0:t0 + T])
                            pe.matmul(o, wh, xh, start=(i == 0), stop=False)
                            pe.matmul(o, wh, xl, start=False, stop=False)
                            mm = pe.matmul(o, wl, xh, start=False, stop=(i == nk - 1))
                            if r == TPS - 1 or i == nk - 1:
                                mm.then_inc(pe_step, 1)
                st["step"] = plan[f"{name}.{L['times']-1}.d{NC-1}"]["end"]

            def experts(hrow):
                pe.wait_ge(act_free, M["A"])
                pe.wait_ge(dve_free, M["D"])
                xh, xl = view(4864, NC, P, F32R), view(5888, NC, P, F32R)
                hid32 = view(7424, 2, 256)
                hh, hl = view(7936, 2 * GB, P, F32R), view(10752, 2 * GB, P, F32R)
                sel, selw, selT = view(4096, 2, P), view(4352, 2, P), arena[:, 4608:4864]
                yrow = arena[:, 13568:14592]

                def one(q, expert):
                    def free(name):
                        rank_of(pe, PC[name]["before"], q, PC[name]["wraps"])

                    def weights(s):
                        pe.wait_ge(lo_ready, q * PSLOTS + (M["slot"] + s + 1))
                        return (M["slot"] + s) % SPL

                    pe.wait_ge(sel_ready, q + 1)
                    for i in range(2):
                        free(f"X{i}")
                        for k in range(4):
                            for t in range(2):
                                mm = pe.matmul(pass_bank(f"X{i}")[:, k * P:(k + 1) * P],
                                               hrow[:, t, (4 * i + k) * P:(4 * i + k + 1) * P], sel[:, t, :],
                                               start=(t == 0), stop=(t == 1), skip_group_check=True)
                        mm.then_inc(pe_step, 1)
                    free("S")
                    for t in range(2):
                        mm = pe.transpose(pass_bank("S")[:, t * P:(t + 1) * P], selw[:, t, :], ident)
                    mm.then_inc(pe_step, 1)
                    rank_of(pe, "X1", q)

                    def turn(b):
                        free(f"HT{b}")
                        rank_of(pe, f"GU{b}", q)
                        for j in range(2):
                            mm = pe.transpose(pass_bank(f"HT{b}")[:, j * P:(j + 1) * P],
                                              hid32[:, b % 2, j * P:(j + 1) * P], ident)
                        mm.then_inc(pe_step, 1)

                    for b in range(GB):
                        free(f"GU{b}")
                        for k in range(NC):
                            if k % 2 == 0:
                                r = weights(4 * b + k // 2)
                            wh, wl = (w[:, r, (k % 2) * 512:(k % 2 + 1) * 512] for w in (whi, wlo))
                            o = pass_bank(f"GU{b}")
                            pe.matmul(o, xh[:, k, :], wh, start=(k == 0), stop=False)
                            pe.matmul(o, xl[:, k, :], wh, start=False, stop=False)
                            mm = pe.matmul(o, xh[:, k, :], wl, start=False, stop=(k == NC - 1))
                            if k % 2:
                                mm.then_inc(pe_step, 1)
                        if b:
                            turn(b - 1)
                    turn(GB - 1)
                    free("DA")
                    free("DB")
                    for f in range(2 * GB):
                        if f % 2 == 0:
                            rank_of(pe, f"HT{f//2}", q)
                        r = weights(4 * GB + f)
                        for j, name in enumerate(("DA", "DB")):
                            wh, wl = (w[:, r, j * 512:(j + 1) * 512] for w in (whi, wlo))
                            o = pass_bank(name)
                            pe.matmul(o, hh[:, f, :], wh, start=(f == 0), stop=False)
                            pe.matmul(o, hl[:, f, :], wh, start=False, stop=False)
                            mm = pe.matmul(o, hh[:, f, :], wl, start=False, stop=(f == 2 * GB - 1))
                            if j or f == 2 * GB - 1:
                                mm.then_inc(pe_step, 1)
                    rank_of(pe, "S", q)
                    rank_of(pe, "DA", q)
                    rank_of(pe, "DB", q)
                    for j in range(4):
                        free(f"O{j}")
                        for i in range(2):
                            n = 2 * j + i
                            mm = pe.matmul(pass_bank(f"O{j}")[:, i * S:(i + 1) * S], yrow[:, n * P:(n + 1) * P],
                                           selT, start=True, stop=True, skip_group_check=True)
                        mm.then_inc(pe_step, 1)

                def skip(q):
                    pe.wait_ge(pe_step, q * per["step"] + M["step"])
                    pe.sem_inc(pe_step, per["step"])

                all_passes(pe, one, skip)
                st["step"] = M["step"] + PASSES * per["step"]
                pe.wait_ge(act_free, M["A"] + PASSES * per["A"])
                pe.wait_ge(dve_free, M["D"] + PASSES * per["D"])

            pe.wait_ge(consts_in, 64)
            pe.wait_ge(cact_ready, 1)
            for b in range(FIRST_MOD + 1):
                side()

            for l, q0, T in LAYERS:
                L = f"L{l}"
                allk = lambda k: (hH[:, k, :], hL[:, k, :])
                qk_ = lambda k: (hH[:, k, q0:q0 + T], hL[:, k, q0:q0 + T])
                mean_square(f"{L}.n1", view(0, NC, 512), NC, 512)
                pe.wait_ge(nlo_ready, split_at(f"{L}.n1", NC))
                for i in range(KVC):
                    lin(f"{L}.kv{i}", allk, 512)
                lin(f"{L}.kr", allk, 512)
                for i in range(QC):
                    lin(f"{L}.q{i}", qk_, T)
                mean_square(f"{L}.nkv", view(4096, KVC, 512), KVC, 512)
                mean_square(f"{L}.nq", view(5120, QC, T), QC, T)
                ckvh, ckvl = view(10240, KVC, 512, F32R), view(11264, KVC, 512, F32R)
                cqh, cql = view(12288, QC, T, F32R), view(12288 + 1536, QC, T, F32R)
                pe.wait_ge(nlo_ready, split_at(f"{L}.nkv", KVC))
                for i in range(4):
                    lin(f"{L}.uk{i}", lambda k: (ckvh[:, k, :], ckvl[:, k, :]), 512)
                s = plan[f"{L}.uv3"]["t0"] // TPS
                for i in range(4):
                    begin(f"{L}.uv{i}")
                    pe.wait_ge(lo_ready, s + 1)
                    o = bank(f"{L}.uv{i}")
                    for k in range(KVC):
                        wh, wl = (w[:, s % SPL, k * 512:(k + 1) * 512] for w in (whi, wlo))
                        xh, xl = (x[:, k, i * P:(i + 1) * P] for x in (ckvh, ckvl))
                        pe.matmul(o, xh, wh, start=(k == 0), stop=False)
                        pe.matmul(o, xl, wh, start=False, stop=False)
                        mm = pe.matmul(o, xh, wl, start=False, stop=(k == KVC - 1))
                    step(mm)
                pe.wait_ge(nlo_ready, split_at(f"{L}.nq", QC))
                for h in range(NH):
                    lin(f"{L}.uq{h}", lambda k: (cqh[:, k, :], cql[:, k, :]), T)
                kT, qT = view(0, NH, 512), view(4096, NH, T)
                pe.wait_ge(rope_ready, (l + 1) * (NH + 1))
                for i in range(4):
                    wait_free(pe, f"{L}.uv{i}")

                def qk(hp, qt, hh):
                    h = 2 * hp + hh
                    nk = S if l == 0 and qt < 2 else 2 * S
                    return qT[0:QD, h, qt * P:(qt + 1) * P], kT[0:QD, h, 0:nk], nk
                attention(L, T // P, qk, view(8192, 4, 512), view(15360, 2, 512), view(14336, 2, 512))

                pe.wait_ge(filt_in, 16 * 5 * (l + 1))
                fw = 16384
                begin(f"f{l}.a")
                step(pe.matmul(bank(f"f{l}.a")[0:FH, 0:S], arena[0:EMB, fw:fw + 64], arena[0:EMB, fw + 128:fw + 384],
                               start=True, stop=True))
                begin(f"f{l}.b")
                pe.wait_ge(filt_a, 3 * l + 2)
                step(pe.matmul(bank(f"f{l}.b")[0:FH, 0:S], arena[0:FH, fw + 64:fw + 128],
                               arena[0:FH, fw + 384:fw + 640], start=True, stop=True))
                pe.wait_ge(filt_a, 3 * l + 3)
                for t in range(4):
                    begin(f"f{l}.h{t}")
                    step(pe.matmul(bank(f"f{l}.h{t}"), arena[0:FH, fw + 640 + (t // 2) * P:fw + 640 + (t // 2 + 1) * P],
                                   arena[0:FH, 14336 + (t % 2) * 512:14336 + (t % 2 + 1) * 512], start=True, stop=True))
                begin(f"f{l}.sum")
                pe.wait_ge(filt_d, 5 * l + 4)
                ab = view(14336, 4, 512)
                for c in range(HYC):
                    for t in range(4):
                        mm = pe.matmul(bank(f"f{l}.sum")[:, c:c + 1], ab[:, t, c * P:(c + 1) * P], ones[:, 0:1],
                                       start=(t == 0), stop=(t == 3))
                step(mm)
                pe.wait_ge(filt_d, 5 * l + 5)
                Fm = C("F").rearrange("p (t f) -> p t f", t=2)
                hsum, hdif, h1 = view(14336, 2, 512), view(15360, 2, 512), view(4096, 4, 512)
                for f in range(4):
                    begin(f"f{l}.K{f}")
                    o = bank(f"f{l}.K{f}")
                    src = hsum if f < 2 else hdif
                    for t in range(2):
                        mm = pe.matmul(o, Fm[:, t, f * P:(f + 1) * P], src[:, t, :], start=(t == 0),
                                       stop=(t == 1 and f != 2))
                    if f == 2:
                        for t in range(2):
                            mm = pe.matmul(o, C("alt2"), h1[:, 2 * t + 1, :], start=False, stop=(t == 1))
                    step(mm)

                for c in range(HYC):
                    for v in range(3):
                        lin(f"{L}.hy{c}{v}", qk_, T)
                    side()
                zT, zrow, Z, Y = view(0, HYC, T), view(8192, 2, 512), view(14336, 4, 512), view(4096, 4, 512)
                G = C("G").rearrange("p (f t) -> p f t", f=4)
                for s in range(T // S):
                    u = (0 if l == 0 else 2) + s
                    pe.wait_ge(z_ready, l + 1)
                    for t in range(2):
                        begin(f"{L}.z{s}{t}")
                        for c in range(HYC):
                            mm = pe.transpose(bank(f"{L}.z{s}{t}")[:, c * P:(c + 1) * P],
                                              zT[:, c, s * S + t * P:s * S + (t + 1) * P], ident)
                        step(mm)
                    wait_free(pe, f"{L}.z{s}1")
                    for f in range(4):
                        begin(f"{L}.Z{s}{f}")
                        for t in range(2):
                            mm = pe.matmul(bank(f"{L}.Z{s}{f}"), Fm[:, t, f * P:(f + 1) * P], zrow[:, t, :],
                                           start=(t == 0), stop=(t == 1))
                        step(mm)
                    pe.wait_ge(Y_ready, u + 1)
                    for c in range(HYC):
                        begin(f"{L}.y{s}{c}")
                        for f in range(4):
                            mm = pe.matmul(bank(f"{L}.y{s}{c}")[:, 0:S], Y[:, f, c * P:(c + 1) * P], G[:, f, :],
                                           start=(f == 0), stop=(f == 3))
                        step(mm)
                pe.wait_ge(hylo_ready, (2, 3)[l])
                oh, ol = view(10240, 4, T, F32R), view(12288, 4, T, F32R)
                yh, yl = view(0, 4, T, F32R), view(2048, 4, T, F32R)
                wait_free(pe, f"{L}.O{len(attention_order(L, T // P)) // 2 - 1}")
                for n in range(NC):
                    lin(f"{L}.ga{n}", qk_, T)
                    lin(f"{L}.ba{n}", lambda k: (oh[:, k, :], ol[:, k, :]), T)
                    lin(f"{L}.gh{n}", qk_, T)
                    lin(f"{L}.bh{n}", lambda k: (yh[:, k, :], yl[:, k, :]), T)
                    side()
                pe.wait_ge(mlo_ready, l + 1)
                for n in range(NC):
                    lin(f"{L}.o{n}", qk_, T)
                mean_square(f"{L}.n2", view(0, NC, T), NC, T)
                pe.wait_ge(nlo_ready, split_at(f"{L}.n2", NC))
                if l == 1:
                    h32 = view(0, NC, S)
                    router = Vv("router").rearrange("p (k e) -> p k e", k=NC)
                    for t in range(2):
                        begin(f"route{t}")
                        for k in range(NC):
                            mm = pe.matmul(bank(f"route{t}")[:, 0:NE], h32[:, k, t * P:(t + 1) * P], router[:, k, :],
                                           start=(k == 0), stop=(k == NC - 1))
                        step(mm)
                    hrow = view(2048, 2, D)
                    for i in range(4):
                        t, h = divmod(i, 2)
                        begin(f"hr{i}")
                        for k in range(4):
                            mm = pe.transpose(bank(f"hr{i}")[:, k * P:(k + 1) * P],
                                              h32[:, 4 * h + k, t * P:(t + 1) * P], ident)
                        step(mm)
                    begin("pos")
                    pe.wait_ge(comb_ready, 2)
                    pe.wait_ge(rt_in, 16)
                    tri, chosen = arena[:, 14592:14720], small[:, 64:80]
                    o = bank("pos")
                    for at, lhs in ((0, (tri, None)), (8, (ones, tri)), (16, (ones, ones))):
                        n = [t for t in range(2) if lhs[t] is not None]
                        for t in n:
                            mm = pe.matmul(o[:, at:at + 8], lhs[t], chosen[:, 8 * t:8 * t + 8], start=(t == n[0]),
                                           stop=(t == n[-1]), skip_group_check=True)
                    step(mm)
                    experts(hrow)
                else:
                    hid = lambda k: (view(FF_AT, HALF, T, F32R)[:, k, :], view(FF_AT + HALF * T, HALF, T, F32R)[:, k, :])
                    for q in range(2):
                        for f in range(HALF):
                            lin(f"{L}.ff.{q}.g{f}", qk_, T)
                            lin(f"{L}.ff.{q}.u{f}", qk_, T)
                            side()
                        pe.wait_ge(hidlo_ready, HALF * (q + 1))
                        for n in range(NC):
                            lin(f"{L}.ff.{q}.d{n}", hid, T)
                            if n % 2:
                                side()
                    while mods[0] <= NMODB:
                        side()

            mean_square("final", view(0, NC, S), NC, S)
            hx = lambda k: (hH[:, k, S:2 * S], hL[:, k, S:2 * S])
            for j in range(3):
                mean_square(f"B.pre{j}", view(0, NC, S), NC, S)
                pe.wait_ge(nlo_ready, split_at(f"B.pre{j}", NC))
                if j != 1:
                    feed_forward(f"B.ff{j}", S, S)
                else:
                    for n in range(8):
                        lin(f"B.qk{n}", hx, S)
                    for i in range(2):
                        begin(f"B.v{i}")
                    for k in range(NC):
                        s = plan["B.v0"]["t0"] // TPS + k // 2
                        pe.wait_ge(lo_ready, s + 1)
                        for i in range(2):
                            o = bank(f"B.v{i}")
                            wh, wl = (w[:, s % SPL, (k % 2) * 512:(k % 2 + 1) * 512] for w in (whi, wlo))
                            xh, xl = (x[:, k, S + i * P:S + (i + 1) * P] for x in (hH, hL))
                            pe.matmul(o, xh, wh, start=(k == 0), stop=False)
                            pe.matmul(o, xl, wh, start=False, stop=False)
                            mm = pe.matmul(o, xh, wl, start=False, stop=(k == NC - 1))
                            if (k % 2 == 1 and i == 1) or k == NC - 1:
                                step(mm)
                    qkT = view(2048, 8, S)
                    for n in range(8):
                        wait_free(pe, f"B.qk{n}")
                    for i in range(2):
                        wait_free(pe, f"B.v{i}")

                    def qk(hp, qt, hh):
                        nk = (qt + 1) * P
                        r = slice(64 * hh, 64 * hh + 64)
                        return qkT[r, hp, qt * P:(qt + 1) * P], qkT[r, 4 + hp, 0:nk], nk
                    attention("B", 2, qk, view(4096, 2, 512), view(8192, 2, S), view(7168, 2, S))
                    for n in range(NC):
                        lin(f"B.xr{n}", hx, S)
                    xc = view(2048, NC, S)
                    lw = view(13312, 2 * NC, P)
                    pe.wait_ge(lru_d, 1)
                    pe.wait_ge(blk_in, 32)
                    for n in range(NC):
                        for i, nm in enumerate(("ra", "rx")):
                            begin(f"B.{nm}{n}")
                            step(pe.matmul(bank(f"B.{nm}{n}")[:, 0:S], lw[:, 2 * n + i, :], xc[:, n, :],
                                           start=True, stop=True))
                    for n in range(NC):
                        lin(f"B.yr{n}", hx, S)
                    oh, ol = view(5120, 4, S, F32R), view(6144, 4, S, F32R)
                    yh, yl = view(2048, NC, S, F32R), view(7168, NC, S, F32R)
                    wait_free(pe, "B.O7")
                    pe.wait_ge(lru_d, 6)
                    for n in range(NC):
                        lin(f"B.ga{n}", hx, S)
                        lin(f"B.ba{n}", lambda k: (oh[:, k, :], ol[:, k, :]), S)
                        lin(f"B.gh{n}", hx, S)
                        lin(f"B.bh{n}", lambda k: (yh[:, k, :], yl[:, k, :]), S)
                    pe.wait_ge(mlo_ready, 3)
                    for n in range(NC):
                        lin(f"B.o{n}", hx, S)
                mean_square(f"B.post{j}", view(2048, NC, S), NC, S)

        def splitter(one):
            st = {"s": 0}

            def ahead(name):
                c = plan.name[name]
                done = plan.complete[c - 1] if c else 0
                cap = min(x for x in caps if x >= st["s"])
                for s in range(st["s"], min(cap, max(done + SPL, -(-plan.c[c]["t1"] // TPS)))):
                    one(s)
                    st["s"] = s + 1
            return ahead, st

        def mod_at(col, r):
            return modT[:, col, r:r + 1]

        def x_scale(L, which, r, n):
            l = int(L[1])
            i = {(0, 0): 0, (0, 1): 2, (1, 0): 4, (1, 1): 5}[(l, which)]
            return dv[:, i + r, n:n + 1], mod_at(48 * l + 24 * which + n, r)

        @block.scalar
        def _(act):
            for name in ("cst",):
                act.dma_start(cst[:, :], io[name]).then_inc(consts_in, 16)
            act.dma_start(xs[:, :, 0:S], io["ctxT"].rearrange("(c p) t -> p c t", p=P)).then_inc(consts_in, 16)
            act.dma_start(xs[:, :, S:2 * S], io["xT"].rearrange("(c p) t -> p c t", p=P)).then_inc(consts_in, 16)

            def split_hi(s):
                g = load_no(s)
                act.wait_ge(raw_in[g % RAW], 16 * (g // RAW + 1))
                if s >= SPL:
                    act.wait_ge(pe_step, plan.slot_end[s - SPL])
                act.activation(whi[:, s % SPL, :], raw[:, g % RAW, :], ACT.Copy).then_inc(hi_ready, 1)

            ahead, st = splitter(split_hi)

            def evac(name, *ops):
                ahead(name)
                wait_chunk(act, name)
                for op in ops:
                    ins = op(bank(name))
                ins.then_inc(act_free, 1)

            def squares(label, src, dst):
                act.activation(dst, src, ACT.Square).then_inc(sq_ready, 1)

            def root(label, rst):
                ahead(label)
                wait_free(act, label)
                act.activation(rst, rst, ACT.Sqrt).then_inc(std_ready, 1)

            def his(label, n_of, src, dst):
                for n in range(n_of):
                    act.wait_ge(norm_ready, norm_at(label, n + 1))
                    act.activation(dst(n), src(n), ACT.Copy).then_inc(nhi_ready, 1)

            def attention(l, tiles, scale, oh):
                items = attention_order(l, tiles)
                n = len(items)
                pb = view(7168, 2, S) if l == "B" else view(14336, 2, 512)

                def exps(i):
                    nk = (items[i][1] + 1) * P if l == "B" else S if l == "L0" and items[i][1] < 2 else 2 * S
                    j = i % 2
                    act.wait_ge(nmax_ready, ATTN[l] + i + 1)
                    if l == "B":
                        act.activation(pb[:, j, 0:nk], pb[:, j, 0:nk], ACT.Exp, bias=small[:, j:j + 1],
                                       accum_out=small[:, 2 + j:3 + j]).then_inc(exp_ready, 1)
                        return
                    if i >= 2:
                        wait_chunk(act, f"{l}.PT{i-2}")
                    act.activation(pb[:, j, 0:nk], bank(f"{l}.S{i}")[:, 0:nk], ACT.Exp, bias=small[:, j:j + 1],
                                   scale=scale, accum_out=small[:, 2 + j:3 + j]).then_inc(act_free, 1)

                exps(0)
                for i in range(n + 1):
                    if i + 1 < n:
                        exps(i + 1)
                    if i >= 1 and (i - 1) % 2 == 1:
                        hp, qt, _ = items[i - 1]
                        o = f"{l}.O{(i-1)//2}"
                        wait_chunk(act, o)
                        act.activation(oh[:, hp, qt * P:(qt + 1) * P], bank(o)[:, 0:P], ACT.Copy).then_inc(ohi_ready, 1)

            def merge(l, n, T, sga, sgh):
                if n >= 2:
                    wait_free(act, f"{l}.ba{n-2}")
                evac(f"{l}.ga{n}", lambda o: act.activation(sga[:, n % 2, :], o[:, 0:T], ACT.Sigmoid))
                ahead(f"{l}.ba{n}")
                if n >= 2:
                    wait_free(act, f"{l}.bh{n-2}")
                evac(f"{l}.gh{n}", lambda o: act.activation(sgh[:, n % 2, :], o[:, 0:T], ACT.Sigmoid))
                ahead(f"{l}.bh{n}")

            def feed_forward(name, T):
                L = plan.loops[name]
                assert st["s"] == L["slot"]
                hid_h = view(FF_AT, HALF, T, F32R)
                sg = view(FF_AT + 2 * HALF * T, 2, T)
                h32 = view(FF_AT + 2 * HALF * T + 2 * T, 2, T)
                ends = [plan.slot_end[L["slot"] + s] - L["step"] for s in range(HSLOTS)]
                steps = ends[-1]

                with act.Fori(0, L["times"]) as q:
                    def hi(s):
                        g = NMOD + L["slot"] + s
                        act.wait_ge(raw_in[g % RAW], q * (16 * HSLOTS // RAW) + 16 * (g // RAW + 1))
                        e = ends[s - SPL] if s >= SPL else ends[HSLOTS + s - SPL] - steps
                        act.wait_ge(pe_step, q * steps + (L["step"] + e))
                        act.activation(whi[:, (L["slot"] + s) % SPL, :], raw[:, g % RAW, :], ACT.Copy)\
                           .then_inc(hi_ready, 1)

                    def silu(f):
                        c = plan.c[L["chunk"] + 2 * f]
                        act.wait_ge(pe_step, q * steps + c["end"])
                        if f >= 2:
                            act.wait_ge(dve_free, q * HD + (L["D"] + f - 1))
                        act.activation(sg[:, f % 2, :], ps[:, (L["chunk"] + 2 * f) % BANKS, 0:T], ACT.Silu)\
                           .then_inc(act_free, 1)

                    def hid_hi(f):
                        act.wait_ge(dve_free, q * HD + (L["D"] + f + 1))
                        act.activation(hid_h[:, f, :], h32[:, f % 2, :], ACT.Copy).then_inc(hidhi_ready, 1)

                    for f in range(HALF):
                        hi(2 * f)
                        hi(2 * f + 1)
                        if f >= 1:
                            silu(f - 1)
                        if f >= 2:
                            hid_hi(f - 2)
                    hi(2 * HALF)
                    silu(HALF - 1)
                    hid_hi(HALF - 2)
                    hi(2 * HALF + 1)
                    hid_hi(HALF - 1)
                    for s in range(2 * HALF + 2, HSLOTS):
                        hi(s)
                st["s"] = L["slot"] + HSLOTS * L["times"]

            def experts():
                xh = view(4864, NC, P, F32R)
                sg = view(6912, 2, 256)
                hh = view(7936, 2 * GB, P, F32R)
                assert st["s"] == M["slot"]

                def one(q, expert):
                    def hi(s):
                        g = NMOD + M["slot"] + s
                        act.wait_ge(raw_in[g % RAW], q * (16 * PSLOTS // RAW) + 16 * (g // RAW + 1))
                        e = M["ends"][s - SPL] if s >= SPL else M["ends"][PSLOTS + s - SPL] - per["step"]
                        act.wait_ge(pe_step, q * per["step"] + (M["step"] + e))
                        act.activation(whi[:, (M["slot"] + s) % SPL, :], raw[:, g % RAW, :], ACT.Copy)\
                           .then_inc(hi_ready, 1)

                    def turned(b):
                        pass_chunk(act, f"HT{b}", q)
                        act.activation(hh[:, 2 * b:2 * b + 2, :], pass_bank(f"HT{b}")[:, 0:2 * P]
                                       .rearrange("p (j t) -> p j t", j=2), ACT.Copy).then_inc(hthi_ready, 1)

                    for s in range(SPL):
                        hi(s)
                    for i in range(2):
                        pass_chunk(act, f"X{i}", q)
                        act.activation(xh[:, 4 * i:4 * i + 4, :], pass_bank(f"X{i}")
                                       .rearrange("p (k t) -> p k t", k=4), ACT.Copy).then_inc(xhi_ready, 1)
                    pass_chunk(act, "S", q)
                    act.activation(arena[:, 4608:4864], pass_bank("S")[:, 0:S], ACT.Copy).then_inc(act_free, 1)
                    for b in range(GB):
                        for s in range(4 * b + 3, 4 * b + 6):
                            hi(s)
                        pass_chunk(act, f"GU{b}", q)
                        if b >= 2:
                            rank_of(act, f"GU{b-2}", q)
                        act.activation(sg[:, b % 2, :], pass_bank(f"GU{b}")[:, 0:256], ACT.Silu).then_inc(silu_ready, 1)
                        hi(4 * b + 6)
                        if b:
                            turned(b - 1)
                    turned(GB - 1)
                    for s in range(4 * GB + 3, PSLOTS):
                        hi(s)
                    pass_chunk(act, "DA", q)
                    act.activation(arena[:, 13568:14080], pass_bank("DA"), ACT.Copy).then_inc(act_free, 1)

                def skip(q):
                    for sem_, n, base in ((hi_ready, PSLOTS, M["slot"]), (xhi_ready, 2, 0), (act_free, per["A"], M["A"]),
                                          (silu_ready, GB, 0), (hthi_ready, GB, 0)):
                        act.wait_ge(sem_, q * n + base)
                        act.sem_inc(sem_, n)

                all_passes(act, one, skip)
                st["s"] = M["slot"] + PASSES * PSLOTS

            act.wait_ge(consts_in, 64)
            act.activation(Vv("c3"), Vv("c3"), ACT.Silu).then_inc(cact_ready, 1)
            act.wait_ge(lam_abs, 1)
            e_lam = arena[:, 8256:8264]
            act.activation(e_lam, e_lam, ACT.Exp).then_inc(lam_exp, 1)
            mods = [0]

            def side():
                b = mods[0]
                if b < NMODB:
                    if b >= 2:
                        wait_chunk(act, f"modT{b-2}")
                    if st["s"]:
                        ahead(f"mod{b}")
                    wait_chunk(act, f"mod{b}")
                    act.activation(modrow[:, b % 2, :], bank(f"mod{b}"), ACT.Copy).then_inc(act_free, 1)
                mods[0] = b + 1

            for b in range(FIRST_MOD + 1):
                side()

            for l, q0, T in LAYERS:
                L = f"L{l}"
                squares(f"{L}.n1", xs[:, :, :], view(0, NC, 512))
                root(f"{L}.n1", arena[:, 4096:4608])
                his(f"{L}.n1", NC, lambda n: view(0, NC, 512)[:, n, :], lambda n: hH[:, n, :])
                for i in range(KVC):
                    ahead(f"{L}.kv{i}")
                wait_free(act, f"{L}.kv{KVC-1}")
                squares(f"{L}.nkv", view(15360, KVC, 512), view(4096, KVC, 512))
                ahead(f"{L}.kr")
                for i in range(QC):
                    ahead(f"{L}.q{i}")
                wait_free(act, f"{L}.q{QC-1}")
                squares(f"{L}.nq", view(8192, QC, T), view(5120, QC, T))
                root(f"{L}.nkv", arena[:, 6656:7168])
                root(f"{L}.nq", arena[:, 7168:7168 + T])
                his(f"{L}.nkv", KVC, lambda n: view(15360, KVC, 512)[:, n, :],
                    lambda n: view(10240, KVC, 512, F32R)[:, n, :])
                his(f"{L}.nq", QC, lambda n: view(8192, QC, T)[:, n, :],
                    lambda n: view(12288, QC, T, F32R)[:, n, :])
                kT = view(0, NH, 512)
                for i in range(4):
                    evac(f"{L}.uk{i}",
                         lambda o: act.activation(kT[0:64, 2 * i, :], o[0:64, :], ACT.Copy),
                         lambda o: act.activation(kT[0:64, 2 * i + 1, :], o[64:128, :], ACT.Copy))
                act.wait_ge(nlo_ready, split_at(f"{L}.nq", QC))
                for i in range(4):
                    evac(f"{L}.uv{i}", lambda o: act.activation(view(8192, 4, 512)[:, i, :], o, ACT.Copy))
                for h in range(NH):
                    ahead(f"{L}.uq{h}")
                attention(L, T // P, SCALE, view(10240, 4, T, F32R))

                ahead(f"f{l}.a")
                act.wait_ge(filt_d, 5 * l + 1)
                for t in range(2):
                    ins = act.activation(view(8192, 2, 1024)[:, t, :], arena[:, 15360:16384], ACT.Exp,
                                         scale=C("negt", t, t + 1))
                ins.then_inc(filt_a, 1)
                for i, at in enumerate((384, 640)):
                    act.wait_ge(filt_d, 5 * l + 2 + i)
                    r = arena[0:FH, 16384 + at:16384 + at + S]
                    act.activation(r, r, ACT.Sin).then_inc(filt_a, 1)
                for c in range(HYC):
                    for v in range(3):
                        ahead(f"{L}.hy{c}{v}")
                        wait_chunk(act, f"{L}.hy{c}{v}")
                    side()
                ahead(f"{L}.z00")
                for s in range(T // S):
                    u = (0 if l == 0 else 2) + s
                    act.wait_ge(o_ready, u + 1)
                    act.activation(view(0, HYC, T, F32R)[:, :, s * S:(s + 1) * S], view(9216, HYC, S), ACT.Copy)\
                       .then_inc(hyhi_ready, 1)
                for n in range(NC):
                    merge(L, n, T, view(8192, 2, T), view(9216, 2, T))
                    side()
                act.wait_ge(m_ready, l + 1)
                act.activation(hH[:, :, q0:q0 + T], view(4096, NC, T), ACT.Copy).then_inc(mhi_ready, 1)
                for n in range(NC):
                    ahead(f"{L}.o{n}")
                    wait_chunk(act, f"{L}.o{n}")
                wait_free(act, f"{L}.o{NC-1}")
                squares(f"{L}.n2", xs[:, :, q0:q0 + T], view(0, NC, T))
                root(f"{L}.n2", arena[:, 4096:4096 + T])
                his(f"{L}.n2", NC, lambda n: view(0, NC, T)[:, n, :], lambda n: hH[:, n, q0:q0 + T])
                if l == 1:
                    act.wait_ge(comb_ready, 1)
                    act.activation(small[:, 18:20], small[:, 16:18], ACT.Sigmoid)
                    act.activation(small[:, 20:22], small[:, 16:18], ACT.Sigmoid, scale=-1.0).then_inc(gates_ready, 1)
                    experts()
                else:
                    hid_h = view(FF_AT, HALF, T, F32R)
                    sg = view(FF_AT + 2 * HALF * T, 2, T)
                    h32 = view(FF_AT + 2 * HALF * T + 2 * T, 2, T)

                    def hid_hi(q, f):
                        wait_free(act, f"{L}.ff.{q}.u{f}")
                        act.activation(hid_h[:, f, :], h32[:, f % 2, :], ACT.Copy).then_inc(hidhi_ready, 1)

                    for q in range(2):
                        for f in range(HALF):
                            if f >= 2:
                                wait_free(act, f"{L}.ff.{q}.u{f-2}")
                            evac(f"{L}.ff.{q}.g{f}", lambda o: act.activation(sg[:, f % 2, :], o[:, 0:T], ACT.Silu))
                            ahead(f"{L}.ff.{q}.u{f}")
                            if f:
                                hid_hi(q, f - 1)
                            side()
                        hid_hi(q, HALF - 1)
                        for n in range(NC):
                            ahead(f"{L}.ff.{q}.d{n}")
                            wait_chunk(act, f"{L}.ff.{q}.d{n}")
                            if n % 2:
                                side()
                    while mods[0] <= NMODB:
                        side()
                    wait_free(act, f"L0.ff.1.d{NC-1}")

            act.wait_ge(dve_free, M["D"] + PASSES * per["D"])
            squares("final", xs[:, :, S:2 * S], view(0, NC, S))
            root("final", arena[:, 4096:4096 + S])
            for j in range(3):
                act.wait_ge(norm_ready, norm_at("final" if j == 0 else f"B.post{j-1}", NC))
                squares(f"B.pre{j}", xs[:, :, S:2 * S], view(0, NC, S))
                root(f"B.pre{j}", arena[:, 4096:4096 + S])
                his(f"B.pre{j}", NC, lambda n: view(0, NC, S)[:, n, :], lambda n: hH[:, n, S:2 * S])
                if j != 1:
                    feed_forward(f"B.ff{j}", S)
                    last = f"B.ff{j}.1.d{NC-1}"
                else:
                    for n in range(8):
                        evac(f"B.qk{n}", lambda o: act.activation(view(2048, 8, S)[:, n, :], o[:, 0:S], ACT.Copy))
                    for i in range(2):
                        evac(f"B.v{i}", lambda o: act.activation(view(4096, 2, 512)[:, i, :], o, ACT.Copy))
                    attention("B", 2, SCALE2, view(5120, 4, S, F32R))
                    for n in range(NC):
                        ahead(f"B.xr{n}")
                        wait_chunk(act, f"B.xr{n}")
                    for n in range(NC):
                        for at, nm, bn in ((7168, "ra", "ba"), (9216, "rx", "bx")):
                            evac(f"B.{nm}{n}", lambda o: act.activation(
                                view(at, NC, S)[:, n, :], o[:, 0:S], ACT.Sigmoid, bias=Vv(bn, n, n + 1)))
                    act.wait_ge(lru_d, 2)
                    act.activation(view(11264, NC, S), view(7168, NC, S), ACT.Exp)
                    act.activation(view(15360, NC, S), view(7168, NC, S), ACT.Tanh).then_inc(lru_a, 1)
                    act.wait_ge(lru_d, 3)
                    act.activation(view(7168, NC, S), view(7168, NC, S), ACT.Sqrt).then_inc(lru_a, 1)
                    for n in range(NC):
                        evac(f"B.yr{n}", lambda o: act.activation(view(15360, NC, S)[:, n, :], o[:, 0:S],
                                                                  ACT.Gelu_apprx_tanh))
                    act.wait_ge(lru_d, 5)
                    act.activation(view(2048, NC, S, F32R), view(11264, NC, S), ACT.Copy).then_inc(lru_a, 1)
                    for n in range(NC):
                        merge("B", n, S, view(15360, 2, S), view(15872, 2, S))
                    act.wait_ge(m_ready, 3)
                    act.activation(hH[:, :, S:2 * S], view(13312, NC, S), ACT.Copy).then_inc(mhi_ready, 1)
                    for n in range(NC):
                        ahead(f"B.o{n}")
                        wait_chunk(act, f"B.o{n}")
                    last = f"B.o{NC-1}"
                wait_free(act, last)
                squares(f"B.post{j}", view(0, NC, S), view(2048, NC, S))
                root(f"B.post{j}", arena[:, 4096:4096 + S])

        @block.vector
        def _(dve):
            chain = [0]

            def link(ins):
                chain[0] += 1
                ins.then_inc(d_link, 1)
                dve.wait_ge(d_link, chain[0])

            def split_lo(s):
                dve.wait_ge(hi_ready, s + 1)
                dve.tensor_tensor(wlo[:, s % SPL, :], raw[:, load_no(s) % RAW, :], whi[:, s % SPL, :].bitcast(F32),
                                  ALU.subtract).then_inc(lo_ready, 1)

            ahead, st = splitter(split_lo)

            def evac(name, *ops):
                ahead(name)
                wait_chunk(dve, name)
                for i, op in enumerate(ops):
                    ins = op(bank(name))
                    if i < len(ops) - 1:
                        link(ins)
                ins.then_inc(dve_free, 1)

            def norm(label, dim, T, rst, n_of, src, gain, shift, h32, lo, hi):
                variance(label, dim, T, rst)
                normalise(label, T, rst, n_of, src, gain, shift, h32, lo, hi)

            def variance(label, dim, T, rst):
                evac(label, lambda o: dve.tensor_scalar(rst, o[:, 0:T], 1.0 / dim, EPS, ALU.mult, ALU.add))

            def normalise(label, T, rst, n_of, src, gain, shift, h32, lo, hi):
                dve.wait_ge(std_ready, NORMS.index(label) + 1)
                link(dve.reciprocal(rst, rst))
                streams = 1 if shift is None else T // S

                def low(n):
                    dve.wait_ge(nhi_ready, split_at(label, n + 1))
                    dve.tensor_tensor(lo(n), h32(n), hi(n).bitcast(F32), ALU.subtract).then_inc(nlo_ready, 1)

                for n in range(n_of):
                    w = T // streams
                    for r in range(streams):
                        c = slice(r * w, (r + 1) * w)
                        ins = dve.scalar_tensor_tensor(out=h32(n)[:, c], in0=src(n)[:, c], scalar=gain(r, n),
                                                       in1=rst[:, c], op0=ALU.mult, op1=ALU.mult)
                    if shift is not None:
                        link(ins)
                        for r in range(streams):
                            c = slice(r * w, (r + 1) * w)
                            ins = dve.tensor_scalar(h32(n)[:, c], h32(n)[:, c], shift(r, n), None, ALU.add)
                    ins.then_inc(norm_ready, 1)
                    if lo is not None and n:
                        low(n - 1)
                if lo is not None:
                    low(n_of - 1)

            def rope(name, T, at, dst, head, rest):
                ta, tb = arena[64:96, 16384:16384 + T], arena[64:96, 16896:16896 + T]
                w = slice(512 - T, 512) if T < 512 else slice(0, 512)
                ops = [lambda o: dve.tensor_copy(dst[0:64, head, :], o[0:64, 0:T])] if rest else []
                ahead(name)
                wait_chunk(dve, name)
                o = bank(name)
                if rest:
                    dve.tensor_copy(dst[0:64, head, :], o[0:64, 0:T])
                dve.tensor_tensor(ta, o[64:96, 0:T], C("cos")[64:96, w], ALU.mult)
                dve.tensor_tensor(tb, o[96:128, 0:T], C("sin")[96:128, w], ALU.mult).then_inc(dve_free, 1)
                wait_free(dve, name)
                dve.tensor_tensor(dst[64:96, head, :], ta, tb, ALU.add).then_inc(rope_ready, 1)
                dve.wait_ge(rope_ready, at)

            def attention(l, tiles, scale, oh, ol):
                items = attention_order(l, tiles)
                n = len(items)
                B = l == "B"
                pb = view(7168, 2, S) if B else view(14336, 2, 512)
                pT = view(8192, 2, S) if B else view(15360, 2, 512)
                bias = view(9216, 16, S)

                def keys(i):
                    return (items[i][1] + 1) * P if B else S if l == "L0" and items[i][1] < 2 else 2 * S

                def maxima(i):
                    hp, qt, hh = items[i]
                    nk, j = keys(i), i % 2
                    wait_chunk(dve, f"{l}.S{i}")
                    s = bank(f"{l}.S{i}")[:, 0:nk]
                    if B:
                        if i >= 2:
                            wait_chunk(dve, f"B.PT{i-2}")
                        dve.scalar_tensor_tensor(out=pb[:, j, 0:nk], in0=s, scalar=scale,
                                                 in1=bias[:, qt * NH + 2 * hp + hh, 0:nk], op0=ALU.mult, op1=ALU.add)\
                           .then_inc(dve_free, 1)
                        wait_free(dve, f"B.S{i}")
                        link(dve.memset(pb[0:64, j, nk - 64:nk], -3.4028234663852886e38))
                        s = pb[:, j, 0:nk]
                    link(dve.tensor_reduce(small[:, 4 + j:5 + j], s, AX.X, ALU.max))
                    dve.tensor_scalar(small[:, j:j + 1], small[:, 4 + j:5 + j], -1.0 if B else -scale, None, ALU.mult)\
                       .then_inc(nmax_ready, 1)

                def probs(i):
                    j = i % 2
                    if B:
                        dve.wait_ge(exp_ready, i + 1)
                    else:
                        wait_free(dve, f"{l}.S{i}")
                    link(dve.reciprocal(small[:, 6 + j:7 + j], small[:, 2 + j:3 + j]))
                    dve.tensor_scalar(pb[:, j, 0:keys(i)], pb[:, j, 0:keys(i)], small[:, 6 + j:7 + j], None, ALU.mult)\
                       .then_inc(prob_ready, 1)

                maxima(0)
                for i in range(n + 1):
                    if i < n:
                        probs(i)
                    if i + 1 < n:
                        maxima(i + 1)
                    if i < n:
                        wait_chunk(dve, f"{l}.PT{i}")
                        if i >= 2:
                            wait_chunk(dve, f"{l}.O{(i-2)//2}")
                        dve.tensor_copy(pT[:, i % 2, 0:keys(i)], bank(f"{l}.PT{i}")[:, 0:keys(i)]).then_inc(dve_free, 1)
                    if i >= 1 and (i - 1) % 2 == 1:
                        hp, qt, _ = items[i - 1]
                        o = f"{l}.O{(i-1)//2}"
                        dve.wait_ge(ohi_ready, (ATTN[l] + i) // 2)
                        c = slice(qt * P, (qt + 1) * P)
                        dve.tensor_tensor(ol[:, hp, c], bank(o)[:, 0:P], oh[:, hp, c].bitcast(F32), ALU.subtract)\
                           .then_inc(dve_free, 1)

            def sine_argument(name, l, i, at, tmp):
                x, k = arena[0:FH, 16384 + at:16384 + at + S], arena[0:FH, 16384 + tmp:16384 + tmp + S]
                evac(name, lambda o: dve.tensor_scalar(x, o[0:FH, 0:S], Vv(f"fb{i}{l}")[0:FH, :], Vv(f"freq{l}")[0:FH, :],
                                                       ALU.add, ALU.mult))
                wait_free(dve, name)
                big = 1.5 * 2 ** 23
                link(dve.tensor_scalar(k, x, 1 / (2 * math.pi), big, ALU.mult, ALU.add))
                link(dve.tensor_scalar(k, k, big, None, ALU.subtract))
                link(dve.scalar_tensor_tensor(out=x, in0=k, scalar=-6.28125, in1=x, op0=ALU.mult, op1=ALU.add))
                link(dve.scalar_tensor_tensor(out=x, in0=k, scalar=-(2 * math.pi - 6.28125), in1=x, op0=ALU.mult,
                                              op1=ALU.add))
                dve.tensor_scalar(x, x, 3.1415925, -3.1415925, ALU.min, ALU.max).then_inc(filt_d, 1)

            def merge(l, n, T, sga, sgh, mg, tmp, last):
                ahead(f"{l}.ga{n}")
                wait_free(dve, f"{l}.ga{n}")
                evac(f"{l}.ba{n}", lambda o: dve.tensor_tensor(mg[:, n, :], sga[:, n % 2, :], o[:, 0:T], ALU.mult))
                ahead(f"{l}.gh{n}")
                wait_free(dve, f"{l}.gh{n}")
                evac(f"{l}.bh{n}", lambda o: dve.tensor_tensor(tmp, sgh[:, n % 2, :], o[:, 0:T], ALU.mult))
                wait_free(dve, f"{l}.bh{n}")
                ins = dve.tensor_tensor(mg[:, n, :], mg[:, n, :], tmp, ALU.add)
                if last:
                    ins.then_inc(m_ready, 1)
                else:
                    link(ins)

            def merged_low(k, hi, lo, mg):
                dve.wait_ge(mhi_ready, k)
                dve.tensor_tensor(lo, mg, hi.bitcast(F32), ALU.subtract).then_inc(mlo_ready, 1)

            def feed_forward(name, T, gate, acc, streams):
                L = plan.loops[name]
                assert st["s"] == L["slot"]
                sg = view(FF_AT + 2 * HALF * T, 2, T)
                h32 = view(FF_AT + 2 * HALF * T + 2 * T, 2, T)
                steps = plan.slot_end[L["slot"] + HSLOTS - 1] - L["step"]

                def turn(q):
                    def lo(s):
                        g = NMOD + L["slot"] + s
                        dve.wait_ge(hi_ready, q * HSLOTS + (L["slot"] + s + 1))
                        dve.tensor_tensor(wlo[:, (L["slot"] + s) % SPL, :], raw[:, g % RAW, :],
                                          whi[:, (L["slot"] + s) % SPL, :].bitcast(F32), ALU.subtract)\
                           .then_inc(lo_ready, 1)

                    def mul(f):
                        c = plan.c[L["chunk"] + 2 * f + 1]
                        dve.wait_ge(act_free, q * HA + (L["A"] + f + 1))
                        dve.wait_ge(pe_step, q * steps + c["end"])
                        if f >= 2:
                            dve.wait_ge(hidlo_ready, q * HALF + (L["half"] * HALF + f - 1))
                        dve.tensor_tensor(h32[:, f % 2, :], sg[:, f % 2, :],
                                          ps[:, (L["chunk"] + 2 * f + 1) % BANKS, 0:T], ALU.mult).then_inc(dve_free, 1)

                    for f in range(HALF):
                        lo(2 * f)
                        lo(2 * f + 1)
                        if f >= 1:
                            mul(f - 1)
                    lo(2 * HALF)
                    mul(HALF - 1)
                    nxt = 2 * HALF + 1
                    for n in range(NC):
                        while nxt < min(HSLOTS, 2 * HALF + (HALF * n) // TPS + SPL):
                            lo(nxt)
                            nxt += 1
                        c = plan.c[L["chunk"] + 2 * HALF + n]
                        dve.wait_ge(pe_step, q * steps + c["end"])
                        for r in range(streams):
                            cs = slice(r * S, (r + 1) * S)
                            ins = dve.scalar_tensor_tensor(
                                out=acc(n)[:, cs], in0=ps[:, (L["chunk"] + 2 * HALF + n) % BANKS, cs],
                                scalar=gate(r, n), in1=acc(n)[:, cs], op0=ALU.mult, op1=ALU.add)
                        ins.then_inc(dve_free, 1)
                        dve.wait_ge(dve_free, q * HD + (L["D"] + HALF + n + 1))

                with dve.Fori(0, L["times"]) as q:
                    turn(q)
                st["s"] = L["slot"] + HSLOTS * L["times"]

            def route(hf):
                lg, top = small[:, 24:32], small[:, 32:40]
                cmb, chosen, before = small[:, 40:56], small[:, 64:80], small[:, 80:96]
                for t in range(2):
                    evac(f"route{t}", lambda o: dve.tensor_copy(lg, o[:, 0:NE]))
                    wait_free(dve, f"route{t}")
                    link(dve.max(top, lg))
                    link(dve.max_index(idx[:, :], top, lg))
                    link(dve.tensor_copy(small[:, 12 + 2 * t:14 + 2 * t], idx[:, 0:2]))
                    ins = dve.tensor_tensor(small[:, 16 + t:17 + t], top[:, 0:1], top[:, 1:2], ALU.subtract)
                    if t == 1:
                        ins.then_inc(comb_ready, 1)
                    else:
                        link(ins)
                dve.wait_ge(gates_ready, 1)
                for t in range(2):
                    i0, i1 = small[:, 12 + 2 * t:13 + 2 * t], small[:, 13 + 2 * t:14 + 2 * t]
                    dve.tensor_scalar(lg, C("iota"), i0, None, ALU.is_equal)
                    link(dve.tensor_scalar(top, C("iota"), i1, None, ALU.is_equal))
                    link(dve.tensor_tensor(chosen[:, 8 * t:8 * t + 8], lg, top, ALU.add))
                    link(dve.tensor_scalar(lg, lg, small[:, 18 + t:19 + t], None, ALU.mult))
                    link(dve.scalar_tensor_tensor(out=cmb[:, 8 * t:8 * t + 8], in0=top, scalar=small[:, 20 + t:21 + t],
                                                  in1=lg, op0=ALU.mult, op1=ALU.add))
                dve.tensor_copy(small[:, 22:23], small[:, 21:22]).then_inc(comb_ready, 1)
                hrow = arena[:, 2048:4096].rearrange("p (i w) -> p i w", i=4)
                for i in range(4):
                    evac(f"hr{i}", lambda o: dve.tensor_copy(hrow[:, i, :], o))
                cnt = small[:, 24:32]
                evac("pos", lambda o: dve.tensor_copy(before, o[:, 0:16]), lambda o: dve.tensor_copy(cnt, o[:, 16:24]))
                wait_free(dve, "pos")
                link(dve.scalar_tensor_tensor(out=before, in0=before, scalar=1.0, in1=chosen, op0=ALU.add, op1=ALU.mult))
                p3 = ptab[:, 0:NE, :].rearrange("p e t -> p t e")
                w3 = wtab[:, 0:NE, :].rearrange("p e t -> p t e")
                b3, c3 = (v.rearrange("p (t e) -> p t e", t=2) for v in (before, cmb))
                dve.tensor_scalar(p3, b3, -1.0, None, ALU.add)
                link(dve.tensor_copy(w3, c3))
                over, upto, one = cnt, small[:, 32:40], small[:, 56:64]
                link(dve.tensor_scalar(over, cnt, float(CAP), None, ALU.is_gt))
                link(dve.tensor_tensor_scan(upto, ones[:, 0:NE], over, 0.0, ALU.mult, ALU.add))
                link(dve.tensor_tensor(upto, upto, over, ALU.subtract))
                for j in range(EXTRA):
                    link(dve.tensor_scalar(one, upto, float(j), None, ALU.is_equal))
                    link(dve.tensor_tensor(one, one, over, ALU.mult))
                    link(dve.tensor_reduce(etab[:, 4 + j:5 + j], one, AX.X, ALU.add))
                    for t in range(2):
                        for src, dst, off in ((before, ptab, -1.0 - CAP), (cmb, wtab, 0.0)):
                            link(dve.tensor_tensor(top8, src[:, 8 * t:8 * t + 8], one, ALU.mult))
                            link(dve.tensor_reduce(dst[:, NE + j, t:t + 1], top8, AX.X, ALU.add))
                            link(dve.tensor_scalar(dst[:, NE + j, t:t + 1], dst[:, NE + j, t:t + 1], off, None,
                                                   ALU.add))
                    link(dve.tensor_tensor(one, one, C("iota"), ALU.mult))
                    link(dve.tensor_reduce(etab[:, j:j + 1], one, AX.X, ALU.add))
                dve.tensor_copy(passes_i[0:1, :], etab[0:1, :]).then_inc(table_ready, 1)

            ptab = arena[:, 14848:14848 + 2 * PASSES].rearrange("p (q t) -> p q t", t=2)
            wtab = arena[:, 14912:14912 + 2 * PASSES].rearrange("p (q t) -> p q t", t=2)
            etab, top8 = arena[:, 14976:14984], arena[:, 14984:14992]

            def experts():
                xh, xlo = view(4864, NC, P, F32R), view(5888, NC, P, F32R)
                sg, hid32 = view(6912, 2, 256), view(7424, 2, 256)
                hh, hl = view(7936, 2 * GB, P, F32R), view(10752, 2 * GB, P, F32R)
                sel, selw = view(4096, 2, P), view(4352, 2, P)
                places = arena[:, 14720:14848]
                assert st["s"] == M["slot"]
                dve.wait_ge(rt_in, 16)

                def one(q, expert):
                    def lo(s):
                        r = (M["slot"] + s) % SPL
                        dve.wait_ge(hi_ready, q * PSLOTS + (M["slot"] + s + 1))
                        dve.tensor_tensor(wlo[:, r, :], raw[:, (NMOD + M["slot"] + s) % RAW, :],
                                          whi[:, r, :].bitcast(F32), ALU.subtract).then_inc(lo_ready, 1)

                    def turned(b):
                        dve.wait_ge(hthi_ready, q * GB + (b + 1))
                        dve.tensor_tensor(hl[:, 2 * b:2 * b + 2, :], pass_bank(f"HT{b}")[:, 0:2 * P]
                                          .rearrange("p (j t) -> p j t", j=2), hh[:, 2 * b:2 * b + 2, :].bitcast(F32),
                                          ALU.subtract).then_inc(dve_free, 1)

                    for t in range(2):
                        place = arena[:, bass.ds(q * 2 + (14848 + t), 1)]
                        weight = arena[:, bass.ds(q * 2 + (14912 + t), 1)]
                        dve.tensor_scalar(sel[:, t, :], places, place, None, ALU.is_equal)
                        ins = dve.tensor_scalar(selw[:, t, :], places, place, weight, ALU.is_equal, ALU.mult)
                    ins.then_inc(sel_ready, 1)
                    for s in range(SPL):
                        lo(s)
                    for i in range(2):
                        dve.wait_ge(xhi_ready, q * 2 + (i + 1))
                        dve.tensor_tensor(xlo[:, 4 * i:4 * i + 4, :],
                                          pass_bank(f"X{i}").rearrange("p (k t) -> p k t", k=4),
                                          xh[:, 4 * i:4 * i + 4, :].bitcast(F32), ALU.subtract).then_inc(dve_free, 1)
                    for b in range(GB):
                        for s in range(4 * b + 3, 4 * b + 6):
                            lo(s)
                        dve.wait_ge(silu_ready, q * GB + (b + 1))
                        dve.tensor_tensor(hid32[:, b % 2, :], sg[:, b % 2, :], pass_bank(f"GU{b}")[:, 256:512],
                                          ALU.mult).then_inc(dve_free, 1)
                        lo(4 * b + 6)
                        if b:
                            turned(b - 1)
                    turned(GB - 1)
                    for s in range(4 * GB + 3, PSLOTS):
                        lo(s)
                    pass_chunk(dve, "DB", q)
                    dve.tensor_copy(arena[:, 14080:14592], pass_bank("DB")).then_inc(dve_free, 1)
                    for j in range(4):
                        pass_chunk(dve, f"O{j}", q)
                        for i in range(2):
                            n = 2 * j + i
                            xv = xs[:, n, S:2 * S]
                            ins = dve.scalar_tensor_tensor(out=xv, in0=pass_bank(f"O{j}")[:, i * S:(i + 1) * S],
                                                           scalar=mod_at(48 + 40 + n, 1), in1=xv, op0=ALU.mult,
                                                           op1=ALU.add)
                        ins.then_inc(dve_free, 1)

                def skip(q):
                    for sem_, n, base in ((lo_ready, PSLOTS, M["slot"]), (sel_ready, 1, 0),
                                          (dve_free, per["D"], M["D"])):
                        dve.wait_ge(sem_, q * n + base)
                        dve.sem_inc(sem_, n)

                all_passes(dve, one, skip)
                st["s"] = M["slot"] + PASSES * PSLOTS

            mods = [0]

            def side():
                b = mods[0] - 1
                if 0 <= b < NMODB:
                    if st["s"]:
                        ahead(f"modT{b}")
                    wait_chunk(dve, f"modT{b}")
                    o = bank(f"modT{b}").rearrange("p (q j r) -> p q r j", q=4, j=4)
                    dve.tensor_reduce(modT[:, 4 * b:4 * b + 4, :], o[:, :, 0:3, :], AX.X, ALU.add).then_inc(dve_free, 1)
                mods[0] += 1

            def add_bias(name, col, n, rs, at=0):
                wait_free(dve, f"modT{(col + n - 1) // 4}")
                for r in rs:
                    m = modT[:, col:col + n, r]
                    ins = dve.tensor_tensor(m, m, Vv(name, at, at + n), ALU.add)
                link(ins)

            def scale_vector(i, col, r, g):
                link(dve.scalar_tensor_tensor(out=dv[:, i, :], in0=modT[:, col:col + NC, r], scalar=1.0, in1=g,
                                              op0=ALU.add, op1=ALU.mult))

            def late_modulation():
                add_bias("bm1", 48, 48, (0, 1))
                add_bias("bm2", 96, 72, (2,))
                for r in range(2):
                    scale_vector(4 + r, 48 + 8, r, Vv("n11"))
                scale_vector(6, 48 + 32, 1, Vv("n21"))
                for j in range(3):
                    scale_vector(7 + j, 96 + 24 * j + 8, 2, Vv("pre", 8 * j, 8 * j + 8))
                    link(dve.scalar_tensor_tensor(out=dv[:, 10 + j, :], in0=modT[:, 112 + 24 * j:120 + 24 * j, 2],
                                                  scalar=(0.5, 1.0, 0.5)[j], in1=Vv("post", 8 * j, 8 * j + 8),
                                                  op0=ALU.mult, op1=ALU.mult))

            dve.wait_ge(consts_in, 64)
            a, e, s2, acc_ = (arena[:, 8192 + 64 * i:8200 + 64 * i] for i in range(4))
            dve.tensor_scalar(dv[:, 13, :], Vv("lam"), -1.0, 0.0, ALU.mult, ALU.max)
            link(dve.scalar_tensor_tensor(out=a, in0=Vv("lam"), scalar=-1.0, in1=Vv("lam"), op0=ALU.mult, op1=ALU.max))
            dve.tensor_scalar(e, a, -1.0, None, ALU.mult).then_inc(lam_abs, 1)
            dve.wait_ge(lam_exp, 1)
            link(dve.tensor_scalar(a, e, 2.0, None, ALU.add))
            link(dve.reciprocal(a, a))
            link(dve.tensor_tensor(a, a, e, ALU.mult))
            link(dve.tensor_tensor(s2, a, a, ALU.mult))
            link(dve.tensor_scalar(acc_, s2, 1 / 15, 1 / 13, ALU.mult, ALU.add))
            for c in (1 / 11, 1 / 9, 1 / 7, 1 / 5, 1 / 3, 1.0):
                link(dve.tensor_tensor(acc_, acc_, s2, ALU.mult))
                link(dve.tensor_scalar(acc_, acc_, c, None, ALU.add))
            link(dve.tensor_tensor(acc_, acc_, a, ALU.mult))
            link(dve.scalar_tensor_tensor(out=acc_, in0=acc_, scalar=2.0, in1=dv[:, 13, :], op0=ALU.mult, op1=ALU.add))
            link(dve.tensor_scalar(dv[:, 13, :], acc_, -8.0, None, ALU.mult))
            for b in range(FIRST_MOD + 1):
                side()
            add_bias("bm0", 0, 16, (0, 1))
            for r in range(2):
                scale_vector(r, 8, r, Vv("n10"))

            for l, q0, T in LAYERS:
                L = f"L{l}"
                hf = view(0, NC, 512)
                norm(f"{L}.n1", D, 512, arena[:, 4096:4608], NC, lambda n: xs[:, n, :],
                     lambda r, n: x_scale(L, 0, r, n)[0], lambda r, n: x_scale(L, 0, r, n)[1],
                     lambda n: hf[:, n, :], lambda n: hL[:, n, :], lambda n: hH[:, n, :])
                pkv, pq = view(15360, KVC, 512), view(8192, QC, T)
                for i in range(KVC):
                    evac(f"{L}.kv{i}", lambda o: dve.tensor_copy(pkv[:, i, :], o))
                kT, qT = view(0, NH, 512), view(4096, NH, T)
                for_l = l * (NH + 1)
                rope(f"{L}.kr", 512, for_l + 1, kT, 0, False)
                for h in range(1, NH):
                    ins = dve.tensor_copy(kT[64:96, h, :], kT[64:96, 0, :])
                link(ins)
                for i in range(QC):
                    evac(f"{L}.q{i}", lambda o: dve.tensor_copy(pq[:, i, :], o[:, 0:T]))
                rkv, rq = arena[:, 6656:7168], arena[:, 7168:7168 + T]
                variance(f"{L}.nkv", KV_LORA, 512, rkv)
                variance(f"{L}.nq", Q_LORA, T, rq)
                normalise(f"{L}.nkv", 512, rkv, KVC, lambda n: pkv[:, n, :], lambda r, n: Vv(f"kvn{l}", n, n + 1), None,
                          lambda n: pkv[:, n, :], lambda n: view(11264, KVC, 512, F32R)[:, n, :],
                          lambda n: view(10240, KVC, 512, F32R)[:, n, :])
                normalise(f"{L}.nq", T, rq, QC, lambda n: pq[:, n, :], lambda r, n: Vv(f"qn{l}", n, n + 1), None,
                          lambda n: pq[:, n, :], lambda n: view(12288 + 1536, QC, T, F32R)[:, n, :],
                          lambda n: view(12288, QC, T, F32R)[:, n, :])
                for i in range(4):
                    ahead(f"{L}.uk{i}")
                for i in range(4):
                    ahead(f"{L}.uv{i}")
                for h in range(NH):
                    rope(f"{L}.uq{h}", T, for_l + 2 + h, qT, h, True)
                oh, ol = view(10240, 4, T, F32R), view(12288, 4, T, F32R)
                attention(L, T // P, SCALE, oh, ol)

                dve.wait_ge(filt_in, 16 * 5 * (l + 1))
                dec = arena[:, 15360:16384]
                dve.scalar_tensor_tensor(out=dec, in0=dec, scalar=-1.0, in1=dec, op0=ALU.mult, op1=ALU.max).then_inc(filt_d, 1)
                sine_argument(f"f{l}.a", l, 1, 384, 640)
                sine_argument(f"f{l}.b", l, 2, 640, 384)
                hh, E = view(4096, 4, 512), view(8192, 4, 512)
                dve.wait_ge(filt_a, 3 * l + 1)
                for t in range(4):
                    evac(f"f{l}.h{t}", lambda o: dve.scalar_tensor_tensor(
                        out=hh[:, t, :], in0=o, scalar=C("h1m", t // 2, t // 2 + 1) if t % 2 else 1.0, in1=E[:, t, :],
                        op0=ALU.mult, op1=ALU.mult))
                wait_free(dve, f"f{l}.h3")
                dve.scalar_tensor_tensor(out=view(14336, 4, 512), in0=hh, scalar=-1.0, in1=hh, op0=ALU.mult, op1=ALU.max).then_inc(filt_d, 1)
                evac(f"f{l}.sum", lambda o: dve.reciprocal(small[:, 8:12], o[:, 0:HYC]))
                h4 = arena[:, 4096:6144].rearrange("p (t w c) -> p t w c", t=2, w=2)
                dve.tensor_tensor(view(14336, 2, 512), h4[:, :, 0, :], h4[:, :, 1, :], ALU.add)
                dve.tensor_tensor(view(15360, 2, 512), h4[:, :, 0, :], h4[:, :, 1, :], ALU.subtract).then_inc(filt_d, 1)
                KF = view(6144, 4, 512)
                for f in range(4):
                    evac(f"f{l}.K{f}", lambda o: dve.tensor_copy(KF[:, f, :], o))

                zT, x0 = view(0, HYC, T), view(2048, HYC, T)
                U = view(16384, 2, T)
                for c in range(HYC):
                    for v in range(3):
                        dst = x0[:, c, :] if v == 2 else U[:, v, :]
                        d3 = dst.rearrange("p (s t) -> p s t", t=S)
                        w = [Vv(f"sw{l}", 12 * j + 4 * v + c, 12 * j + 4 * v + c + 1) for j in range(3)]
                        bb = Vv(f"sb{l}", 4 * v + c, 4 * v + c + 1)

                        def o3(o):
                            return o[:, 0:T].rearrange("p (s t) -> p s t", t=S)
                        evac(f"{L}.hy{c}{v}",
                             lambda o: dve.tensor_scalar(dst, o[:, 0:T], w[1], bb, ALU.mult, ALU.add),
                             lambda o: dve.scalar_tensor_tensor(out=d3[:, :, 1:S], in0=o3(o)[:, :, 0:S - 1], scalar=w[0],
                                                                in1=d3[:, :, 1:S], op0=ALU.mult, op1=ALU.add),
                             lambda o: dve.scalar_tensor_tensor(out=d3[:, :, 0:S - 1], in0=o3(o)[:, :, 1:S], scalar=w[2],
                                                                in1=d3[:, :, 0:S - 1], op0=ALU.mult, op1=ALU.add))
                        if v == 1:
                            wait_free(dve, f"{L}.hy{c}1")
                            ins = dve.tensor_tensor(zT[:, c, :], U[:, 0, :], U[:, 1, :], ALU.mult)
                            if c == HYC - 1:
                                ins.then_inc(z_ready, 1)
                            else:
                                link(ins)
                    side()
                dve.wait_ge(z_ready, l + 1)
                wait_free(dve, f"{L}.hy{HYC-1}2")
                zrow, Z, Y, T1 = view(8192, 2, 512), view(14336, 4, 512), view(4096, 4, 512), view(9216, 2, 512)
                for s in range(T // S):
                    u = (0 if l == 0 else 2) + s
                    for t in range(2):
                        evac(f"{L}.z{s}{t}", lambda o: dve.tensor_copy(zrow[:, t, :], o))
                    for f in range(4):
                        evac(f"{L}.Z{s}{f}", lambda o: dve.tensor_copy(Z[:, f, :], o))
                    wait_free(dve, f"{L}.Z{s}3")
                    dve.tensor_tensor(T1, Z[:, 2:4, :], KF[:, 2:4, :], ALU.mult)
                    dve.tensor_tensor(Y[:, 2:4, :], Z[:, 0:2, :], KF[:, 2:4, :], ALU.mult)
                    link(dve.tensor_tensor(Y[:, 0:2, :], Z[:, 0:2, :], KF[:, 0:2, :], ALU.mult))
                    link(dve.tensor_tensor(Z[:, 0:2, :], Z[:, 2:4, :], KF[:, 0:2, :], ALU.mult))
                    for t in range(2):
                        dve.scalar_tensor_tensor(out=Y[:, t, :], in0=T1[:, t, :], scalar=C("negm", t, t + 1),
                                                 in1=Y[:, t, :], op0=ALU.mult, op1=ALU.add)
                    link(dve.tensor_tensor(Y[:, 2:4, :], Y[:, 2:4, :], Z[:, 0:2, :], ALU.add))
                    dve.tensor_copy(Y[0:1, 2, :], T1[0:1, 0, :]).then_inc(Y_ready, 1)
                    dve.wait_ge(Y_ready, u + 1)
                    o32, tmp = view(9216, HYC, S), view(14336, 2, S)
                    for c in range(HYC):
                        zc, xc = zT[:, c, s * S:(s + 1) * S], x0[:, c, s * S:(s + 1) * S]
                        link(dve.tensor_scalar(tmp[:, 0, :], zc, Vv(f"hb{l}", c, c + 1), None, ALU.mult))
                        evac(f"{L}.y{s}{c}", lambda o: dve.scalar_tensor_tensor(
                            out=tmp[:, 1, :], in0=o[:, 0:S], scalar=small[:, 8 + c:9 + c], in1=tmp[:, 0, :],
                            op0=ALU.mult, op1=ALU.add))
                        wait_free(dve, f"{L}.y{s}{c}")
                        ins = dve.tensor_tensor(o32[:, c, :], tmp[:, 1, :], xc, ALU.mult)
                        if c == HYC - 1:
                            ins.then_inc(o_ready, 1)
                        else:
                            link(ins)
                    dve.wait_ge(hyhi_ready, u + 1)
                    dve.tensor_tensor(view(2048, HYC, T, F32R)[:, :, s * S:(s + 1) * S], o32,
                                      view(0, HYC, T, F32R)[:, :, s * S:(s + 1) * S].bitcast(F32), ALU.subtract)\
                        .then_inc(hylo_ready, 1)
                    dve.wait_ge(hylo_ready, u + 1)
                mg = view(4096, NC, T)
                for n in range(NC):
                    merge(L, n, T, view(8192, 2, T), view(9216, 2, T), mg, arena[:, 14336:14336 + T], n == NC - 1)
                    side()
                merged_low(l + 1, hH[:, :, q0:q0 + T], hL[:, :, q0:q0 + T], mg)
                if l == 0:
                    add_bias("bm0", 16, 32, (0, 1), 16)
                    for r in range(2):
                        scale_vector(2 + r, 32, r, Vv("n20"))
                for n in range(NC):
                    ops = []
                    ahead(f"{L}.o{n}")
                    wait_chunk(dve, f"{L}.o{n}")
                    for s in range(T // S):
                        r = 1 if l == 1 else s
                        xv = xs[:, n, q0 + s * S:q0 + (s + 1) * S]
                        ins = dve.scalar_tensor_tensor(out=xv, in0=bank(f"{L}.o{n}")[:, s * S:(s + 1) * S],
                                                       scalar=mod_at(48 * l + 16 + n, r), in1=xv, op0=ALU.mult,
                                                       op1=ALU.add)
                    ins.then_inc(dve_free, 1)
                hf = view(0, NC, T)
                norm(f"{L}.n2", D, T, arena[:, 4096:4096 + T], NC, lambda n: xs[:, n, q0:q0 + T],
                     lambda r, n: x_scale(L, 1, r + l, n)[0], lambda r, n: x_scale(L, 1, r + l, n)[1],
                     lambda n: hf[:, n, :], lambda n: hL[:, n, q0:q0 + T], lambda n: hH[:, n, q0:q0 + T])
                if l == 1:
                    route(hf)
                    experts()
                    continue
                sg = view(FF_AT + 2 * HALF * T, 2, T)
                h32 = view(FF_AT + 2 * HALF * T + 2 * T, 2, T)
                for q in range(2):
                    for f in range(HALF):
                        ahead(f"{L}.ff.{q}.g{f}")
                        wait_free(dve, f"{L}.ff.{q}.g{f}")
                        if q * HALF + f >= 2:
                            dve.wait_ge(hidlo_ready, q * HALF + f - 1)
                        evac(f"{L}.ff.{q}.u{f}",
                             lambda o: dve.tensor_tensor(h32[:, f % 2, :], sg[:, f % 2, :], o[:, 0:T], ALU.mult))
                        side()
                    for n in range(NC):
                        ahead(f"{L}.ff.{q}.d{n}")
                        wait_chunk(dve, f"{L}.ff.{q}.d{n}")
                        for s in range(2):
                            xv = xs[:, n, s * S:(s + 1) * S]
                            ins = dve.scalar_tensor_tensor(out=xv, in0=bank(f"{L}.ff.{q}.d{n}")[:, s * S:(s + 1) * S],
                                                           scalar=mod_at(40 + n, s), in1=xv, op0=ALU.mult, op1=ALU.add)
                        ins.then_inc(dve_free, 1)
                        if n % 2:
                            side()
                while mods[0] <= NMODB:
                    side()
                late_modulation()
                wait_free(dve, f"{L}.ff.1.d{NC-1}")

            dve.wait_ge(dve_free, M["D"] + PASSES * per["D"])
            xl = lambda n: xs[:, n, S:2 * S]
            norm("final", D, S, arena[:, 4096:4096 + S], NC, xl, lambda r, n: Vv("fg", n, n + 1), None, xl, None, None)
            fh = view(0, NC, S)
            for j in range(3):
                norm(f"B.pre{j}", D, S, arena[:, 4096:4096 + S], NC, xl, lambda r, n: dv[:, 7 + j, n:n + 1],
                     lambda r, n: mod_at(96 + 24 * j + n, 2), lambda n: fh[:, n, :], lambda n: hL[:, n, S:2 * S],
                     lambda n: hH[:, n, S:2 * S])
                if j != 1:
                    dve.wait_ge(nlo_ready, split_at(f"B.pre{j}", NC))
                    link(dve.memset(fh, 0.0))
                    feed_forward(f"B.ff{j}", S, lambda r, n: 1.0, lambda n: fh[:, n, :], 1)
                else:
                    for n in range(8):
                        ahead(f"B.qk{n}")
                    for i in range(2):
                        ahead(f"B.v{i}")
                    dve.wait_ge(blk_in, 32)
                    attention("B", 2, SCALE2, view(5120, 4, S, F32R), view(6144, 4, S, F32R))
                    xc = view(2048, NC, S)
                    for n in range(NC):
                        w = [Vv("cw", 8 * i + n, 8 * i + n + 1) for i in range(4)]

                        def tap(i):
                            return lambda o: dve.scalar_tensor_tensor(
                                out=xc[:, n, i:S], in0=o[:, 0:S - i], scalar=w[3 - i], in1=xc[:, n, i:S],
                                op0=ALU.mult, op1=ALU.add)
                        evac(f"B.xr{n}",
                             lambda o: dve.tensor_scalar(xc[:, n, :], o[:, 0:S], w[3], Vv("cb", n, n + 1), ALU.mult,
                                                         ALU.add), tap(1), tap(2), tap(3))
                    wait_free(dve, f"B.xr{NC-1}")
                    link(dve.tensor_copy(small[:, 90:91], small[:, 8:9]))
                    dve.tensor_copy(small[:, 91:92], small[:, 8:9]).then_inc(lru_d, 1)
                    for n in range(NC):
                        ahead(f"B.ra{n}")
                        ahead(f"B.rx{n}")
                    rr, ii, aa, th = view(7168, NC, S), view(9216, NC, S), view(11264, NC, S), view(15360, NC, S)
                    wait_free(dve, f"B.rx{NC-1}")
                    for n in range(NC):
                        ins = dve.tensor_scalar(rr[:, n, :], rr[:, n, :], dv[:, 13, n:n + 1], None, ALU.mult)
                    ins.then_inc(lru_d, 1)
                    link(dve.tensor_tensor(ii, ii, xc, ALU.mult))
                    dve.wait_ge(lru_a, 1)
                    link(dve.tensor_scalar(rr, th, -1.0, 1.0, ALU.mult, ALU.add))
                    link(dve.reciprocal(rr, rr))
                    link(dve.tensor_tensor(rr, rr, th, ALU.mult))
                    dve.tensor_scalar(rr, rr, -2.0, 0.0, ALU.mult, ALU.max).then_inc(lru_d, 1)
                    dve.wait_ge(lru_a, 2)
                    link(dve.tensor_tensor(rr, rr, ii, ALU.mult))
                    for n in range(NC):
                        ins = dve.tensor_tensor_scan(ii[:, n, :], aa[:, n, :], rr[:, n, :], 0.0, ALU.mult, ALU.add)
                    ins.then_inc(lru_d, 1)
                    dve.wait_ge(lru_d, 4)
                    for n in range(NC):
                        ahead(f"B.yr{n}")
                        wait_free(dve, f"B.yr{n}")
                    dve.tensor_tensor(aa, ii, th, ALU.mult).then_inc(lru_d, 1)
                    dve.wait_ge(lru_a, 3)
                    dve.tensor_tensor(view(7168, NC, S, F32R), aa, view(2048, NC, S, F32R).bitcast(F32),
                                      ALU.subtract).then_inc(lru_d, 1)
                    mg = view(13312, NC, S)
                    for n in range(NC):
                        merge("B", n, S, view(15360, 2, S), view(15872, 2, S), mg, arena[:, 16384:16384 + S],
                              n == NC - 1)
                    merged_low(3, hH[:, :, S:2 * S], hL[:, :, S:2 * S], mg)
                    for n in range(NC):
                        evac(f"B.o{n}", lambda o: dve.tensor_copy(fh[:, n, :], o[:, 0:S]))
                rst, t32 = arena[:, 4096:4096 + S], view(2048, NC, S)
                variance(f"B.post{j}", D, S, rst)
                dve.wait_ge(std_ready, NORMS.index(f"B.post{j}") + 1)
                link(dve.reciprocal(rst, rst))
                for n in range(NC):
                    link(dve.scalar_tensor_tensor(out=t32[:, n, :], in0=fh[:, n, :], scalar=dv[:, 10 + j, n:n + 1],
                                                  in1=rst, op0=ALU.mult, op1=ALU.mult))
                    dve.tensor_tensor(xl(n), xl(n), t32[:, n, :], ALU.add).then_inc(norm_ready, 1)
            dve.wait_ge(norm_ready, norm_at("B.post2", NC))
            dve.tensor_copy(small[:, 92:93], small[:, 8:9]).then_inc(out_ready, 1)

        @block.gpsimd
        def _(pool):
            def hidden_low(name, T):
                L = plan.loops.get(name, dict(times=2, half=0))
                hid_h, hid_l = view(FF_AT, HALF, T, F32R).bitcast(F32), view(FF_AT + HALF * T, HALF, T, F32R)
                h32 = view(FF_AT + 2 * HALF * T + 2 * T, 2, T)
                with pool.Fori(0, L["times"]) as q:
                    for f in range(HALF):
                        pool.wait_ge(hidhi_ready, q * HALF + (L["half"] * HALF + f + 1))
                        pool.tensor_tensor(hid_l[:, f, :], h32[:, f % 2, :], hid_h[:, f, :], ALU.subtract)\
                            .then_inc(hidlo_ready, 1)

            for l, q0, T in LAYERS:
                wait_free(pool, f"L{l}.O{len(attention_order('', T // P)) // 2 - 1}")
                fw = 16384
                pool.dma_start(arena[0:EMB, fw:fw + 64], io["fw1"][l]).then_inc(filt_in, 16)
                pool.dma_start(arena[0:FH, fw + 64:fw + 128], io["fw2"][l]).then_inc(filt_in, 16)
                pool.dma_start(arena[0:EMB, fw + 128:fw + 384], io["emb"]).then_inc(filt_in, 16)
                pool.dma_start(arena[0:FH, 14336:15360], io["fw3"][l]).then_inc(filt_in, 16)
                pool.dma_start(arena[:, 15360:16384], io["decay"][l:l + 1, :].broadcast_to([P, 1024]))\
                    .then_inc(filt_in, 16)
                if l == 0:
                    hidden_low("L0.ff", T)
            wait_free(pool, f"L1.bh{NC-1}")
            pool.dma_start(arena[:, 14592:14848], io["rt"]).then_inc(rt_in, 16)
            hidden_low("B.ff0", S)
            wait_free(pool, f"B.ff0.1.d{NC-1}")
            pool.dma_start(arena[:, 9216:13312], io["bias"]).then_inc(blk_in, 16)
            pool.dma_start(arena[:, 13312:15360], io["lru"]).then_inc(blk_in, 16)
            hidden_low("B.ff2", S)


def _tiles(w):
    k, n = w.shape
    return w.reshape(k // P, P, n // P, P).transpose(2, 0, 1, 3).reshape(-1, P, P)


def _rows(w):
    k, n = w.shape
    return w.reshape(k // P, P, n // P, P).transpose(0, 2, 1, 3).reshape(-1, P, P)


def _cols(v):
    return v.reshape(-1, P).T


def _constants():
    c = np.zeros((P, NCST), np.float32)

    def put(name, a, rows=slice(0, P)):
        at, w = CST[name]
        c[rows, at:at + w] = a
    put("ident", np.eye(P))
    put("ones", 1.0)
    t = np.arange(S)
    f = np.arange(S)
    ang = 2 * np.pi * ((t[:, None] * f[None, :]) % (2 * S)) / (2 * S)
    Fr, Fi = np.cos(ang), -np.sin(ang)
    Fi[:, 0] = (-1.0) ** t
    F = np.concatenate([Fr, Fi], 1)
    put("F", F.reshape(2, P, 2 * S).transpose(1, 0, 2).reshape(P, -1))
    Gr, Gi = 2 * np.cos(ang).T / (2 * S), -2 * np.sin(ang).T / (2 * S)
    Gr[0] = 1 / (2 * S)
    Gi[0] = (-1.0) ** t / (2 * S)
    G = np.concatenate([Gr, Gi], 0)
    put("G", G.reshape(4, P, S).transpose(1, 0, 2).reshape(P, -1))
    alt = np.zeros((P, P))
    alt[:, 0] = 2 * (-1.0) ** np.arange(P)
    put("alt2", alt)
    nf = ROPE // 4
    inv = (np.float32(10000.0) ** (-np.arange(nf, dtype=np.float32) / np.float32(nf))).astype(np.float32)
    r = np.repeat(np.arange(S // 64, dtype=np.float32), 64)
    col = np.tile(np.arange(64, dtype=np.float32), S // 64)
    a = np.concatenate([r[:, None] * inv, col[:, None] * inv], -1)
    cos, sin = np.cos(a).T, np.sin(a).T
    put("cos", np.concatenate([np.ones((ROPE, S)), np.concatenate([cos, cos], 0)], 1), slice(64, 96))
    put("sin", np.concatenate([np.zeros((ROPE, S)), np.concatenate([-sin, sin], 0)], 1), slice(96, 128))
    put("iota", np.arange(NE)[None, :])
    lin = np.linspace(0.0, 1.0, S, dtype=np.float32)
    put("negt", -lin.reshape(2, P).T)
    m = np.ones((P, 2))
    m[0, 0] = 0
    put("mask", m)
    put("negm", -m)
    put("h1m", m)
    bands = (EMB - 1) // 2
    phase = np.float32(2.0 * math.pi / S) * np.arange(S, dtype=np.float32)[:, None] * \
        np.linspace(1e-4, bands - 1, bands, dtype=np.float32)
    emb = np.concatenate([lin[:, None], np.cos(phase), -np.sin(phase)], -1).T
    return c, np.ascontiguousarray(emb, np.float32)


def _lay_out(i):
    f = lambda n: np.asarray(i[n], np.float32)
    tiles = []
    z = lambda k, n: np.zeros((k, n), np.float32)
    half = ROPE // 2

    def swap(w):
        return np.concatenate([w[:, half:], w[:, :half]], 1)

    def ffn(g, u, d):
        out = []
        for h in range(2):
            cs = slice(h * HALF * P, (h + 1) * HALF * P)
            gt, ut = (_tiles(w[:, cs]).reshape(HALF, NC, P, P) for w in (g, u))
            out += [np.stack([gt, ut], 1).reshape(-1, P, P), _tiles(d[cs])]
        return out

    for l in range(2):
        w = f("w_in")[l]
        tiles.append(_tiles(w[:, KV_START:KV_START + KV_LORA]))
        kr = w[:, KV_START + KV_LORA:HY_START]
        tiles.append(_tiles(np.concatenate([z(D, 64), kr, swap(kr)], 1)))
        tiles.append(_tiles(w[:, :Q_LORA]))
        tiles.append(_tiles(f("w_uk")[l]))
        tiles.append(_rows(f("w_uv")[l]))
        uq = f("w_uq")[l].reshape(Q_LORA, NH, QD)
        for h in range(NH):
            tiles.append(_tiles(np.concatenate([uq[:, h], swap(uq[:, h, NOPE:])], 1)))
        hy = _tiles(w[:, HY_START:GATE_START]).reshape(3, HYC, NC, P, P)
        tiles.append(hy.transpose(1, 0, 2, 3, 4).reshape(-1, P, P))
        ga = _tiles(w[:, GATE_START:GATE_START + D]).reshape(NC, NC, P, P)
        gh = _tiles(w[:, GATE_START + D:]).reshape(NC, NC, P, P)
        ba, bh = (_tiles(f(n)[l]).reshape(NC, 4, P, P) for n in ("w_br_attn", "w_br_hy"))
        tiles.append(np.concatenate([ga, ba, gh, bh], 1).reshape(-1, P, P))
        tiles.append(_tiles(f("w_out")[l]))
        if l == 0:
            tiles += ffn(f("ffn_w_gate")[0], f("ffn_w_up")[0], f("ffn_w_down")[0])
        else:
            for e in range(NE):
                g, u = (f(n)[0, e].reshape(NC, P, GB, 2, P).transpose(2, 0, 3, 1, 4)
                        for n in ("moe_w_gate", "moe_w_up"))
                tiles.append(np.concatenate([g, u], 2).reshape(-1, P, P))
                tiles.append(_rows(f("moe_w_down")[0, e]))
    gu = f("ffn1_w_gu_2")[0]
    tiles += ffn(gu[:, :DFF], gu[:, DFF:], f("ffn1_w_down_2")[0])
    w = f("w_in_2")[0]
    tiles.append(_tiles(w[:, :2 * AW]))
    tiles.append(_rows(w[:, 2 * AW:3 * AW]))
    tiles.append(_tiles(w[:, 3 * AW:3 * AW + 2 * D]))
    w = w[:, 3 * AW + 2 * D:]
    ga, gh, bh = (_tiles(m).reshape(NC, NC, P, P) for m in (w[:, :D], w[:, D:], f("w_rec_o_2")[0]))
    ba = _tiles(f("w_att_o_2")[0]).reshape(NC, 4, P, P)
    tiles.append(np.concatenate([ga, ba, gh, bh], 1).reshape(-1, P, P))
    tiles.append(_tiles(f("w_out_2")[0]))
    gu = f("ffn2_w_gu_2")[0]
    tiles += ffn(gu[:, :DFF], gu[:, DFF:], f("ffn2_w_down_2")[0])
    total = sum(t.shape[0] for t in tiles)
    wsplit = np.empty((total // TPS, P, TPS, P), np.float32)
    at = 0
    for t in tiles:
        for s in range(t.shape[0]):
            wsplit[(at + s) // TPS, :, (at + s) % TPS] = t[s]
        at += t.shape[0]

    wm = np.concatenate([f("w_mod")[0], f("w_mod")[1], f("w_ada_2")[0]], 1)
    wmod = np.ascontiguousarray(wm.reshape(NC // 2, 2, P, NMODB, 512).transpose(3, 0, 2, 1, 4)).reshape(NMOD, P, SLOT)

    v = np.zeros((P, NVEC), np.float32)

    def put(name, a, rows=P):
        at, w = VEC[name]
        v[0:rows, at:at + w] = a
    for l in range(2):
        put(f"n1{l}", _cols(f("norm1_g")[l]))
        put(f"n2{l}", _cols(f("norm2_g")[l]))
        put(f"qn{l}", _cols(f("q_norm_g")[l]))
        put(f"kvn{l}", _cols(f("kv_norm_g")[l]))
        put(f"sw{l}", _cols(f("hy_short_w")[l].reshape(-1)))
        put(f"sb{l}", _cols(f("hy_short_b")[l]))
        put(f"hb{l}", _cols(f("hy_bias")[l]))
        put(f"bm{l}", _cols(f("b_mod")[l]))
        put(f"fb1{l}", f("hy_b1")[l][:, None], FH)
        put(f"fb2{l}", f("hy_b2")[l][:, None], FH)
        put(f"freq{l}", f("hy_freq")[l][:, None], FH)
    put("fg", _cols(f("final_g")))
    put("bm2", _cols(f("b_ada_2")[0]))
    put("pre", _cols(f("norm_pre_2")[0].reshape(-1)))
    put("post", _cols(f("norm_post_2")[0].reshape(-1)))
    put("cw", _cols(f("conv_w_2")[0].reshape(-1)))
    put("cb", _cols(f("conv_b_2")[0]))
    put("ba", _cols(f("lru_ba_2")[0]))
    put("bx", _cols(f("lru_bx_2")[0]))
    put("lam", _cols(f("lru_lambda_2")[0]))
    put("router", f("moe_router")[0].reshape(NC, P, NE).transpose(1, 0, 2).reshape(P, -1))
    c3 = np.zeros((P, NC, 32), np.float32)
    for r, n in enumerate(("c_ctx", "c", "c_2")):
        c3[:, :, r] = _cols(f(n).reshape(-1))
    put("c3", c3.reshape(P, -1))
    cst, emb = _constants()
    q = np.arange(S)[:, None] - np.arange(S)[None, :]
    bias = f("rel_bias_2")[0][:, np.clip(q, -MAXREL, MAXREL) + MAXREL]
    bias = bias.reshape(NH, 2, P, S).transpose(2, 1, 0, 3).reshape(P, -1)
    lru = np.zeros((P, NC, 2, P), np.float32)
    for j, n in enumerate(("lru_wa_2", "lru_wx_2")):
        w = f(n)[0]
        for b in range(2 * NC):
            r = slice(64 * (b % 2), 64 * (b % 2) + 64)
            lru[r, b // 2, j, r] = w[b]
    return {
        "wsplit": wsplit.reshape(total // TPS, P, SLOT), "wmod": wmod, "vec": v, "cst": cst, "emb": emb,
        "xT": np.ascontiguousarray(f("x")[0].T), "ctxT": np.ascontiguousarray(f("ctx")[0].T),
        "fw1": f("hy_w1"), "fw2": f("hy_w2"), "fw3": f("hy_w3"), "decay": f("hy_decay").reshape(2, 2 * HY),
        "rt": np.concatenate([np.triu(np.ones((P, P), np.float32), 1),
                              np.tile(np.arange(P, dtype=np.float32), (P, 1))], 1),
        "bias": np.ascontiguousarray(bias), "lru": lru.reshape(P, -1),
    }


def kernel(**inputs):
    import concourse.bacc as _bacc
    from concourse.bass_utils import run_bass_kernel_spmd as _run

    nc = _bacc.Bacc("TRN2", target_bir_lowering=False, num_devices=1)
    arrays = {f"in_{k}": np.ascontiguousarray(v) for k, v in _lay_out(inputs).items()}
    io = {k[3:]: nc.dram_tensor(k, a.shape, F32, kind="ExternalInput").ap() for k, a in arrays.items()}
    io["out"] = nc.dram_tensor("out_xT", (D, S), F32, kind="ExternalOutput").ap()
    build(nc, io)
    r = _run(nc, [arrays], core_ids=[0])
    return np.ascontiguousarray(r.results[0]["out_xT"].T)[None]
```

```python
import math
from contextlib import ExitStack

import numpy as np

import concourse.bass as bass
from concourse import mybir

ALU = mybir.AluOpType
ACT = mybir.ActivationFunctionType
AX = mybir.AxisListType
F32 = mybir.dt.float32
F32R = mybir.dt.float32r
U32 = mybir.dt.uint32

P = 128
D = 1024
S = 256
NC = D // P
NH = 8
Q_LORA, KV_LORA, NOPE, ROPE, VH = 384, 256, 64, 32, 64
QD = NOPE + ROPE
QC, KVC = Q_LORA // P, KV_LORA // P
HY = 512
HYC = HY // P
EMB, FH = 17, 64
DFF = 2816
HALF = DFF // P // 2
NE = 8
KV_START = Q_LORA
HY_START = KV_START + KV_LORA + ROPE
GATE_START = HY_START + 3 * HY
EPS = 1e-6
SCALE = QD ** -0.5
SCALE2 = 64 ** -0.5
MAXREL = 128
AW = 512
TPS = 8
SLOT = TPS * P
RAW = 11
SPL = 3
NMODB = (2 * 6 + 9) * D // 512
NMOD = NMODB * NC // 2
BANKS = 6
FIRST_MOD = 4
FILTER_STAGES = [[f"f{l}.a" for l in range(2)], [f"f{l}.b" for l in range(2)],
                 [f"f{l}.h{t}" for l in range(2) for t in range(4)], [f"f{l}.sum" for l in range(2)], []]
SPECTRA = [f"f{l}.K{t}" for l in range(2) for t in range(4)]
FILTER_AT = (dict(w=14336, h=4096, E=6144), dict(w=8192, h=10240, E=12288))
FILTER_NORM = (8, 96)
HSLOTS = 3 * HALF
HCHUNKS = 2 * HALF + NC
HA, HD = HALF, HALF + NC
CAP = P
GB = DFF // 256
PSLOTS = GB * 4 + 2 * GB
EXTRA = 2 * S // (CAP + 1)
PASSES = NE + EXTRA


def pass_table():
    order = [("X0", 3, "D"), ("X1", 4, "D"), ("S", 5, "A")]
    for b in range(GB):
        order.append((f"GU{b}", b % 3, "D"))
        if b:
            order.append((f"HT{b-1}", 3 + (b - 1) % 2, "D"))
    order += [(f"HT{GB-1}", 3 + (GB - 1) % 2, "D"), ("DA", 6, "A"), ("DB", 7, "D")]
    order += [(f"O{j}", (5, 0, 1, 2)[j], "D") for j in range(4)]
    chunks, ends, step, rank, slot = {}, [], 0, {"A": 0, "D": 0}, 0
    last = {}
    for name, bank, owner in order:
        if name.startswith("GU"):
            for _ in range(3):
                step += 1
                ends.append(step)
        if name == "DA":
            for _ in range(2 * GB - 1):
                step += 1
                ends.append(step)
        step += 1
        if name.startswith("GU") or name == "DB":
            ends.append(step)
        rank[owner] += 1
        chunks[name] = dict(bank=bank, owner=owner, end=step, rank=rank[owner], before=last.get(bank))
        last[bank] = name
    for c in chunks.values():
        c["wraps"] = c["before"] is None
        if c["wraps"]:
            c["before"] = last[c["bank"]]
    assert len(ends) == PSLOTS
    return chunks, ends, step, rank

VEC = {}
_n = 0
for _name, _w in ([(f"{v}{l}", w) for l in range(2) for v, w in
                   (("n1", 8), ("n2", 8), ("qn", QC), ("kvn", KVC), ("sw", 36), ("sb", 12), ("hb", 4),
                    ("bm", 48), ("fb1", 1), ("fb2", 1), ("freq", 1))] +
                  [("fg", 8), ("bm2", 72), ("pre", 24), ("post", 24), ("cw", 32), ("cb", 8), ("ba", 8),
                   ("bx", 8), ("lam", 8), ("router", 64), ("c3", 256)]):
    VEC[_name] = (_n, _w)
    _n += _w
NVEC = _n
CST = {}
_n = 0
for _name, _w in (("ident", 128), ("ones", 128), ("F", 1024), ("G", 1024), ("cos", 512), ("sin", 512),
                  ("iota", 8), ("negt", 2), ("mask", 2), ("negm", 2), ("h1m", 2), ("alt2", 128)):
    CST[_name] = (_n, _w)
    _n += _w
NCST = _n


class Plan:

    def __init__(self):
        self.c, self.name = [], {}
        self.tiles = 0
        self.steps = 0
        self.slot_end = {}
        self.rank = {"A": 0, "D": 0}
        self.complete = []
        self.mod_end = []
        self.loops = {}
        self.caps = []
        self.mods = 0
        self.order = []

    def chunk(self, name, owner, tiles=0, mod=False):
        if mod:
            self.mod_end += [self.steps + j + 1 for j in range(NC // 2)]
            self.steps += NC // 2 - 1
        t0 = self.tiles
        t1 = t0 + tiles
        for t in range(t0, t1):
            if t % TPS == TPS - 1 and t != t1 - 1:
                self.steps += 1
                self.slot_end[t // TPS] = self.steps
        self.steps += 1
        if tiles and t1 % TPS == 0:
            self.slot_end[t1 // TPS - 1] = self.steps
        self.order += [("split", s) for s in range(-(-t0 // TPS), -(-t1 // TPS))]
        self.tiles = t1
        self.rank[owner] += 1
        self.name[name] = len(self.c)
        self.c.append(dict(name=name, owner=owner, t0=t0, t1=t1, end=self.steps, rank=self.rank[owner]))
        self.complete.append(t1 // TPS)

    def loop(self, name, times):
        assert self.tiles % TPS == 0
        s0 = self.tiles // TPS
        for i in range(SPL if s0 >= SPL else 0):
            assert self.slot_end[s0 - SPL + i] <= self.steps - (3, 1, 0)[i]
        self.caps.append(s0)
        self.loops[name] = dict(slot=s0, chunk=len(self.c), step=self.steps, A=self.rank["A"],
                                D=self.rank["D"], half=2 + sum(v["times"] for v in self.loops.values()), times=times)
        for q in range(times):
            for f in range(HALF):
                self.chunk(f"{name}.{q}.g{f}", "A", TPS)
                self.chunk(f"{name}.{q}.u{f}", "D", TPS)
            for n in range(NC):
                self.chunk(f"{name}.{q}.d{n}", "D", HALF)

    def passes(self):
        chunks, ends, steps, rank = pass_table()
        assert self.tiles % TPS == 0
        s0 = self.tiles // TPS
        for i in range(SPL):
            assert self.slot_end[s0 - SPL + i] <= self.steps - steps + ends[PSLOTS - SPL + i]
        assert min(self.rank["A"] - rank["A"], self.rank["D"] - rank["D"]) >= 0
        self.caps.append(s0)
        self.moe = dict(slot=s0, step=self.steps, A=self.rank["A"], D=self.rank["D"], chunks=chunks, ends=ends,
                        per=dict(step=steps, **rank))
        self.steps += steps * PASSES
        for k in "AD":
            self.rank[k] += rank[k] * PASSES
        for i in range(SPL):
            self.slot_end[s0 + PSLOTS * PASSES - SPL + i] = self.steps - steps + ends[PSLOTS - SPL + i]
        self.tiles += PSLOTS * PASSES * TPS
        for i in range(BANKS):
            self.c.append(dict(name=f"drained{i}", owner="D", t0=self.tiles, t1=self.tiles, end=self.steps,
                               rank=self.rank["D"]))
            self.name[f"drained{i}"] = len(self.c) - 1
            self.complete.append(self.tiles // TPS)

    def side(self):
        b = self.mods
        if b > NMODB:
            return
        self.order += [("mod", 4 * b + j) for j in range(4)] if b < NMODB else []
        if b:
            self.chunk(f"modT{b-1}", "D")
        if b < NMODB:
            self.chunk(f"mod{b}", "A", mod=True)
        self.mods = b + 1

    def __getitem__(self, name):
        return self.c[self.name[name]]


def attention_order(label, tiles):
    items = [(hp, qt, hh) for hp in range(NH // 2) for qt in range(tiles) for hh in range(2)]
    return items


def make_plan():
    p = Plan()

    def attn(l, tiles):
        n = len(attention_order(l, tiles))
        for i in range(2):
            p.chunk(f"{l}.S{i}", "D" if l == "B" else "A")
        for i in range(n + 1):
            if i + 2 < n:
                p.chunk(f"{l}.S{i+2}", "D" if l == "B" else "A")
            if i < n:
                p.chunk(f"{l}.PT{i}", "A")
            if i >= 1 and (i - 1) % 2 == 1:
                p.chunk(f"{l}.O{(i-1)//2}", "D")
        if l != "B":
            names = ["S0"] + [x for i in range(n) for x in ([f"S{i+1}"] if i + 1 < n else []) + [f"PT{i}"]]
            first = p[f"{l}.S0"]["rank"]
            for k, x in enumerate(names):
                p[f"{l}.{x}"]["rank"] = first + k

    for b in range(FIRST_MOD + 1):
        p.side()
        for name in FILTER_STAGES[b]:
            p.chunk(name, "D")
    for l in range(2):
        L = f"L{l}"
        p.chunk(f"{L}.n1", "D")
        if l == 0:
            for name in SPECTRA:
                p.chunk(name, "A")
        for i in range(KVC):
            p.chunk(f"{L}.kv{i}", "D", NC)
        p.chunk(f"{L}.kr", "D", NC)
        p.chunk(f"{L}.nkv", "D")
        for i in range(QC):
            p.chunk(f"{L}.q{i}", "D", NC)
            if l == 0:
                p.side()
        p.chunk(f"{L}.nq", "D")
        for i in range(4):
            p.chunk(f"{L}.uk{i}", "A", KVC)
        for i in range(4):
            p.chunk(f"{L}.uv{i}", "A", 2 * 4 if i == 3 else 0)
        for h in range(NH):
            p.chunk(f"{L}.uq{h}", "D", QC)
            if l == 0 and h % 2:
                p.side()
        attn(L, 4 if l == 0 else 2)
        for c in range(HYC):
            for v in range(3):
                p.chunk(f"{L}.hy{c}{v}", "D", NC)
            p.side()
        streams = range(2 if l == 0 else 1)
        for s in streams:
            p.chunk(f"{L}.z{s}0", "A")
            p.chunk(f"{L}.z{s}1", "D")
        for s in streams:
            for f in range(4):
                p.chunk(f"{L}.Z{s}{f}", "A")
        for s in streams:
            for c in range(HYC):
                p.chunk(f"{L}.y{s}{c}", "D")
        for n in range(NC):
            p.chunk(f"{L}.ga{n}", "A", NC)
            p.chunk(f"{L}.ba{n}", "D", 4)
            p.chunk(f"{L}.gh{n}", "A", NC)
            p.chunk(f"{L}.bh{n}", "D", 4)
            p.side()
        for n in range(NC):
            p.chunk(f"{L}.o{n}", "D", NC)
        p.chunk(f"{L}.n2", "D")
        if l == 1:
            for t in range(2):
                p.chunk(f"route{t}", "D")
            for t in range(4):
                p.chunk(f"hr{t}", "D")
            p.chunk("pos", "D")
            p.passes()
        else:
            for q in range(2):
                for f in range(HALF):
                    p.chunk(f"{L}.ff.{q}.g{f}", "A", NC)
                    p.chunk(f"{L}.ff.{q}.u{f}", "D", NC)
                    p.side()
                for n in range(NC):
                    p.chunk(f"{L}.ff.{q}.d{n}", "D", HALF)
                    if q and n % 2:
                        p.side()
            while p.mods <= NMODB:
                p.side()
    p.chunk("final", "D")
    for j in range(3):
        p.chunk(f"B.pre{j}", "D")
        if j != 1:
            p.loop(f"B.ff{j}", 2)
        else:
            for n in range(8):
                p.chunk(f"B.qk{n}", "A", NC)
            for t in range(2):
                p.chunk(f"B.v{t}", "A", 1 if t == 1 else 31)
            attn("B", 2)
            for n in range(NC):
                p.chunk(f"B.xr{n}", "D", NC)
            for n in range(NC):
                p.chunk(f"B.ra{n}", "A")
                p.chunk(f"B.rx{n}", "A")
            for n in range(NC):
                p.chunk(f"B.yr{n}", "A", NC)
            for n in range(NC):
                p.chunk(f"B.ga{n}", "A", NC)
                p.chunk(f"B.ba{n}", "D", 4)
                p.chunk(f"B.gh{n}", "A", NC)
                p.chunk(f"B.bh{n}", "D", NC)
            for n in range(NC):
                p.chunk(f"B.o{n}", "D", NC)
        p.chunk(f"B.post{j}", "D")
    assert p.tiles % TPS == 0 and p.mods == NMODB + 1
    p.load_at = {key: g for g, key in enumerate(p.order) if key[0] == "mod" or key[1] < p.moe["slot"]}
    assert all(p.load_at[("split", s)] == s + NMOD for s in range(p.moe["slot"] - 3, p.moe["slot"]))
    return p


ARENA = 17408
FF_AT = 4096


def build(nc, io):
    plan = make_plan()
    NSPLIT = plan.tiles // TPS
    caps = plan.caps + [NSPLIT]
    with ExitStack() as ctx:
        def sb(name, shape, dt=F32):
            return ctx.enter_context(nc.sbuf_tensor(name, shape, dt))

        def sem(name):
            return ctx.enter_context(nc.semaphore(name))

        raw = sb("raw", [P, RAW, SLOT])
        whi = sb("whi", [P, SPL, SLOT], F32R)
        wlo = sb("wlo", [P, SPL, SLOT], F32R)
        xs = sb("xs", [P, NC, 2 * S])
        early_at = -(-nc.sbuf_base // 32) * 32
        hH = sb("hH", [P, NC, 2 * S], F32R)
        early = nc.alloc_sbuf_tensor_at("early", [P, NC * 2 * S], F32, offset=early_at)
        hL = sb("hL", [P, NC, 2 * S], F32R)
        arena_at = -(-nc.sbuf_base // 32) * 32
        arena = sb("arena", [P, ARENA])
        rounded = nc.alloc_sbuf_tensor_at("rounded", [P, ARENA], F32R, offset=arena_at)
        vec = sb("vec", [P, NVEC])
        cst = sb("cst", [P, NCST])
        modT = sb("modT", [P, (12 + 12 + 18) * 4, 3])
        dv = sb("dv", [P, 14, NC])
        modrow = sb("modrow", [P, 2, 512])
        passes_i = sb("passes_i", [1, 8], mybir.dt.int32)
        small = sb("small", [P, 104])
        idx = sb("idx", [P, 8], U32)
        ps = ctx.enter_context(nc.psum_tensor("ps", [P, 8, 512], F32))
        M = plan.moe
        per = M["per"]
        PC = M["chunks"]

        def view(at, n, width, dt=F32):
            v = (arena if dt is F32 else rounded)[:, at:at + n * width]
            return v.rearrange("p (n w) -> p n w", n=n)

        def C(name, a=0, b=None):
            at, w = CST[name]
            return cst[:, at + a:at + (w if b is None else b)]

        def Vv(name, a=0, b=None):
            at, w = VEC[name]
            return vec[:, at + a:at + (w if b is None else b)]

        ident, ones = C("ident"), C("ones")

        raw_in = [sem(f"raw_in{i}") for i in range(RAW)]
        hi_ready = sem("hi_ready")
        lo_ready = sem("lo_ready")
        pe_step = sem("pe_step")
        act_free = sem("act_free")
        dve_free = sem("dve_free")
        free_of = {"A": act_free, "D": dve_free}
        vec_in = sem("vec_in")
        consts_in = sem("consts_in")
        streams_in = sem("streams_in")
        cact_ready = sem("cact_ready")
        sq_ready = sem("sq_ready")
        std_ready = sem("std_ready")
        norm_ready = sem("norm_ready")
        nhi_ready = sem("nhi_ready")
        nlo_ready = sem("nlo_ready")
        rope_ready = sem("rope_ready")
        nmax_ready = sem("nmax_ready")
        exp_ready = sem("exp_ready")
        prob_ready = sem("prob_ready")
        ohi_ready = sem("ohi_ready")
        sel_ready = sem("sel_ready")
        xhi_ready = sem("xhi_ready")
        silu_ready = sem("silu_ready")
        hthi_ready = sem("hthi_ready")
        table_ready = sem("table_ready")
        rt_in = sem("rt_in")
        filt_in = sem("filt_in")
        spec_out = sem("spec_out")
        spec_in = sem("spec_in")
        filt_d = sem("filt_d")
        filt_a = sem("filt_a")
        z_ready = sem("z_ready")
        Y_ready = sem("Y_ready")
        o_ready = sem("o_ready")
        hyhi_ready = sem("hyhi_ready")
        hylo_ready = sem("hylo_ready")
        m_ready = sem("m_ready")
        mhi_ready = sem("mhi_ready")
        mlo_ready = sem("mlo_ready")
        hidhi_ready = sem("hidhi_ready")
        hidlo_ready = sem("hidlo_ready")
        comb_ready = sem("comb_ready")
        gates_ready = sem("gates_ready")
        blk_in = sem("blk_in")
        lru_d = sem("lru_d")
        lru_a = sem("lru_a")
        lam_abs = sem("lam_abs")
        lam_exp = sem("lam_exp")
        out_ready = sem("out_ready")
        out_done = sem("out_done")
        d_link = sem("d_link")
        a_link = sem("a_link")
        p_link = sem("p_link")

        NORMS = ["L0.n1", "L0.nkv", "L0.nq", "L0.n2", "L1.n1", "L1.nkv", "L1.nq", "L1.n2", "final",
                 "B.pre0", "B.post0", "B.pre1", "B.post1", "B.pre2", "B.post2"]
        NORM_CHUNKS = {n: KVC if "nkv" in n else QC if "nq" in n else NC for n in NORMS}

        def norm_at(label, n=0):
            return sum(NORM_CHUNKS[m] for m in NORMS[:NORMS.index(label)]) + n

        def sq_at(label, n):
            return norm_at(label, n)

        SPLIT = [n for n in NORMS if n not in ("final", "L1.n2") and "post" not in n]

        def split_at(label, n=0):
            return sum(NORM_CHUNKS[m] for m in SPLIT[:SPLIT.index(label)]) + n

        ATTN = {"L0": 0, "L1": 32, "B": 48}
        ZROW = (8192, 16384)
        LAYERS = ((0, 0, 2 * S), (1, S, S))

        spectra = nc.dram_tensor("spectra", (2, P, 4 * HY), F32, kind="Internal").ap()

        def filter_work(l, at, n):
            return early[0:FH, at:at + n] if l else arena[0:FH, 16384 + at:16384 + at + n]

        block = ctx.enter_context(nc.Block())

        def wait_chunk(eng, name):
            eng.wait_ge(pe_step, plan[name]["end"])

        def wait_free(eng, name):
            eng.wait_ge(free_of[plan[name]["owner"]], plan[name]["rank"])

        def bank(name):
            return ps[:, plan.name[name] % BANKS, :]

        def load_no(s):
            return plan.load_at.get(("split", s), NMOD + s)

        def rank_of(eng, name, q, prior=False):
            c = PC[name]
            o = c["owner"]
            eng.wait_ge(free_of[o], q * per[o] + (M[o] + c["rank"] - (per[o] if prior else 0)))

        def pass_chunk(eng, name, q):
            eng.wait_ge(pe_step, q * per["step"] + (M["step"] + PC[name]["end"]))

        def pass_bank(name):
            return ps[:, PC[name]["bank"], :]

        def all_passes(eng, body, skip, table=True):
            with eng.Fori(0, NE) as q:
                body(q, q)
            eng.wait_ge(table_ready, 1)
            with eng.Fori(0, EXTRA) as j:
                expert = eng.value_load(passes_i[0:1, bass.ds(j, 1)], min_val=0, max_val=NE - 1)
                runs = eng.value_load(passes_i[0:1, bass.ds(j + 4, 1)], min_val=0, max_val=1)
                with eng.If(runs != 0):
                    body(j + NE, expert)
                with eng.Else():
                    skip(j + NE)

        @block.sync
        def _(sp):
            sp.dma_start(vec[:, :], io["vec"]).then_inc(vec_in, 16)
            for l in range(2):
                sp.dma_start(filter_work(l, 0, 64)[0:EMB], io["fw1"][l]).then_inc(filt_in, 16)
                sp.dma_start(filter_work(l, 64, 64), io["fw2"][l]).then_inc(filt_in, 16)
                sp.dma_start(filter_work(l, 128, 256)[0:EMB], io["emb"]).then_inc(filt_in, 16)
                w = FILTER_AT[l]["w"]
                sp.dma_start(arena[0:FH, w:w + 1024], io["fw3"][l]).then_inc(filt_in, 16)
                sp.dma_start(arena[:, w + 1024:w + 2048], io["decay"][l:l + 1, :].broadcast_to([P, 1024]))\
                    .then_inc(filt_in, 16)

            def emptied(key):
                if key[0] == "mod":
                    sp.wait_ge(pe_step, plan.mod_end[key[1]])
                else:
                    sp.wait_ge(lo_ready, key[1] + 1)

            first = [k for k in plan.order if k in plan.load_at]
            for g, (kind, i) in enumerate(first):
                if g >= RAW:
                    emptied(first[g - RAW])
                sp.dma_start(raw[:, g % RAW, :], io["wmod" if kind == "mod" else "wsplit"][i])\
                  .then_inc(raw_in[g % RAW], 16)
            s0 = M["slot"]

            def load_pass(q, expert):
                with sp.Fori(0, PSLOTS // RAW) as k:
                    for j in range(RAW):
                        sp.wait_ge(lo_ready, q * PSLOTS + k * RAW + (s0 - RAW + j + 1))
                        sp.dma_start(raw[:, (NMOD + s0 + j) % RAW, :],
                                     io["wsplit"][bass.ds(expert * PSLOTS + k * RAW + (s0 + j), 1)]
                                     .rearrange("o p w -> p (o w)")).then_inc(raw_in[(NMOD + s0 + j) % RAW], 16)

            def skip(q):
                for j in range(RAW):
                    r = (NMOD + s0 + j) % RAW
                    sp.wait_ge(raw_in[r], q * (16 * PSLOTS // RAW) + 16 * ((NMOD + s0 + j) // RAW))
                    sp.sem_inc(raw_in[r], 16 * PSLOTS // RAW)

            all_passes(sp, load_pass, skip)
            s1 = s0 + PASSES * PSLOTS
            gone = EXTRA * PSLOTS
            turns = (NSPLIT - s1) // RAW
            with sp.Fori(0, turns) as k:
                for j in range(RAW):
                    sp.wait_ge(lo_ready, k * RAW + (s1 - RAW + j + 1))
                    sp.dma_start(raw[:, (NMOD + s1 + j) % RAW, :],
                                 io["wsplit"][bass.ds(k * RAW + (s1 - gone + j), 1)].rearrange("o p w -> p (o w)"))\
                      .then_inc(raw_in[(NMOD + s1 + j) % RAW], 16)
            for s in range(s1 + turns * RAW, NSPLIT):
                sp.wait_ge(lo_ready, s - RAW + 1)
                sp.dma_start(raw[:, (NMOD + s) % RAW, :], io["wsplit"][s - gone]).then_inc(raw_in[(NMOD + s) % RAW], 16)
            sp.wait_ge(out_ready, 1)
            sp.dma_start(io["out"].rearrange("(c p) t -> p c t", p=P), xs[:, :, S:2 * S]).then_inc(out_done, 16)
            sp.wait_ge(out_done, 16)

        @block.tensor
        def _(pe):
            st = {"step": 0}

            def step(mm):
                mm.then_inc(pe_step, 1)
                st["step"] += 1

            def begin(name):
                c = plan.name[name]
                if c >= BANKS:
                    wait_free(pe, plan.c[c - BANKS]["name"])

            def lin(name, mov, T, norm=None, merged=None):
                begin(name)
                c = plan[name]
                for i, t in enumerate(range(c["t0"], c["t1"])):
                    s, r = divmod(t, TPS)
                    if i == 0 or r == 0:
                        pe.wait_ge(lo_ready, s + 1)
                    wh = whi[:, s % SPL, r * P:(r + 1) * P]
                    wl = wlo[:, s % SPL, r * P:(r + 1) * P]
                    xh, xl = mov(i)
                    if norm:
                        pe.wait_ge(nlo_ready, split_at(norm, i + 1))
                    if merged is not None:
                        pe.wait_ge(mlo_ready, merged * NC + i + 1)
                    o = bank(name)[:, 0:T]
                    last = t == c["t1"] - 1
                    pe.matmul(o, wh, xh, start=(i == 0), stop=False)
                    pe.matmul(o, wh, xl, start=False, stop=False)
                    mm = pe.matmul(o, wl, xh, start=False, stop=last)
                    if r == TPS - 1 or last:
                        step(mm)
                assert st["step"] == c["end"], name

            def mean_square(label, sq, n, T):
                begin(label)
                for k in range(n):
                    pe.wait_ge(sq_ready, sq_at(label, k + 1))
                    mm = pe.matmul(bank(label)[:, 0:T], ones, sq[:, k, :], start=(k == 0), stop=(k == n - 1))
                step(mm)

            def mod_block(b):
                begin(f"mod{b}")
                cact = Vv("c3").rearrange("p (k r) -> p k r", k=NC)
                for k in range(NC):
                    g = plan.load_at[("mod", b * (NC // 2) + k // 2)]
                    if k % 2 == 0:
                        pe.wait_ge(raw_in[g % RAW], 16 * (g // RAW + 1))
                    j = k % 4
                    mm = pe.matmul(bank(f"mod{b}")[32 * j:32 * j + 32, :], cact[:, k, :],
                                   raw[:, g % RAW, (k % 2) * 512:(k % 2 + 1) * 512],
                                   start=(k < 4), stop=(k >= 4), skip_group_check=True, tile_position=(0, 32 * j))
                    if k % 2:
                        step(mm)

            def mod_turn(b):
                begin(f"modT{b}")
                wait_free(pe, f"mod{b}")
                for q in range(4):
                    mm = pe.transpose(bank(f"modT{b}")[:, q * P:(q + 1) * P], modrow[:, b % 2, q * P:(q + 1) * P],
                                      ident)
                step(mm)

            mods = [0]

            def side():
                b = mods[0]
                if b > NMODB:
                    return
                if b:
                    mod_turn(b - 1)
                if b < NMODB:
                    mod_block(b)
                mods[0] += 1

            def attention(l, tiles, qk, vt, pT, pv_rows, bufs=2):
                items = attention_order(l, tiles)
                n = len(items)

                def scores(i):
                    begin(f"{l}.S{i}")
                    qa, ka, nk = qk(*items[i])
                    step(pe.matmul(bank(f"{l}.S{i}")[:, 0:nk], qa, ka, start=True, stop=True))

                def turn(i):
                    begin(f"{l}.PT{i}")
                    pe.wait_ge(prob_ready, ATTN[l] + i + 1)
                    nk = qk(*items[i])[2]
                    for c in range(nk // P):
                        mm = pe.transpose(bank(f"{l}.PT{i}")[:, c * P:(c + 1) * P], pv_rows[:, i % bufs, c * P:(c + 1) * P],
                                          ident)
                    step(mm)

                def out(i):
                    hp, qt, hh = items[i]
                    o = f"{l}.O{i//2}"
                    if hh == 0:
                        begin(o)
                    wait_free(pe, f"{l}.PT{i}")
                    nk = qk(*items[i])[2]
                    h = 2 * hp + hh
                    for c in range(nk // P):
                        mm = pe.matmul(bank(o)[64 * hh:64 * hh + 64, 0:P], vt[:, c, h * VH:(h + 1) * VH],
                                       pT[:, i % 2, c * P:(c + 1) * P], start=(c == 0), stop=(c == nk // P - 1),
                                       skip_group_check=True, tile_position=(0, 64 * hh))
                    if hh == 1:
                        step(mm)

                scores(0)
                scores(1)
                for i in range(n + 1):
                    if i + 2 < n:
                        scores(i + 2)
                    if i < n:
                        turn(i)
                    if i >= 1:
                        out(i - 1)

            def feed_forward(name, T, t0):
                L = plan.loops[name]
                for sem_, key in ((act_free, "A"), (dve_free, "D")):
                    pe.wait_ge(sem_, L[key])
                hid_h = view(FF_AT, HALF, T, F32R)
                hid_l = view(FF_AT + HALF * T, HALF, T, F32R)
                with pe.Fori(0, L["times"]) as q:
                    for c in range(HCHUNKS):
                        owner, rank = ("A", c // 2) if c < 2 * HALF and c % 2 == 0 else \
                            ("D", c // 2 if c < 2 * HALF else c - HALF)
                        b = c - BANKS
                        if b < 0:
                            pe.wait_ge(dve_free, q * HD + (L["D"] + 1 + b))
                        elif b < 2 * HALF and b % 2 == 0:
                            pe.wait_ge(act_free, q * HA + (L["A"] + b // 2 + 1))
                        else:
                            pe.wait_ge(dve_free, q * HD + (L["D"] + (b // 2 if b < 2 * HALF else b - HALF) + 1))
                        o = ps[:, (L["chunk"] + c) % BANKS, 0:T]
                        down = c >= 2 * HALF
                        t0_ = c * TPS if not down else 2 * HALF * TPS + (c - 2 * HALF) * HALF
                        nk = HALF if down else NC
                        for i in range(nk):
                            s, r = divmod(t0_ + i, TPS)
                            if i == 0 or r == 0:
                                pe.wait_ge(lo_ready, q * HSLOTS + (L["slot"] + s + 1))
                            if c == 0:
                                pe.wait_ge(nlo_ready, split_at(f"B.pre{name[-1]}", i + 1))
                            if c == 2 * HALF:
                                pe.wait_ge(hidlo_ready, q * HALF + (L["half"] * HALF + i + 1))
                            wh = whi[:, (L["slot"] + s) % SPL, r * P:(r + 1) * P]
                            wl = wlo[:, (L["slot"] + s) % SPL, r * P:(r + 1) * P]
                            xh, xl = (hid_h[:, i, :], hid_l[:, i, :]) if down else \
                                (hH[:, i, t0:t0 + T], hL[:, i, t0:t0 + T])
                            pe.matmul(o, wh, xh, start=(i == 0), stop=False)
                            pe.matmul(o, wh, xl, start=False, stop=False)
                            mm = pe.matmul(o, wl, xh, start=False, stop=(i == nk - 1))
                            if r == TPS - 1 or i == nk - 1:
                                mm.then_inc(pe_step, 1)
                st["step"] = plan[f"{name}.{L['times']-1}.d{NC-1}"]["end"]

            def experts(hrow):
                pe.wait_ge(act_free, M["A"])
                pe.wait_ge(dve_free, M["D"])
                xh, xl = view(4864, NC, P, F32R), view(5888, NC, P, F32R)
                hid32 = view(7424, 2, 256)
                hh, hl = view(7936, 2 * GB, P, F32R), view(10752, 2 * GB, P, F32R)
                sel, selw, selT = view(4096, 2, P), view(4352, 2, P), arena[:, 4608:4864]
                yrow = arena[:, 13568:14592]

                def one(q, expert):
                    def free(name):
                        rank_of(pe, PC[name]["before"], q, PC[name]["wraps"])

                    def weights(s):
                        pe.wait_ge(lo_ready, q * PSLOTS + (M["slot"] + s + 1))
                        return (M["slot"] + s) % SPL

                    def high(s):
                        pe.wait_ge(hi_ready, q * PSLOTS + (M["slot"] + s + 1))
                        return (M["slot"] + s) % SPL

                    pe.wait_ge(sel_ready, q + 1)
                    for i in range(2):
                        free(f"X{i}")
                        for k in range(4):
                            for t in range(2):
                                mm = pe.matmul(pass_bank(f"X{i}")[:, k * P:(k + 1) * P],
                                               hrow[:, t, (4 * i + k) * P:(4 * i + k + 1) * P], sel[:, t, :],
                                               start=(t == 0), stop=(t == 1), skip_group_check=True)
                        mm.then_inc(pe_step, 1)
                    free("S")
                    for t in range(2):
                        mm = pe.transpose(pass_bank("S")[:, t * P:(t + 1) * P], selw[:, t, :], ident)
                    mm.then_inc(pe_step, 1)
                    rank_of(pe, "X1", q)

                    def turn(b):
                        free(f"HT{b}")
                        rank_of(pe, f"GU{b}", q)
                        for j in range(2):
                            mm = pe.transpose(pass_bank(f"HT{b}")[:, j * P:(j + 1) * P],
                                              hid32[:, b % 2, j * P:(j + 1) * P], ident)
                        mm.then_inc(pe_step, 1)

                    for b in range(GB):
                        free(f"GU{b}")
                        o = pass_bank(f"GU{b}")

                        def low_product(i, last):
                            r = weights(4 * b + i)
                            for k in (2 * i, 2 * i + 1):
                                mm = pe.matmul(o, xh[:, k, :], wlo[:, r, (k % 2) * 512:(k % 2 + 1) * 512],
                                               start=False, stop=(last and k % 2 == 1))
                            return mm

                        for i in range(4):
                            r = high(4 * b + i)
                            for k in (2 * i, 2 * i + 1):
                                wh = whi[:, r, (k % 2) * 512:(k % 2 + 1) * 512]
                                pe.matmul(o, xh[:, k, :], wh, start=(k == 0), stop=False)
                                mm = pe.matmul(o, xl[:, k, :], wh, start=False, stop=False)
                            if i:
                                mm = low_product(i - 1, False)
                            if i == 3:
                                mm = low_product(3, True)
                            mm.then_inc(pe_step, 1)
                        if b:
                            turn(b - 1)
                    turn(GB - 1)
                    free("DA")
                    free("DB")
                    for f in range(2 * GB):
                        if f % 2 == 0:
                            rank_of(pe, f"HT{f//2}", q)
                        r = high(4 * GB + f)
                        for j, name in enumerate(("DA", "DB")):
                            wh = whi[:, r, j * 512:(j + 1) * 512]
                            pe.matmul(pass_bank(name), hh[:, f, :], wh, start=(f == 0), stop=False)
                            mm = pe.matmul(pass_bank(name), hl[:, f, :], wh, start=False, stop=False)
                        last = f == 2 * GB - 1
                        for g in ([f - 1] if f else []) + ([f] if last else []):
                            r = weights(4 * GB + g)
                            for j, name in enumerate(("DA", "DB")):
                                mm = pe.matmul(pass_bank(name), hh[:, g, :], wlo[:, r, j * 512:(j + 1) * 512],
                                               start=False, stop=(g == f))
                                if g == f:
                                    mm.then_inc(pe_step, 1)
                        if not last:
                            mm.then_inc(pe_step, 1)
                    rank_of(pe, "S", q)
                    rank_of(pe, "DA", q)
                    rank_of(pe, "DB", q)
                    for j in range(4):
                        free(f"O{j}")
                        for i in range(2):
                            n = 2 * j + i
                            mm = pe.matmul(pass_bank(f"O{j}")[:, i * S:(i + 1) * S], yrow[:, n * P:(n + 1) * P],
                                           selT, start=True, stop=True, skip_group_check=True)
                        mm.then_inc(pe_step, 1)

                def skip(q):
                    pe.wait_ge(pe_step, q * per["step"] + M["step"])
                    pe.sem_inc(pe_step, per["step"])

                all_passes(pe, one, skip)
                st["step"] = M["step"] + PASSES * per["step"]
                pe.wait_ge(act_free, M["A"] + PASSES * per["A"])
                pe.wait_ge(dve_free, M["D"] + PASSES * per["D"])

            pe.wait_ge(cact_ready, 1)
            def filters(stage):
                for l in range(2):
                    W = FILTER_AT[l]
                    if stage == 0:
                        pe.wait_ge(filt_in, 16 * 5 * 2)
                        begin(f"f{l}.a")
                        step(pe.matmul(bank(f"f{l}.a")[0:FH, 0:S], filter_work(l, 0, 64)[0:EMB],
                                       filter_work(l, 128, 256)[0:EMB], start=True, stop=True))
                    if stage == 1:
                        begin(f"f{l}.b")
                        pe.wait_ge(filt_a, 1 + l)
                        step(pe.matmul(bank(f"f{l}.b")[0:FH, 0:S], filter_work(l, 64, 64), filter_work(l, 384, 256),
                                       start=True, stop=True))
                    if stage == 2:
                        pe.wait_ge(filt_a, 5 + l)
                        for t in range(4):
                            begin(f"f{l}.h{t}")
                            w3 = W["w"] + (t % 2) * 512
                            step(pe.matmul(bank(f"f{l}.h{t}"), filter_work(l, 640 + (t // 2) * P, P),
                                           arena[0:FH, w3:w3 + 512], start=True, stop=True))
                    if stage == 3:
                        begin(f"f{l}.sum")
                        pe.wait_ge(filt_d, 7 + l)
                        ab = view(W["w"], 4, 512)
                        for c in range(HYC):
                            for t in range(4):
                                mm = pe.matmul(bank(f"f{l}.sum")[:, c:c + 1], ab[:, t, c * P:(c + 1) * P],
                                               ones[:, 0:1], start=(t == 0), stop=(t == 3))
                        step(mm)
                    if stage == 4:
                        pe.wait_ge(filt_d, 9 + l)
                        Fm = C("F").rearrange("p (t f) -> p t f", t=2)
                        hsum, hdif, h1 = view(W["w"], 2, 512), view(W["w"] + 1024, 2, 512), view(W["h"], 4, 512)
                        for f in range(4):
                            begin(f"f{l}.K{f}")
                            o = bank(f"f{l}.K{f}")
                            src = hsum if f < 2 else hdif
                            for t in range(2):
                                mm = pe.matmul(o, Fm[:, t, f * P:(f + 1) * P], src[:, t, :], start=(t == 0),
                                               stop=(t == 1 and f != 2))
                            if f == 2:
                                for t in range(2):
                                    mm = pe.matmul(o, C("alt2"), h1[:, 2 * t + 1, :], start=False, stop=(t == 1))
                            step(mm)

            for b in range(FIRST_MOD + 1):
                side()
                if b == 0:
                    pe.wait_ge(consts_in, 16)
                if b < FIRST_MOD:
                    filters(b)

            for l, q0, T in LAYERS:
                L = f"L{l}"
                allk = lambda k: (hH[:, k, :], hL[:, k, :])
                qk_ = lambda k: (hH[:, k, q0:q0 + T], hL[:, k, q0:q0 + T])
                mean_square(f"{L}.n1", view(0, NC, 512), NC, 512)
                if l == 0:
                    filters(4)
                for i in range(KVC):
                    lin(f"{L}.kv{i}", allk, 512, f"{L}.n1" if i == 0 else None)
                lin(f"{L}.kr", allk, 512)
                mean_square(f"{L}.nkv", view(4096, KVC, 512), KVC, 512)
                for i in range(QC):
                    lin(f"{L}.q{i}", qk_, T)
                    if l == 0:
                        side()
                mean_square(f"{L}.nq", view(5120, QC, T), QC, T)
                ckvh, ckvl = view(10240, KVC, 512, F32R), view(11264, KVC, 512, F32R)
                cqh, cql = view(12288, QC, T, F32R), view(12288 + 1536, QC, T, F32R)
                for i in range(4):
                    lin(f"{L}.uk{i}", lambda k: (ckvh[:, k, :], ckvl[:, k, :]), 512, f"{L}.nkv" if i == 0 else None)
                s = plan[f"{L}.uv3"]["t0"] // TPS
                for i in range(4):
                    begin(f"{L}.uv{i}")
                    pe.wait_ge(lo_ready, s + 1)
                    o = bank(f"{L}.uv{i}")
                    for k in range(KVC):
                        wh, wl = (w[:, s % SPL, k * 512:(k + 1) * 512] for w in (whi, wlo))
                        xh, xl = (x[:, k, i * P:(i + 1) * P] for x in (ckvh, ckvl))
                        pe.matmul(o, xh, wh, start=(k == 0), stop=False)
                        pe.matmul(o, xl, wh, start=False, stop=False)
                        mm = pe.matmul(o, xh, wl, start=False, stop=(k == KVC - 1))
                    step(mm)
                pe.wait_ge(nlo_ready, split_at(f"{L}.nq", QC))
                for h in range(NH):
                    lin(f"{L}.uq{h}", lambda k: (cqh[:, k, :], cql[:, k, :]), T)
                    if l == 0 and h % 2:
                        side()
                kT, qT = view(0, NH, 512), view(4096, NH, T)
                pe.wait_ge(rope_ready, (l + 1) * (NH + 1))
                for i in range(4):
                    wait_free(pe, f"{L}.uv{i}")

                def qk(hp, qt, hh):
                    h = 2 * hp + hh
                    nk = S if l == 0 and qt < 2 else 2 * S
                    return qT[0:QD, h, qt * P:(qt + 1) * P], kT[0:QD, h, 0:nk], nk
                attention(L, T // P, qk, view(8192, 4, 512), view(15360, 2, 512), view(14336, 2, 512))

                for c in range(HYC):
                    for v in range(3):
                        lin(f"{L}.hy{c}{v}", qk_, T)
                    side()
                zT, Z, Y = view(0, HYC, T), view(14336, 4, 512), view(4096, 4, 512)
                Fm = C("F").rearrange("p (t f) -> p t f", t=2)
                G = C("G").rearrange("p (f t) -> p f t", f=4)
                pe.wait_ge(z_ready, l + 1)
                for s in range(T // S):
                    for t in range(2):
                        begin(f"{L}.z{s}{t}")
                        for c in range(HYC):
                            mm = pe.transpose(bank(f"{L}.z{s}{t}")[:, c * P:(c + 1) * P],
                                              zT[:, c, s * S + t * P:s * S + (t + 1) * P], ident)
                        step(mm)
                for s in range(T // S):
                    zrow = view(ZROW[s], 2, 512)
                    wait_free(pe, f"{L}.z{s}0")
                    wait_free(pe, f"{L}.z{s}1")
                    for f in range(4):
                        begin(f"{L}.Z{s}{f}")
                        for t in range(2):
                            mm = pe.matmul(bank(f"{L}.Z{s}{f}"), Fm[:, t, f * P:(f + 1) * P], zrow[:, t, :],
                                           start=(t == 0), stop=(t == 1))
                        step(mm)
                for s in range(T // S):
                    u = (0 if l == 0 else 2) + s
                    pe.wait_ge(Y_ready, u + 1)
                    for c in range(HYC):
                        begin(f"{L}.y{s}{c}")
                        for f in range(4):
                            mm = pe.matmul(bank(f"{L}.y{s}{c}")[:, 0:S], Y[:, f, c * P:(c + 1) * P], G[:, f, :],
                                           start=(f == 0), stop=(f == 3))
                        step(mm)
                oh, ol = view(10240, 4, T, F32R), view(12288, 4, T, F32R)
                yh, yl = view(0, 4, T, F32R), view(2048, 4, T, F32R)
                wait_free(pe, f"{L}.O{len(attention_order(L, T // P)) // 2 - 1}")
                for n in range(NC):
                    lin(f"{L}.ga{n}", qk_, T)
                    lin(f"{L}.ba{n}", lambda k: (oh[:, k, :], ol[:, k, :]), T)
                    lin(f"{L}.gh{n}", qk_, T)
                    pe.wait_ge(hylo_ready, (2, 3)[l])
                    lin(f"{L}.bh{n}", lambda k: (yh[:, k, :], yl[:, k, :]), T)
                    side()
                for n in range(NC):
                    lin(f"{L}.o{n}", qk_, T, merged=l if n == 0 else None)
                mean_square(f"{L}.n2", view(0, NC, T), NC, T)
                if l == 1:
                    h32 = view(0, NC, S)
                    router = Vv("router").rearrange("p (k e) -> p k e", k=NC)
                    for t in range(2):
                        begin(f"route{t}")
                        for k in range(NC):
                            pe.wait_ge(norm_ready, norm_at("L1.n2", k + 1))
                            mm = pe.matmul(bank(f"route{t}")[:, 0:NE], h32[:, k, t * P:(t + 1) * P], router[:, k, :],
                                           start=(k == 0), stop=(k == NC - 1))
                        step(mm)
                    hrow = view(2048, 2, D)
                    for i in range(4):
                        t, h = divmod(i, 2)
                        begin(f"hr{i}")
                        for k in range(4):
                            mm = pe.transpose(bank(f"hr{i}")[:, k * P:(k + 1) * P],
                                              h32[:, 4 * h + k, t * P:(t + 1) * P], ident)
                        step(mm)
                    begin("pos")
                    pe.wait_ge(comb_ready, 2)
                    pe.wait_ge(rt_in, 16)
                    tri, chosen = arena[:, 14592:14720], small[:, 64:80]
                    o = bank("pos")
                    for at, lhs in ((0, (tri, None)), (8, (ones, tri)), (16, (ones, ones))):
                        n = [t for t in range(2) if lhs[t] is not None]
                        for t in n:
                            mm = pe.matmul(o[:, at:at + 8], lhs[t], chosen[:, 8 * t:8 * t + 8], start=(t == n[0]),
                                           stop=(t == n[-1]), skip_group_check=True)
                    step(mm)
                    experts(hrow)
                else:
                    hid = lambda k: (view(FF_AT, HALF, T, F32R)[:, k, :], view(FF_AT + HALF * T, HALF, T, F32R)[:, k, :])
                    for q in range(2):
                        for f in range(HALF):
                            lin(f"{L}.ff.{q}.g{f}", qk_, T, f"{L}.n2" if q + f == 0 else None)
                            lin(f"{L}.ff.{q}.u{f}", qk_, T)
                            side()
                        pe.wait_ge(hidlo_ready, HALF * (q + 1))
                        for n in range(NC):
                            lin(f"{L}.ff.{q}.d{n}", hid, T)
                            if q and n % 2:
                                side()
                    while mods[0] <= NMODB:
                        side()

            mean_square("final", view(0, NC, S), NC, S)
            hx = lambda k: (hH[:, k, S:2 * S], hL[:, k, S:2 * S])
            for j in range(3):
                mean_square(f"B.pre{j}", view(0, NC, S), NC, S)
                if j != 1:
                    feed_forward(f"B.ff{j}", S, S)
                else:
                    for n in range(8):
                        lin(f"B.qk{n}", hx, S, "B.pre1" if n == 0 else None)
                    for i in range(2):
                        begin(f"B.v{i}")
                    for k in range(NC):
                        s = plan["B.v0"]["t0"] // TPS + k // 2
                        pe.wait_ge(lo_ready, s + 1)
                        for i in range(2):
                            o = bank(f"B.v{i}")
                            wh, wl = (w[:, s % SPL, (k % 2) * 512:(k % 2 + 1) * 512] for w in (whi, wlo))
                            xh, xl = (x[:, k, S + i * P:S + (i + 1) * P] for x in (hH, hL))
                            pe.matmul(o, xh, wh, start=(k == 0), stop=False)
                            pe.matmul(o, xl, wh, start=False, stop=False)
                            mm = pe.matmul(o, xh, wl, start=False, stop=(k == NC - 1))
                            if (k % 2 == 1 and i == 1) or k == NC - 1:
                                step(mm)
                    qkT = view(2048, 8, S)
                    for n in range(8):
                        wait_free(pe, f"B.qk{n}")
                    for i in range(2):
                        wait_free(pe, f"B.v{i}")

                    def qk(hp, qt, hh):
                        nk = (qt + 1) * P
                        r = slice(64 * hh, 64 * hh + 64)
                        return qkT[r, hp, qt * P:(qt + 1) * P], qkT[r, 4 + hp, 0:nk], nk
                    attention("B", 2, qk, view(4096, 2, 512), view(8192, 2, S), view(7168, 4, S), 4)
                    for n in range(NC):
                        lin(f"B.xr{n}", hx, S)
                    xc = view(2048, NC, S)
                    lw = view(13312, 2 * NC, P)
                    pe.wait_ge(lru_d, 1)
                    pe.wait_ge(blk_in, 32)
                    for n in range(NC):
                        for i, nm in enumerate(("ra", "rx")):
                            begin(f"B.{nm}{n}")
                            step(pe.matmul(bank(f"B.{nm}{n}")[:, 0:S], lw[:, 2 * n + i, :], xc[:, n, :],
                                           start=True, stop=True))
                    for n in range(NC):
                        lin(f"B.yr{n}", hx, S)
                    oh, ol = view(5120, 4, S, F32R), view(6144, 4, S, F32R)
                    yh, yl = view(2048, NC, S, F32R), view(7168, NC, S, F32R)
                    wait_free(pe, "B.O7")
                    for n in range(NC):
                        lin(f"B.ga{n}", hx, S)
                        lin(f"B.ba{n}", lambda k: (oh[:, k, :], ol[:, k, :]), S)
                        lin(f"B.gh{n}", hx, S)
                        pe.wait_ge(lru_d, 6)
                        lin(f"B.bh{n}", lambda k: (yh[:, k, :], yl[:, k, :]), S)
                    for n in range(NC):
                        lin(f"B.o{n}", hx, S, merged=2 if n == 0 else None)
                mean_square(f"B.post{j}", view(2048, NC, S), NC, S)

        def splitter(one):
            st = {"s": 0}

            def ahead(name):
                if name[0:2] in ("f0", "f1"):
                    return
                c = plan.name[name]
                done = plan.complete[c - 1] if c else 0
                cap = min(x for x in caps if x >= st["s"])
                for s in range(st["s"], min(cap, max(done + SPL, -(-plan.c[c]["t1"] // TPS)))):
                    one(s)
                    st["s"] = s + 1
            return ahead, st

        def mod_at(col, r):
            return modT[:, col, r:r + 1]

        def x_scale(L, which, r, n):
            l = int(L[1])
            i = {(0, 0): 0, (0, 1): 2, (1, 0): 4, (1, 1): 5}[(l, which)]
            return dv[:, i + r, n:n + 1], mod_at(48 * l + 24 * which + n, r)

        @block.scalar
        def _(act):
            for name in ("cst",):
                act.dma_start(cst[:, :], io[name]).then_inc(consts_in, 16)
            act.dma_start(xs[:, :, 0:S], io["ctxT"].rearrange("(c p) t -> p c t", p=P)).then_inc(streams_in, 16)
            act.dma_start(xs[:, :, S:2 * S], io["xT"].rearrange("(c p) t -> p c t", p=P)).then_inc(streams_in, 16)

            def split_hi(s):
                g = load_no(s)
                act.wait_ge(raw_in[g % RAW], 16 * (g // RAW + 1))
                if s >= SPL:
                    act.wait_ge(pe_step, plan.slot_end[s - SPL])
                act.activation(whi[:, s % SPL, :], raw[:, g % RAW, :], ACT.Copy).then_inc(hi_ready, 1)

            ahead, st = splitter(split_hi)

            def evac(name, *ops):
                ahead(name)
                wait_chunk(act, name)
                for op in ops:
                    ins = op(bank(name))
                ins.then_inc(act_free, 1)

            def square(src, dst, n):
                act.activation(dst[:, n, :], src[:, n, :], ACT.Square).then_inc(sq_ready, 1)

            def root(label, rst):
                ahead(label)
                wait_free(act, label)
                act.activation(rst, rst, ACT.Sqrt).then_inc(std_ready, 1)

            def his(label, n_of, src, dst, shift=None, streams=1, beside=()):
                for n in range(n_of):
                    act.wait_ge(norm_ready, norm_at(label, n + 1))
                    if shift is None:
                        ins = act.activation(dst(n), src(n), ACT.Copy)
                    for r in range(streams if shift else 0):
                        c = slice(r * S, (r + 1) * S)
                        ins = act.activation(dst(n)[:, c], src(n)[:, c], ACT.Identity, bias=shift(r, n))
                    ins.then_inc(nhi_ready, 1)
                    if beside:
                        l, f = divmod(n, 4)
                        evac(beside[n], lambda o: act.activation(view(FILTER_AT[l]["E"], 4, 512)[:, f, :], o, ACT.Copy))

            def attention(l, tiles, scale, oh):
                items = attention_order(l, tiles)
                n = len(items)
                pb = view(7168, 4, S) if l == "B" else view(14336, 2, 512)
                pT = view(8192, 2, S) if l == "B" else view(15360, 2, 512)

                def keys(i):
                    return (items[i][1] + 1) * P if l == "B" else S if l == "L0" and items[i][1] < 2 else 2 * S

                def exps(i):
                    nk = keys(i)
                    j = i % 2
                    act.wait_ge(nmax_ready, ATTN[l] + i + 1)
                    if l == "B":
                        act.activation(pb[:, i % 4, 0:nk], pb[:, i % 4, 0:nk], ACT.Exp, bias=small[:, j:j + 1],
                                       accum_out=small[:, 2 + j:3 + j]).then_inc(exp_ready, 1)
                        return
                    if i >= 2:
                        wait_chunk(act, f"{l}.PT{i-2}")
                    act.activation(pb[:, j, 0:nk], bank(f"{l}.S{i}")[:, 0:nk], ACT.Exp, bias=small[:, j:j + 1],
                                   scale=scale, accum_out=small[:, 2 + j:3 + j]).then_inc(act_free, 1)

                exps(0)
                for i in range(n + 1):
                    if i + 1 < n:
                        exps(i + 1)
                    if i < n:
                        nk = keys(i)
                        wait_chunk(act, f"{l}.PT{i}")
                        if i >= 2:
                            wait_chunk(act, f"{l}.O{(i-2)//2}")
                        act.activation(pT[:, i % 2, 0:nk], bank(f"{l}.PT{i}")[:, 0:nk], ACT.Copy).then_inc(act_free, 1)
                    if i >= 1 and (i - 1) % 2 == 1:
                        hp, qt, _ = items[i - 1]
                        o = f"{l}.O{(i-1)//2}"
                        wait_chunk(act, o)
                        act.activation(oh[:, hp, qt * P:(qt + 1) * P], bank(o)[:, 0:P], ACT.Copy).then_inc(ohi_ready, 1)

            def merge(l, n, T, sga, sgh):
                if n >= 2:
                    wait_free(act, f"{l}.ba{n-2}")
                evac(f"{l}.ga{n}", lambda o: act.activation(sga[:, n % 2, :], o[:, 0:T], ACT.Sigmoid))
                ahead(f"{l}.ba{n}")
                if n >= 2:
                    wait_free(act, f"{l}.bh{n-2}")
                evac(f"{l}.gh{n}", lambda o: act.activation(sgh[:, n % 2, :], o[:, 0:T], ACT.Sigmoid))
                ahead(f"{l}.bh{n}")

            def feed_forward(name, T):
                L = plan.loops[name]
                assert st["s"] == L["slot"]
                hid_h = view(FF_AT, HALF, T, F32R)
                sg = view(FF_AT + 2 * HALF * T, 2, T)
                h32 = view(FF_AT + 2 * HALF * T + 2 * T, 2, T)
                ends = [plan.slot_end[L["slot"] + s] - L["step"] for s in range(HSLOTS)]
                steps = ends[-1]

                with act.Fori(0, L["times"]) as q:
                    def hi(s):
                        g = NMOD + L["slot"] + s
                        act.wait_ge(raw_in[g % RAW], q * (16 * HSLOTS // RAW) + 16 * (g // RAW + 1))
                        e = ends[s - SPL] if s >= SPL else ends[HSLOTS + s - SPL] - steps
                        act.wait_ge(pe_step, q * steps + (L["step"] + e))
                        act.activation(whi[:, (L["slot"] + s) % SPL, :], raw[:, g % RAW, :], ACT.Copy)\
                           .then_inc(hi_ready, 1)

                    def silu(f):
                        c = plan.c[L["chunk"] + 2 * f]
                        act.wait_ge(pe_step, q * steps + c["end"])
                        if f >= 2:
                            act.wait_ge(dve_free, q * HD + (L["D"] + f - 1))
                        act.activation(sg[:, f % 2, :], ps[:, (L["chunk"] + 2 * f) % BANKS, 0:T], ACT.Silu)\
                           .then_inc(act_free, 1)

                    def hid_hi(f):
                        act.wait_ge(dve_free, q * HD + (L["D"] + f + 1))
                        act.activation(hid_h[:, f, :], h32[:, f % 2, :], ACT.Copy).then_inc(hidhi_ready, 1)

                    for f in range(HALF):
                        hi(2 * f)
                        hi(2 * f + 1)
                        if f >= 1:
                            silu(f - 1)
                        if f >= 2:
                            hid_hi(f - 2)
                    hi(2 * HALF)
                    silu(HALF - 1)
                    hid_hi(HALF - 2)
                    hi(2 * HALF + 1)
                    hid_hi(HALF - 1)
                    for s in range(2 * HALF + 2, HSLOTS):
                        hi(s)
                st["s"] = L["slot"] + HSLOTS * L["times"]

            def experts():
                xh = view(4864, NC, P, F32R)
                sg = view(6912, 2, 256)
                hh = view(7936, 2 * GB, P, F32R)
                assert st["s"] == M["slot"]

                def one(q, expert):
                    def hi(s):
                        g = NMOD + M["slot"] + s
                        act.wait_ge(raw_in[g % RAW], q * (16 * PSLOTS // RAW) + 16 * (g // RAW + 1))
                        e = M["ends"][s - SPL] if s >= SPL else M["ends"][PSLOTS + s - SPL] - per["step"]
                        act.wait_ge(pe_step, q * per["step"] + (M["step"] + e))
                        act.wait_ge(lo_ready, q * PSLOTS + (M["slot"] + s - SPL + 1))
                        act.activation(whi[:, (M["slot"] + s) % SPL, :], raw[:, g % RAW, :], ACT.Copy)\
                           .then_inc(hi_ready, 1)

                    def turned(b):
                        pass_chunk(act, f"HT{b}", q)
                        act.activation(hh[:, 2 * b:2 * b + 2, :], pass_bank(f"HT{b}")[:, 0:2 * P]
                                       .rearrange("p (j t) -> p j t", j=2), ACT.Copy).then_inc(hthi_ready, 1)

                    for s in range(SPL):
                        hi(s)
                    for i in range(2):
                        pass_chunk(act, f"X{i}", q)
                        act.activation(xh[:, 4 * i:4 * i + 4, :], pass_bank(f"X{i}")
                                       .rearrange("p (k t) -> p k t", k=4), ACT.Copy).then_inc(xhi_ready, 1)
                    pass_chunk(act, "S", q)
                    act.activation(arena[:, 4608:4864], pass_bank("S")[:, 0:S], ACT.Copy).then_inc(act_free, 1)
                    for b in range(GB):
                        for s in range(4 * b + 3, 4 * b + 6):
                            hi(s)
                        pass_chunk(act, f"GU{b}", q)
                        if b >= 2:
                            rank_of(act, f"GU{b-2}", q)
                        act.activation(sg[:, b % 2, :], pass_bank(f"GU{b}")[:, 0:256], ACT.Silu).then_inc(silu_ready, 1)
                        hi(4 * b + 6)
                        if b:
                            turned(b - 1)
                    turned(GB - 1)
                    for s in range(4 * GB + 3, PSLOTS):
                        hi(s)
                    pass_chunk(act, "DA", q)
                    act.activation(arena[:, 13568:14080], pass_bank("DA"), ACT.Copy).then_inc(act_free, 1)

                def skip(q):
                    for sem_, n, base in ((hi_ready, PSLOTS, M["slot"]), (xhi_ready, 2, 0), (act_free, per["A"], M["A"]),
                                          (silu_ready, GB, 0), (hthi_ready, GB, 0)):
                        act.wait_ge(sem_, q * n + base)
                        act.sem_inc(sem_, n)

                all_passes(act, one, skip)
                st["s"] = M["slot"] + PASSES * PSLOTS

            act.wait_ge(vec_in, 16)
            act.activation(Vv("c3"), Vv("c3"), ACT.Silu).then_inc(cact_ready, 1)
            act.wait_ge(lam_abs, 1)
            e_lam = small[:, 32:40]
            act.activation(e_lam, e_lam, ACT.Exp).then_inc(lam_exp, 1)
            mods = [0]

            def side():
                b = mods[0]
                if b < NMODB:
                    if b >= 2:
                        wait_chunk(act, f"modT{b-2}")
                    if st["s"]:
                        ahead(f"mod{b}")
                    wait_chunk(act, f"mod{b}")
                    act.activation(modrow[:, b % 2, :], bank(f"mod{b}"), ACT.Copy).then_inc(act_free, 1)
                mods[0] = b + 1

            for b in range(FIRST_MOD + 1):
                side()
                if b < 2:
                    for l in range(2):
                        act.wait_ge(filt_d, 1 + 4 * b + l)
                        r = filter_work(l, (384, 640)[b], S)
                        act.activation(r, r, ACT.Sin).then_inc(filt_a, 1)
                if b == 0:
                    for l in range(2):
                        act.wait_ge(filt_d, 3 + l)
                        W = FILTER_AT[l]
                        for t in range(2):
                            ins = act.activation(view(W["E"], 2, 1024)[:, t, :], arena[:, W["w"] + 1024:W["w"] + 2048],
                                                 ACT.Exp, scale=C("negt", t, t + 1))
                        ins.then_inc(filt_a, 1)

            for l, q0, T in LAYERS:
                L = f"L{l}"
                if l == 0:
                    act.wait_ge(streams_in, 32)
                    for n in range(NC):
                        square(xs, view(0, NC, 512), n)
                root(f"{L}.n1", early[:, 3584:4096] if l == 0 else arena[:, 4096:4608])
                his(f"{L}.n1", NC, lambda n: view(0, NC, 512)[:, n, :], lambda n: hH[:, n, :],
                    lambda r, n: x_scale(L, 0, r, n)[1], 2, SPECTRA if l == 0 else ())
                for i in range(KVC):
                    ahead(f"{L}.kv{i}")
                act.wait_ge(spec_out, 32)
                for i in range(KVC):
                    wait_free(act, f"{L}.kv{i}")
                    square(view(15360, KVC, 512), view(4096, KVC, 512), i)
                ahead(f"{L}.kr")
                root(f"{L}.nkv", arena[:, 6656:7168])
                for i in range(QC):
                    ahead(f"{L}.q{i}")
                    if i == 0:
                        his(f"{L}.nkv", KVC, lambda n: view(15360, KVC, 512)[:, n, :],
                            lambda n: view(10240, KVC, 512, F32R)[:, n, :])
                    if l == 0:
                        side()
                for i in range(QC):
                    wait_free(act, f"{L}.q{i}")
                    square(view(8192, QC, T), view(5120, QC, T), i)
                root(f"{L}.nq", arena[:, 7168:7168 + T])
                his(f"{L}.nq", QC, lambda n: view(8192, QC, T)[:, n, :],
                    lambda n: view(12288, QC, T, F32R)[:, n, :])
                kT = view(0, NH, 512)
                for i in range(4):
                    evac(f"{L}.uk{i}",
                         lambda o: act.activation(kT[0:64, 2 * i, :], o[0:64, :], ACT.Copy),
                         lambda o: act.activation(kT[0:64, 2 * i + 1, :], o[64:128, :], ACT.Copy))
                act.wait_ge(nlo_ready, split_at(f"{L}.nq", QC))
                for i in range(4):
                    evac(f"{L}.uv{i}", lambda o: act.activation(view(8192, 4, 512)[:, i, :], o, ACT.Copy))
                for h in range(NH):
                    ahead(f"{L}.uq{h}")
                    if l == 0 and h % 2:
                        side()
                attention(L, T // P, SCALE, view(10240, 4, T, F32R))

                for c in range(HYC):
                    for v in range(3):
                        ahead(f"{L}.hy{c}{v}")
                        wait_chunk(act, f"{L}.hy{c}{v}")
                    side()
                for s in range(T // S):
                    evac(f"{L}.z{s}0", lambda o: act.activation(view(ZROW[s], 2, 512)[:, 0, :], o, ACT.Copy))
                for s in range(T // S):
                    if s:
                        act.wait_ge(Y_ready, 1)
                    for f in range(4):
                        evac(f"{L}.Z{s}{f}", lambda o: act.activation(view(14336, 4, 512)[:, f, :], o, ACT.Copy))
                for s in range(T // S):
                    u = (0 if l == 0 else 2) + s
                    act.wait_ge(o_ready, u + 1)
                    act.activation(view(0, HYC, T, F32R)[:, :, s * S:(s + 1) * S], view(9216, HYC, S), ACT.Copy)\
                       .then_inc(hyhi_ready, 1)
                act.wait_ge(hylo_ready, (2, 3)[l])
                for n in range(NC):
                    merge(L, n, T, view(8192, 2, T), view(9216, 2, T))
                    side()
                act.wait_ge(m_ready, l + 1)
                for k in range(NC):
                    act.activation(hH[:, k, q0:q0 + T], view(4096, NC, T)[:, k, :], ACT.Copy).then_inc(mhi_ready, 1)
                for n in range(NC):
                    ahead(f"{L}.o{n}")
                    if n:
                        wait_free(act, f"{L}.o{n-1}")
                        square(xs[:, :, q0:q0 + T], view(0, NC, T), n - 1)
                    wait_chunk(act, f"{L}.o{n}")
                ahead(f"{L}.n2")
                wait_free(act, f"{L}.o{NC-1}")
                square(xs[:, :, q0:q0 + T], view(0, NC, T), NC - 1)
                root(f"{L}.n2", arena[:, 4096:4096 + T])
                if l == 0:
                    his(f"{L}.n2", NC, lambda n: view(0, NC, T)[:, n, :], lambda n: hH[:, n, q0:q0 + T],
                        lambda r, n: x_scale(L, 1, r, n)[1], 2)
                if l == 1:
                    act.wait_ge(comb_ready, 1)
                    act.activation(small[:, 18:20], small[:, 16:18], ACT.Sigmoid)
                    act.activation(small[:, 20:22], small[:, 16:18], ACT.Sigmoid, scale=-1.0).then_inc(gates_ready, 1)
                    experts()
                else:
                    hid_h = view(FF_AT, HALF, T, F32R)
                    sg = view(FF_AT + 2 * HALF * T, 2, T)
                    h32 = view(FF_AT + 2 * HALF * T + 2 * T, 2, T)

                    def hid_hi(q, f):
                        wait_free(act, f"{L}.ff.{q}.u{f}")
                        act.activation(hid_h[:, f, :], h32[:, f % 2, :], ACT.Copy).then_inc(hidhi_ready, 1)

                    for q in range(2):
                        for f in range(HALF):
                            if f >= 2:
                                wait_free(act, f"{L}.ff.{q}.u{f-2}")
                            evac(f"{L}.ff.{q}.g{f}", lambda o: act.activation(sg[:, f % 2, :], o[:, 0:T], ACT.Silu))
                            ahead(f"{L}.ff.{q}.u{f}")
                            if f:
                                hid_hi(q, f - 1)
                            side()
                        hid_hi(q, HALF - 1)
                        for n in range(NC):
                            ahead(f"{L}.ff.{q}.d{n}")
                            if q and n:
                                wait_free(act, f"{L}.ff.1.d{n-1}")
                                square(xs, view(0, NC, 512), n - 1)
                            wait_chunk(act, f"{L}.ff.{q}.d{n}")
                            if q and n % 2:
                                side()
                    while mods[0] <= NMODB:
                        side()
                    ahead("L1.n1")
                    wait_free(act, f"L0.ff.1.d{NC-1}")
                    square(xs, view(0, NC, 512), NC - 1)

            act.wait_ge(dve_free, M["D"] + PASSES * per["D"])
            for n in range(NC):
                square(xs[:, :, S:2 * S], view(0, NC, S), n)
            root("final", arena[:, 4096:4096 + S])
            for j in range(3):
                for n in range(NC):
                    act.wait_ge(norm_ready, norm_at("final" if j == 0 else f"B.post{j-1}", n + 1))
                    square(xs[:, :, S:2 * S], view(0, NC, S), n)
                root(f"B.pre{j}", arena[:, 4096:4096 + S])
                his(f"B.pre{j}", NC, lambda n: view(0, NC, S)[:, n, :], lambda n: hH[:, n, S:2 * S],
                    lambda r, n: mod_at(96 + 24 * j + n, 2))
                if j != 1:
                    feed_forward(f"B.ff{j}", S)
                    for n in range(NC):
                        wait_free(act, f"B.ff{j}.1.d{n}")
                        square(view(0, NC, S), view(2048, NC, S), n)
                else:
                    for n in range(8):
                        evac(f"B.qk{n}", lambda o: act.activation(view(2048, 8, S)[:, n, :], o[:, 0:S], ACT.Copy))
                    for i in range(2):
                        evac(f"B.v{i}", lambda o: act.activation(view(4096, 2, 512)[:, i, :], o, ACT.Copy))
                    attention("B", 2, SCALE2, view(5120, 4, S, F32R))
                    for n in range(NC):
                        ahead(f"B.xr{n}")
                        wait_chunk(act, f"B.xr{n}")
                    for n in range(NC):
                        for at, nm, bn in ((7168, "ra", "ba"), (9216, "rx", "bx")):
                            evac(f"B.{nm}{n}", lambda o: act.activation(
                                view(at, NC, S)[:, n, :], o[:, 0:S], ACT.Sigmoid, bias=Vv(bn, n, n + 1)))
                    act.wait_ge(lru_d, 2)
                    act.activation(view(11264, NC, S), view(7168, NC, S), ACT.Exp)
                    act.activation(view(15360, NC, S), view(7168, NC, S), ACT.Tanh).then_inc(lru_a, 1)
                    for n in range(NC):
                        if n == 3:
                            act.wait_ge(lru_d, 3)
                            act.activation(view(7168, NC, S), view(7168, NC, S), ACT.Sqrt).then_inc(lru_a, 1)
                        evac(f"B.yr{n}", lambda o: act.activation(view(0, NC, S)[:, n, :], o[:, 0:S],
                                                                  ACT.Gelu_apprx_tanh))
                    act.wait_ge(lru_d, 5)
                    act.activation(view(2048, NC, S, F32R), view(11264, NC, S), ACT.Copy).then_inc(lru_a, 1)
                    for n in range(NC):
                        merge("B", n, S, view(15360, 2, S), view(15872, 2, S))
                    act.wait_ge(m_ready, 3)
                    for k in range(NC):
                        act.activation(hH[:, k, S:2 * S], view(13312, NC, S)[:, k, :], ACT.Copy).then_inc(mhi_ready, 1)
                    for n in range(NC):
                        ahead(f"B.o{n}")
                        if n:
                            wait_free(act, f"B.o{n-1}")
                            square(view(0, NC, S), view(2048, NC, S), n - 1)
                        wait_chunk(act, f"B.o{n}")
                    ahead("B.post1")
                    wait_free(act, f"B.o{NC-1}")
                    square(view(0, NC, S), view(2048, NC, S), NC - 1)
                root(f"B.post{j}", arena[:, 4096:4096 + S])

        @block.vector
        def _(dve):
            chain = [0]

            def link(ins):
                chain[0] += 1
                ins.then_inc(d_link, 1)
                dve.wait_ge(d_link, chain[0])

            def split_lo(s):
                dve.wait_ge(hi_ready, s + 1)
                dve.tensor_tensor(wlo[:, s % SPL, :], raw[:, load_no(s) % RAW, :], whi[:, s % SPL, :].bitcast(F32),
                                  ALU.subtract).then_inc(lo_ready, 1)

            ahead, st = splitter(split_lo)

            def evac(name, *ops):
                ahead(name)
                wait_chunk(dve, name)
                for i, op in enumerate(ops):
                    ins = op(bank(name))
                    if i < len(ops) - 1:
                        link(ins)
                ins.then_inc(dve_free, 1)

            def norm(label, dim, T, rst, n_of, src, gain, shift, h32, lo, hi, full=False):
                variance(label, dim, T, rst)
                normalise(label, T, rst, n_of, src, gain, shift, h32, lo, hi, full)

            def variance(label, dim, T, rst):
                evac(label, lambda o: dve.tensor_scalar(rst, o[:, 0:T], 1.0 / dim, EPS, ALU.mult, ALU.add))

            def normalise(label, T, rst, n_of, src, gain, shift, h32, lo, hi, full=False):
                dve.wait_ge(std_ready, NORMS.index(label) + 1)
                link(dve.reciprocal(rst, rst))
                streams = 1 if shift is None else T // S
                added = shift is not None and full

                def low(n):
                    dve.wait_ge(nhi_ready, split_at(label, n + 1))
                    if shift is None or full:
                        ins = dve.tensor_tensor(lo(n), h32(n), hi(n).bitcast(F32), ALU.subtract)
                    else:
                        for r in range(streams):
                            c = slice(r * S, (r + 1) * S)
                            ins = dve.scalar_tensor_tensor(out=lo(n)[:, c], in0=h32(n)[:, c], scalar=shift(r, n),
                                                           in1=hi(n)[:, c].bitcast(F32), op0=ALU.add, op1=ALU.subtract)
                    ins.then_inc(nlo_ready, 1)

                for n in range(n_of):
                    w = T // streams
                    for r in range(streams):
                        c = slice(r * w, (r + 1) * w)
                        ins = dve.scalar_tensor_tensor(out=h32(n)[:, c], in0=src(n)[:, c], scalar=gain(r, n),
                                                       in1=rst[:, c], op0=ALU.mult, op1=ALU.mult)
                    if added:
                        link(ins)
                        for r in range(streams):
                            c = slice(r * w, (r + 1) * w)
                            ins = dve.tensor_scalar(h32(n)[:, c], h32(n)[:, c], shift(r, n), None, ALU.add)
                    ins.then_inc(norm_ready, 1)
                    if lo is not None and n:
                        low(n - 1)
                if lo is not None:
                    low(n_of - 1)

            def rope(name, T, at, dst, head, rest):
                ta, tb = arena[64:96, 16384:16384 + T], arena[64:96, 16896:16896 + T]
                w = slice(512 - T, 512) if T < 512 else slice(0, 512)
                ops = [lambda o: dve.tensor_copy(dst[0:64, head, :], o[0:64, 0:T])] if rest else []
                ahead(name)
                wait_chunk(dve, name)
                o = bank(name)
                if rest:
                    dve.tensor_copy(dst[0:64, head, :], o[0:64, 0:T])
                dve.tensor_tensor(ta, o[64:96, 0:T], C("cos")[64:96, w], ALU.mult)
                dve.tensor_tensor(tb, o[96:128, 0:T], C("sin")[96:128, w], ALU.mult).then_inc(dve_free, 1)
                wait_free(dve, name)
                dve.tensor_tensor(dst[64:96, head, :], ta, tb, ALU.add).then_inc(rope_ready, 1)
                dve.wait_ge(rope_ready, at)

            def attention(l, tiles, scale, oh, ol):
                items = attention_order(l, tiles)
                n = len(items)
                B = l == "B"
                pb = view(7168, 4, S) if B else view(14336, 2, 512)
                bias = view(9216, 16, S)

                def keys(i):
                    return (items[i][1] + 1) * P if B else S if l == "L0" and items[i][1] < 2 else 2 * S

                def maxima(i):
                    hp, qt, hh = items[i]
                    nk, j = keys(i), i % 2
                    wait_chunk(dve, f"{l}.S{i}")
                    s = bank(f"{l}.S{i}")[:, 0:nk]
                    if B:
                        if i >= 4:
                            wait_chunk(dve, f"B.PT{i-4}")
                        dve.scalar_tensor_tensor(out=pb[:, i % 4, 0:nk], in0=s, scalar=scale,
                                                 in1=bias[:, qt * NH + 2 * hp + hh, 0:nk], op0=ALU.mult, op1=ALU.add)\
                           .then_inc(dve_free, 1)
                        wait_free(dve, f"B.S{i}")
                        link(dve.memset(pb[0:64, i % 4, nk - 64:nk], -3.4028234663852886e38))
                        s = pb[:, i % 4, 0:nk]
                    link(dve.tensor_reduce(small[:, 4 + j:5 + j], s, AX.X, ALU.max))
                    dve.tensor_scalar(small[:, j:j + 1], small[:, 4 + j:5 + j], -1.0 if B else -scale, None, ALU.mult)\
                       .then_inc(nmax_ready, 1)

                def probs(i):
                    j = i % 2
                    if B:
                        dve.wait_ge(exp_ready, i + 1)
                    else:
                        wait_free(dve, f"{l}.S{i}")
                    link(dve.reciprocal(small[:, 6 + j:7 + j], small[:, 2 + j:3 + j]))
                    b = i % (4 if B else 2)
                    dve.tensor_scalar(pb[:, b, 0:keys(i)], pb[:, b, 0:keys(i)], small[:, 6 + j:7 + j], None, ALU.mult)\
                       .then_inc(prob_ready, 1)

                maxima(0)
                maxima(1)
                for i in range(n + 1):
                    if i < n:
                        probs(i)
                    if i + 2 < n:
                        maxima(i + 2)
                    if i >= 1 and (i - 1) % 2 == 1:
                        hp, qt, _ = items[i - 1]
                        o = f"{l}.O{(i-1)//2}"
                        dve.wait_ge(ohi_ready, (ATTN[l] + i) // 2)
                        c = slice(qt * P, (qt + 1) * P)
                        dve.tensor_tensor(ol[:, hp, c], bank(o)[:, 0:P], oh[:, hp, c].bitcast(F32), ALU.subtract)\
                           .then_inc(dve_free, 1)

            def sine_argument(name, l, i, at, tmp):
                x, k = filter_work(l, at, S), filter_work(l, tmp, S)
                evac(name, lambda o: dve.tensor_scalar(x, o[0:FH, 0:S], Vv(f"fb{i}{l}")[0:FH, :], Vv(f"freq{l}")[0:FH, :],
                                                       ALU.add, ALU.mult))
                wait_free(dve, name)
                big = 1.5 * 2 ** 23
                link(dve.tensor_scalar(k, x, 1 / (2 * math.pi), big, ALU.mult, ALU.add))
                link(dve.tensor_scalar(k, k, big, None, ALU.subtract))
                link(dve.scalar_tensor_tensor(out=x, in0=k, scalar=-6.28125, in1=x, op0=ALU.mult, op1=ALU.add))
                link(dve.scalar_tensor_tensor(out=x, in0=k, scalar=-(2 * math.pi - 6.28125), in1=x, op0=ALU.mult,
                                              op1=ALU.add))
                dve.tensor_scalar(x, x, 3.1415925, -3.1415925, ALU.min, ALU.max).then_inc(filt_d, 1)

            def merge(l, n, T, sga, sgh, mg, tmp, last):
                ahead(f"{l}.ga{n}")
                wait_free(dve, f"{l}.ga{n}")
                evac(f"{l}.ba{n}", lambda o: dve.tensor_tensor(mg[:, n, :], sga[:, n % 2, :], o[:, 0:T], ALU.mult))
                ahead(f"{l}.gh{n}")
                wait_free(dve, f"{l}.gh{n}")
                evac(f"{l}.bh{n}", lambda o: dve.tensor_tensor(tmp, sgh[:, n % 2, :], o[:, 0:T], ALU.mult))
                wait_free(dve, f"{l}.bh{n}")
                ins = dve.tensor_tensor(mg[:, n, :], mg[:, n, :], tmp, ALU.add)
                if last:
                    ins.then_inc(m_ready, 1)
                else:
                    link(ins)

            def merged_low(which, hi, lo, mg):
                for k in range(NC):
                    dve.wait_ge(mhi_ready, which * NC + k + 1)
                    dve.tensor_tensor(lo[:, k, :], mg[:, k, :], hi[:, k, :].bitcast(F32), ALU.subtract)\
                       .then_inc(mlo_ready, 1)

            def feed_forward(name, T, gate, acc, streams):
                L = plan.loops[name]
                assert st["s"] == L["slot"]
                sg = view(FF_AT + 2 * HALF * T, 2, T)
                h32 = view(FF_AT + 2 * HALF * T + 2 * T, 2, T)
                steps = plan.slot_end[L["slot"] + HSLOTS - 1] - L["step"]

                def turn(q):
                    def lo(s):
                        g = NMOD + L["slot"] + s
                        dve.wait_ge(hi_ready, q * HSLOTS + (L["slot"] + s + 1))
                        dve.tensor_tensor(wlo[:, (L["slot"] + s) % SPL, :], raw[:, g % RAW, :],
                                          whi[:, (L["slot"] + s) % SPL, :].bitcast(F32), ALU.subtract)\
                           .then_inc(lo_ready, 1)

                    def mul(f):
                        c = plan.c[L["chunk"] + 2 * f + 1]
                        dve.wait_ge(act_free, q * HA + (L["A"] + f + 1))
                        dve.wait_ge(pe_step, q * steps + c["end"])
                        if f >= 2:
                            dve.wait_ge(hidlo_ready, q * HALF + (L["half"] * HALF + f - 1))
                        dve.tensor_tensor(h32[:, f % 2, :], sg[:, f % 2, :],
                                          ps[:, (L["chunk"] + 2 * f + 1) % BANKS, 0:T], ALU.mult).then_inc(dve_free, 1)

                    for f in range(HALF):
                        lo(2 * f)
                        lo(2 * f + 1)
                        if f >= 1:
                            mul(f - 1)
                    lo(2 * HALF)
                    mul(HALF - 1)
                    nxt = 2 * HALF + 1
                    for n in range(NC):
                        while nxt < min(HSLOTS, 2 * HALF + (HALF * n) // TPS + SPL):
                            lo(nxt)
                            nxt += 1
                        c = plan.c[L["chunk"] + 2 * HALF + n]
                        dve.wait_ge(pe_step, q * steps + c["end"])
                        for r in range(streams):
                            cs = slice(r * S, (r + 1) * S)
                            ins = dve.scalar_tensor_tensor(
                                out=acc(n)[:, cs], in0=ps[:, (L["chunk"] + 2 * HALF + n) % BANKS, cs],
                                scalar=gate(r, n), in1=acc(n)[:, cs], op0=ALU.mult, op1=ALU.add)
                        ins.then_inc(dve_free, 1)
                        dve.wait_ge(dve_free, q * HD + (L["D"] + HALF + n + 1))

                with dve.Fori(0, L["times"]) as q:
                    turn(q)
                st["s"] = L["slot"] + HSLOTS * L["times"]

            def route(hf):
                lg, top = small[:, 24:32], small[:, 32:40]
                cmb, chosen, before = small[:, 40:56], small[:, 64:80], small[:, 80:96]
                for t in range(2):
                    evac(f"route{t}", lambda o: dve.tensor_copy(lg, o[:, 0:NE]))
                    wait_free(dve, f"route{t}")
                    link(dve.max(top, lg))
                    link(dve.max_index(idx[:, :], top, lg))
                    link(dve.tensor_copy(small[:, 12 + 2 * t:14 + 2 * t], idx[:, 0:2]))
                    ins = dve.tensor_tensor(small[:, 16 + t:17 + t], top[:, 0:1], top[:, 1:2], ALU.subtract)
                    if t == 1:
                        ins.then_inc(comb_ready, 1)
                    else:
                        link(ins)
                dve.wait_ge(gates_ready, 1)
                for t in range(2):
                    i0, i1 = small[:, 12 + 2 * t:13 + 2 * t], small[:, 13 + 2 * t:14 + 2 * t]
                    dve.tensor_scalar(lg, C("iota"), i0, None, ALU.is_equal)
                    link(dve.tensor_scalar(top, C("iota"), i1, None, ALU.is_equal))
                    link(dve.tensor_tensor(chosen[:, 8 * t:8 * t + 8], lg, top, ALU.add))
                    link(dve.tensor_scalar(lg, lg, small[:, 18 + t:19 + t], None, ALU.mult))
                    link(dve.scalar_tensor_tensor(out=cmb[:, 8 * t:8 * t + 8], in0=top, scalar=small[:, 20 + t:21 + t],
                                                  in1=lg, op0=ALU.mult, op1=ALU.add))
                dve.tensor_copy(small[:, 22:23], small[:, 21:22]).then_inc(comb_ready, 1)
                hrow = arena[:, 2048:4096].rearrange("p (i w) -> p i w", i=4)
                for i in range(4):
                    evac(f"hr{i}", lambda o: dve.tensor_copy(hrow[:, i, :], o))
                cnt = small[:, 24:32]
                evac("pos", lambda o: dve.tensor_copy(before, o[:, 0:16]), lambda o: dve.tensor_copy(cnt, o[:, 16:24]))
                wait_free(dve, "pos")
                link(dve.scalar_tensor_tensor(out=before, in0=before, scalar=1.0, in1=chosen, op0=ALU.add, op1=ALU.mult))
                p3 = ptab[:, 0:NE, :].rearrange("p e t -> p t e")
                w3 = wtab[:, 0:NE, :].rearrange("p e t -> p t e")
                b3, c3 = (v.rearrange("p (t e) -> p t e", t=2) for v in (before, cmb))
                dve.tensor_scalar(p3, b3, -1.0, None, ALU.add)
                link(dve.tensor_copy(w3, c3))
                over, upto = cnt, small[:, 32:40]
                link(dve.tensor_scalar(over, cnt, float(CAP), None, ALU.is_gt))
                link(dve.tensor_tensor_scan(upto, ones[:, 0:NE], over, 0.0, ALU.mult, ALU.add))
                link(dve.tensor_tensor(upto, upto, over, ALU.subtract))
                for j in range(EXTRA):
                    one = picks[:, 8 * j:8 * j + 8]
                    ins = dve.scalar_tensor_tensor(out=one, in0=upto, scalar=float(j), in1=over, op0=ALU.is_equal,
                                                   op1=ALU.mult)
                link(ins)
                for j in range(EXTRA):
                    one = picks[:, 8 * j:8 * j + 8]
                    dve.tensor_tensor(picked[:, j, 0, :], one, C("iota"), ALU.mult)
                    for t in range(2):
                        dve.tensor_tensor(picked[:, j, 1 + t, :], before[:, 8 * t:8 * t + 8], one, ALU.mult)
                        ins = dve.tensor_tensor(picked[:, j, 3 + t, :], cmb[:, 8 * t:8 * t + 8], one, ALU.mult)
                link(ins)
                for j in range(EXTRA):
                    dve.tensor_reduce(etab[:, 4 + j:5 + j], picks[:, 8 * j:8 * j + 8], AX.X, ALU.add)
                    dve.tensor_reduce(etab[:, j:j + 1], picked[:, j, 0:1, :], AX.X, ALU.add)
                    dve.tensor_reduce(ptab[:, NE + j, :], picked[:, j, 1:3, :], AX.X, ALU.add)
                    ins = dve.tensor_reduce(wtab[:, NE + j, :], picked[:, j, 3:5, :], AX.X, ALU.add)
                link(ins)
                link(dve.tensor_scalar(ptab[:, NE:PASSES, :], ptab[:, NE:PASSES, :], -1.0 - CAP, None, ALU.add))
                dve.tensor_copy(passes_i[0:1, :], etab[0:1, :]).then_inc(table_ready, 1)

            ptab = arena[:, 14848:14848 + 2 * PASSES].rearrange("p (q t) -> p q t", t=2)
            wtab = arena[:, 14912:14912 + 2 * PASSES].rearrange("p (q t) -> p q t", t=2)
            etab, picks = arena[:, 14976:14984], arena[:, 14984:14984 + 8 * EXTRA]
            picked = arena[:, 15104:15104 + 40 * EXTRA].rearrange("p (j v e) -> p j v e", v=5, e=NE)

            def experts():
                xh, xlo = view(4864, NC, P, F32R), view(5888, NC, P, F32R)
                sg, hid32 = view(6912, 2, 256), view(7424, 2, 256)
                hh, hl = view(7936, 2 * GB, P, F32R), view(10752, 2 * GB, P, F32R)
                sel, selw = view(4096, 2, P), view(4352, 2, P)
                places = arena[:, 14720:14848]
                assert st["s"] == M["slot"]
                dve.wait_ge(rt_in, 16)

                def one(q, expert):
                    def lo(s):
                        r = (M["slot"] + s) % SPL
                        dve.wait_ge(hi_ready, q * PSLOTS + (M["slot"] + s + 1))
                        e = M["ends"][s + 1 - SPL] if s >= SPL - 1 else M["ends"][PSLOTS + s + 1 - SPL] - per["step"]
                        dve.wait_ge(pe_step, q * per["step"] + (M["step"] + e))
                        dve.tensor_tensor(wlo[:, r, :], raw[:, (NMOD + M["slot"] + s) % RAW, :],
                                          whi[:, r, :].bitcast(F32), ALU.subtract).then_inc(lo_ready, 1)

                    def turned(b):
                        dve.wait_ge(hthi_ready, q * GB + (b + 1))
                        dve.tensor_tensor(hl[:, 2 * b:2 * b + 2, :], pass_bank(f"HT{b}")[:, 0:2 * P]
                                          .rearrange("p (j t) -> p j t", j=2), hh[:, 2 * b:2 * b + 2, :].bitcast(F32),
                                          ALU.subtract).then_inc(dve_free, 1)

                    for t in range(2):
                        place = arena[:, bass.ds(q * 2 + (14848 + t), 1)]
                        weight = arena[:, bass.ds(q * 2 + (14912 + t), 1)]
                        dve.tensor_scalar(sel[:, t, :], places, place, None, ALU.is_equal)
                        ins = dve.tensor_scalar(selw[:, t, :], places, place, weight, ALU.is_equal, ALU.mult)
                    ins.then_inc(sel_ready, 1)
                    for s in range(SPL - 1):
                        lo(s)
                    for i in range(2):
                        dve.wait_ge(xhi_ready, q * 2 + (i + 1))
                        dve.tensor_tensor(xlo[:, 4 * i:4 * i + 4, :],
                                          pass_bank(f"X{i}").rearrange("p (k t) -> p k t", k=4),
                                          xh[:, 4 * i:4 * i + 4, :].bitcast(F32), ALU.subtract).then_inc(dve_free, 1)
                    lo(SPL - 1)
                    for b in range(GB):
                        for s in range(4 * b + 3, 4 * b + 6):
                            lo(s)
                        dve.wait_ge(silu_ready, q * GB + (b + 1))
                        dve.tensor_tensor(hid32[:, b % 2, :], sg[:, b % 2, :], pass_bank(f"GU{b}")[:, 256:512],
                                          ALU.mult).then_inc(dve_free, 1)
                        lo(4 * b + 6)
                        if b:
                            turned(b - 1)
                    turned(GB - 1)
                    for s in range(4 * GB + 3, PSLOTS):
                        lo(s)
                    pass_chunk(dve, "DB", q)
                    dve.tensor_copy(arena[:, 14080:14592], pass_bank("DB")).then_inc(dve_free, 1)
                    for j in range(4):
                        pass_chunk(dve, f"O{j}", q)
                        for i in range(2):
                            n = 2 * j + i
                            xv = xs[:, n, S:2 * S]
                            ins = dve.scalar_tensor_tensor(out=xv, in0=pass_bank(f"O{j}")[:, i * S:(i + 1) * S],
                                                           scalar=mod_at(48 + 40 + n, 1), in1=xv, op0=ALU.mult,
                                                           op1=ALU.add)
                        ins.then_inc(dve_free, 1)

                def skip(q):
                    for sem_, n, base in ((lo_ready, PSLOTS, M["slot"]), (sel_ready, 1, 0),
                                          (dve_free, per["D"], M["D"])):
                        dve.wait_ge(sem_, q * n + base)
                        dve.sem_inc(sem_, n)

                all_passes(dve, one, skip)
                st["s"] = M["slot"] + PASSES * PSLOTS

            mods = [0]

            def side():
                b = mods[0] - 1
                if 0 <= b < NMODB:
                    if st["s"]:
                        ahead(f"modT{b}")
                    wait_chunk(dve, f"modT{b}")
                    o = bank(f"modT{b}").rearrange("p (q j r) -> p q r j", q=4, j=4)
                    dve.tensor_reduce(modT[:, 4 * b:4 * b + 4, :], o[:, :, 0:3, :], AX.X, ALU.add).then_inc(dve_free, 1)
                mods[0] += 1

            def add_bias(name, col, n, rs, at=0):
                wait_free(dve, f"modT{(col + n - 1) // 4}")
                for r in rs:
                    m = modT[:, col:col + n, r]
                    ins = dve.tensor_tensor(m, m, Vv(name, at, at + n), ALU.add)
                link(ins)

            def scale_vector(i, col, r, g):
                link(dve.scalar_tensor_tensor(out=dv[:, i, :], in0=modT[:, col:col + NC, r], scalar=1.0, in1=g,
                                              op0=ALU.add, op1=ALU.mult))

            def softplus():
                dve.wait_ge(lam_exp, 1)
                link(dve.tensor_scalar(a, e, 2.0, None, ALU.add))
                link(dve.reciprocal(a, a))
                link(dve.tensor_tensor(a, a, e, ALU.mult))
                link(dve.tensor_tensor(s2, a, a, ALU.mult))
                link(dve.tensor_scalar(acc_, s2, 1 / 15, 1 / 13, ALU.mult, ALU.add))
                for c in (1 / 11, 1 / 9, 1 / 7, 1 / 5, 1 / 3, 1.0):
                    link(dve.tensor_tensor(acc_, acc_, s2, ALU.mult))
                    link(dve.tensor_scalar(acc_, acc_, c, None, ALU.add))
                link(dve.tensor_tensor(acc_, acc_, a, ALU.mult))
                link(dve.scalar_tensor_tensor(out=acc_, in0=acc_, scalar=2.0, in1=dv[:, 13, :], op0=ALU.mult, op1=ALU.add))
                link(dve.tensor_scalar(dv[:, 13, :], acc_, -8.0, None, ALU.mult))

            def late_modulation():
                add_bias("bm1", 48, 48, (0, 1))
                add_bias("bm2", 96, 72, (2,))
                for r in range(2):
                    scale_vector(4 + r, 48 + 8, r, Vv("n11"))
                scale_vector(6, 48 + 32, 1, Vv("n21"))
                for j in range(3):
                    scale_vector(7 + j, 96 + 24 * j + 8, 2, Vv("pre", 8 * j, 8 * j + 8))
                    link(dve.scalar_tensor_tensor(out=dv[:, 10 + j, :], in0=modT[:, 112 + 24 * j:120 + 24 * j, 2],
                                                  scalar=(0.5, 1.0, 0.5)[j], in1=Vv("post", 8 * j, 8 * j + 8),
                                                  op0=ALU.mult, op1=ALU.mult))

            def filters(stage):
                for l in range(2):
                    W = FILTER_AT[l]
                    h = view(W["h"], 4, 512)
                    if stage == 0:
                        sine_argument(f"f{l}.a", l, 1, 384, 640)
                        if l == 1:
                            for W in FILTER_AT:
                                dec = arena[:, W["w"] + 1024:W["w"] + 2048]
                                dve.scalar_tensor_tensor(out=dec, in0=dec, scalar=-1.0, in1=dec, op0=ALU.mult,
                                                         op1=ALU.max).then_inc(filt_d, 1)
                    if stage == 1:
                        sine_argument(f"f{l}.b", l, 2, 640, 384)
                    if stage == 2:
                        dve.wait_ge(filt_a, 3 + l)
                        E = view(W["E"], 4, 512)
                        for t in range(4):
                            evac(f"f{l}.h{t}", lambda o: dve.scalar_tensor_tensor(
                                out=h[:, t, :], in0=o, scalar=C("h1m", t // 2, t // 2 + 1) if t % 2 else 1.0,
                                in1=E[:, t, :], op0=ALU.mult, op1=ALU.mult))
                        wait_free(dve, f"f{l}.h3")
                        dve.scalar_tensor_tensor(out=view(W["w"], 4, 512), in0=h, scalar=-1.0, in1=h, op0=ALU.mult,
                                                 op1=ALU.max).then_inc(filt_d, 1)
                    if stage == 3:
                        at = FILTER_NORM[l]
                        evac(f"f{l}.sum", lambda o: dve.reciprocal(small[:, at:at + HYC], o[:, 0:HYC]))
                        h4 = arena[:, W["h"]:W["h"] + 2048].rearrange("p (t w c) -> p t w c", t=2, w=2)
                        dve.tensor_tensor(view(W["w"], 2, 512), h4[:, :, 0, :], h4[:, :, 1, :], ALU.add)
                        dve.tensor_tensor(view(W["w"] + 1024, 2, 512), h4[:, :, 0, :], h4[:, :, 1, :], ALU.subtract)\
                           .then_inc(filt_d, 1)

            dve.wait_ge(vec_in, 16)
            a, e, s2, acc_ = (small[:, 24 + 8 * i:32 + 8 * i] for i in range(4))
            dve.tensor_scalar(dv[:, 13, :], Vv("lam"), -1.0, 0.0, ALU.mult, ALU.max)
            link(dve.scalar_tensor_tensor(out=a, in0=Vv("lam"), scalar=-1.0, in1=Vv("lam"), op0=ALU.mult, op1=ALU.max))
            dve.tensor_scalar(e, a, -1.0, None, ALU.mult).then_inc(lam_abs, 1)
            dve.wait_ge(filt_in, 16 * 5 * 2)
            dve.wait_ge(consts_in, 16)
            for b in range(FIRST_MOD + 1):
                side()
                filters(b)
            add_bias("bm0", 0, 16, (0, 1))
            for r in range(2):
                scale_vector(r, 8, r, Vv("n10"))

            for l, q0, T in LAYERS:
                L = f"L{l}"
                hf = view(0, NC, 512)
                norm(f"{L}.n1", D, 512, early[:, 3584:4096] if l == 0 else arena[:, 4096:4608], NC, lambda n: xs[:, n, :],
                     lambda r, n: x_scale(L, 0, r, n)[0], lambda r, n: x_scale(L, 0, r, n)[1],
                     lambda n: hf[:, n, :], lambda n: hL[:, n, :], lambda n: hH[:, n, :])
                pkv, pq = view(15360, KVC, 512), view(8192, QC, T)
                for i in range(KVC):
                    evac(f"{L}.kv{i}", lambda o: dve.tensor_copy(pkv[:, i, :], o))
                kT, qT = view(0, NH, 512), view(4096, NH, T)
                for_l = l * (NH + 1)
                rope(f"{L}.kr", 512, for_l + 1, kT, 0, False)
                for h in range(1, NH):
                    ins = dve.tensor_copy(kT[64:96, h, :], kT[64:96, 0, :])
                link(ins)
                rkv, rq = arena[:, 6656:7168], arena[:, 7168:7168 + T]
                dve.wait_ge(spec_out, 32)
                variance(f"{L}.nkv", KV_LORA, 512, rkv)
                normalise(f"{L}.nkv", 512, rkv, KVC, lambda n: pkv[:, n, :], lambda r, n: Vv(f"kvn{l}", n, n + 1), None,
                          lambda n: pkv[:, n, :], lambda n: view(11264, KVC, 512, F32R)[:, n, :],
                          lambda n: view(10240, KVC, 512, F32R)[:, n, :])
                for i in range(QC):
                    evac(f"{L}.q{i}", lambda o: dve.tensor_copy(pq[:, i, :], o[:, 0:T]))
                    if l == 0:
                        side()
                variance(f"{L}.nq", Q_LORA, T, rq)
                normalise(f"{L}.nq", T, rq, QC, lambda n: pq[:, n, :], lambda r, n: Vv(f"qn{l}", n, n + 1), None,
                          lambda n: pq[:, n, :], lambda n: view(12288 + 1536, QC, T, F32R)[:, n, :],
                          lambda n: view(12288, QC, T, F32R)[:, n, :])
                for i in range(4):
                    ahead(f"{L}.uk{i}")
                for i in range(4):
                    ahead(f"{L}.uv{i}")
                for h in range(NH):
                    rope(f"{L}.uq{h}", T, for_l + 2 + h, qT, h, True)
                    if l == 0 and h % 2:
                        side()
                oh, ol = view(10240, 4, T, F32R), view(12288, 4, T, F32R)
                attention(L, T // P, SCALE, oh, ol)

                KF = view(6144, 4, 512)
                zT, x0 = view(0, HYC, T), view(2048, HYC, T)
                U = view(16384, 2, T)
                for c in range(HYC):
                    for v in range(3):
                        dst = x0[:, c, :] if v == 2 else U[:, v, :]
                        d3 = dst.rearrange("p (s t) -> p s t", t=S)
                        w = [Vv(f"sw{l}", 12 * j + 4 * v + c, 12 * j + 4 * v + c + 1) for j in range(3)]
                        bb = Vv(f"sb{l}", 4 * v + c, 4 * v + c + 1)

                        def o3(o):
                            return o[:, 0:T].rearrange("p (s t) -> p s t", t=S)
                        evac(f"{L}.hy{c}{v}",
                             lambda o: dve.tensor_scalar(dst, o[:, 0:T], w[1], bb, ALU.mult, ALU.add),
                             lambda o: dve.scalar_tensor_tensor(out=d3[:, :, 1:S], in0=o3(o)[:, :, 0:S - 1], scalar=w[0],
                                                                in1=d3[:, :, 1:S], op0=ALU.mult, op1=ALU.add),
                             lambda o: dve.scalar_tensor_tensor(out=d3[:, :, 0:S - 1], in0=o3(o)[:, :, 1:S], scalar=w[2],
                                                                in1=d3[:, :, 0:S - 1], op0=ALU.mult, op1=ALU.add))
                        if v == 1:
                            wait_free(dve, f"{L}.hy{c}1")
                            ins = dve.tensor_tensor(zT[:, c, :], U[:, 0, :], U[:, 1, :], ALU.mult)
                            if c == HYC - 1:
                                ins.then_inc(z_ready, 1)
                            else:
                                link(ins)
                    side()
                dve.wait_ge(z_ready, l + 1)
                wait_free(dve, f"{L}.hy{HYC-1}2")
                Z, Y, T1 = view(14336, 4, 512), view(4096, 4, 512), view(9216, 2, 512)
                for s in range(T // S):
                    evac(f"{L}.z{s}1", lambda o: dve.tensor_copy(view(ZROW[s], 2, 512)[:, 1, :], o))
                for s in range(T // S):
                    u = (0 if l == 0 else 2) + s
                    wait_free(dve, f"{L}.Z{s}3")
                    dve.wait_ge(spec_in, 16 * (l + 1))
                    dve.tensor_tensor(T1, Z[:, 2:4, :], KF[:, 2:4, :], ALU.mult)
                    dve.tensor_tensor(Y[:, 2:4, :], Z[:, 0:2, :], KF[:, 2:4, :], ALU.mult)
                    link(dve.tensor_tensor(Y[:, 0:2, :], Z[:, 0:2, :], KF[:, 0:2, :], ALU.mult))
                    link(dve.tensor_tensor(Z[:, 0:2, :], Z[:, 2:4, :], KF[:, 0:2, :], ALU.mult))
                    for t in range(2):
                        dve.scalar_tensor_tensor(out=Y[:, t, :], in0=T1[:, t, :], scalar=C("negm", t, t + 1),
                                                 in1=Y[:, t, :], op0=ALU.mult, op1=ALU.add)
                    link(dve.tensor_tensor(Y[:, 2:4, :], Y[:, 2:4, :], Z[:, 0:2, :], ALU.add))
                    dve.tensor_copy(Y[0:1, 2, :], T1[0:1, 0, :]).then_inc(Y_ready, 1)
                    dve.wait_ge(Y_ready, u + 1)
                    o32, tmp = view(9216, HYC, S), view(8192, 2, S)
                    for c in range(HYC):
                        zc, xc = zT[:, c, s * S:(s + 1) * S], x0[:, c, s * S:(s + 1) * S]
                        link(dve.tensor_scalar(tmp[:, 0, :], zc, Vv(f"hb{l}", c, c + 1), None, ALU.mult))
                        evac(f"{L}.y{s}{c}", lambda o: dve.scalar_tensor_tensor(
                            out=tmp[:, 1, :], in0=o[:, 0:S], scalar=small[:, FILTER_NORM[l] + c:FILTER_NORM[l] + c + 1], in1=tmp[:, 0, :],
                            op0=ALU.mult, op1=ALU.add))
                        wait_free(dve, f"{L}.y{s}{c}")
                        ins = dve.tensor_tensor(o32[:, c, :], tmp[:, 1, :], xc, ALU.mult)
                        if c == HYC - 1:
                            ins.then_inc(o_ready, 1)
                        else:
                            link(ins)
                    dve.wait_ge(hyhi_ready, u + 1)
                    dve.tensor_tensor(view(2048, HYC, T, F32R)[:, :, s * S:(s + 1) * S], o32,
                                      view(0, HYC, T, F32R)[:, :, s * S:(s + 1) * S].bitcast(F32), ALU.subtract)\
                        .then_inc(hylo_ready, 1)
                    dve.wait_ge(hylo_ready, u + 1)
                mg = view(4096, NC, T)
                for n in range(NC):
                    merge(L, n, T, view(8192, 2, T), view(9216, 2, T), mg, arena[:, 14336:14336 + T], n == NC - 1)
                    side()
                merged_low(l, hH[:, :, q0:q0 + T], hL[:, :, q0:q0 + T], mg)
                if l == 0:
                    add_bias("bm0", 16, 32, (0, 1), 16)
                    for r in range(2):
                        scale_vector(2 + r, 32, r, Vv("n20"))
                for n in range(NC):
                    ops = []
                    ahead(f"{L}.o{n}")
                    wait_chunk(dve, f"{L}.o{n}")
                    for s in range(T // S):
                        r = 1 if l == 1 else s
                        xv = xs[:, n, q0 + s * S:q0 + (s + 1) * S]
                        ins = dve.scalar_tensor_tensor(out=xv, in0=bank(f"{L}.o{n}")[:, s * S:(s + 1) * S],
                                                       scalar=mod_at(48 * l + 16 + n, r), in1=xv, op0=ALU.mult,
                                                       op1=ALU.add)
                    ins.then_inc(dve_free, 1)
                hf = view(0, NC, T)
                norm(f"{L}.n2", D, T, arena[:, 4096:4096 + T], NC, lambda n: xs[:, n, q0:q0 + T],
                     lambda r, n: x_scale(L, 1, r + l, n)[0], lambda r, n: x_scale(L, 1, r + l, n)[1],
                     lambda n: hf[:, n, :], None if l else lambda n: hL[:, n, q0:q0 + T],
                     None if l else lambda n: hH[:, n, q0:q0 + T], l == 1)
                if l == 1:
                    route(hf)
                    experts()
                    continue
                sg = view(FF_AT + 2 * HALF * T, 2, T)
                h32 = view(FF_AT + 2 * HALF * T + 2 * T, 2, T)
                for q in range(2):
                    for f in range(HALF):
                        ahead(f"{L}.ff.{q}.g{f}")
                        wait_free(dve, f"{L}.ff.{q}.g{f}")
                        if q * HALF + f >= 2:
                            dve.wait_ge(hidlo_ready, q * HALF + f - 1)
                        evac(f"{L}.ff.{q}.u{f}",
                             lambda o: dve.tensor_tensor(h32[:, f % 2, :], sg[:, f % 2, :], o[:, 0:T], ALU.mult))
                        side()
                    for n in range(NC):
                        ahead(f"{L}.ff.{q}.d{n}")
                        wait_chunk(dve, f"{L}.ff.{q}.d{n}")
                        for s in range(2):
                            xv = xs[:, n, s * S:(s + 1) * S]
                            ins = dve.scalar_tensor_tensor(out=xv, in0=bank(f"{L}.ff.{q}.d{n}")[:, s * S:(s + 1) * S],
                                                           scalar=mod_at(40 + n, s), in1=xv, op0=ALU.mult, op1=ALU.add)
                        ins.then_inc(dve_free, 1)
                        if q and n % 2:
                            side()
                while mods[0] <= NMODB:
                    side()
                late_modulation()
                softplus()
                wait_free(dve, f"{L}.ff.1.d{NC-1}")

            dve.wait_ge(dve_free, M["D"] + PASSES * per["D"])
            xl = lambda n: xs[:, n, S:2 * S]
            norm("final", D, S, arena[:, 4096:4096 + S], NC, xl, lambda r, n: Vv("fg", n, n + 1), None, xl, None, None)
            fh = view(0, NC, S)
            for j in range(3):
                norm(f"B.pre{j}", D, S, arena[:, 4096:4096 + S], NC, xl, lambda r, n: dv[:, 7 + j, n:n + 1],
                     lambda r, n: mod_at(96 + 24 * j + n, 2), lambda n: fh[:, n, :], lambda n: hL[:, n, S:2 * S],
                     lambda n: hH[:, n, S:2 * S])
                if j != 1:
                    dve.wait_ge(nlo_ready, split_at(f"B.pre{j}", NC))
                    link(dve.memset(fh, 0.0))
                    feed_forward(f"B.ff{j}", S, lambda r, n: 1.0, lambda n: fh[:, n, :], 1)
                else:
                    for n in range(8):
                        ahead(f"B.qk{n}")
                    for i in range(2):
                        ahead(f"B.v{i}")
                    dve.wait_ge(blk_in, 32)
                    attention("B", 2, SCALE2, view(5120, 4, S, F32R), view(6144, 4, S, F32R))
                    xc = view(2048, NC, S)
                    for n in range(NC):
                        w = [Vv("cw", 8 * i + n, 8 * i + n + 1) for i in range(4)]

                        def tap(i):
                            return lambda o: dve.scalar_tensor_tensor(
                                out=xc[:, n, i:S], in0=o[:, 0:S - i], scalar=w[3 - i], in1=xc[:, n, i:S],
                                op0=ALU.mult, op1=ALU.add)
                        evac(f"B.xr{n}",
                             lambda o: dve.tensor_scalar(xc[:, n, :], o[:, 0:S], w[3], Vv("cb", n, n + 1), ALU.mult,
                                                         ALU.add), tap(1), tap(2), tap(3))
                    wait_free(dve, f"B.xr{NC-1}")
                    link(dve.tensor_copy(small[:, 90:91], small[:, 8:9]))
                    dve.tensor_copy(small[:, 91:92], small[:, 8:9]).then_inc(lru_d, 1)
                    for n in range(NC):
                        ahead(f"B.ra{n}")
                        ahead(f"B.rx{n}")
                    rr, ii, aa, th = view(7168, NC, S), view(9216, NC, S), view(11264, NC, S), view(15360, NC, S)
                    wait_free(dve, f"B.rx{NC-1}")
                    for n in range(NC):
                        ins = dve.tensor_scalar(rr[:, n, :], rr[:, n, :], dv[:, 13, n:n + 1], None, ALU.mult)
                    ins.then_inc(lru_d, 1)
                    link(dve.tensor_tensor(ii, ii, xc, ALU.mult))
                    dve.wait_ge(lru_a, 1)
                    link(dve.tensor_scalar(rr, th, -1.0, 1.0, ALU.mult, ALU.add))
                    ahead("B.yr0")
                    link(dve.reciprocal(rr, rr))
                    ahead("B.yr1")
                    link(dve.tensor_tensor(rr, rr, th, ALU.mult))
                    ahead("B.yr2")
                    dve.tensor_scalar(rr, rr, -2.0, 0.0, ALU.mult, ALU.max).then_inc(lru_d, 1)
                    dve.wait_ge(lru_a, 2)
                    link(dve.tensor_tensor(rr, rr, ii, ALU.mult))
                    for n in range(NC):
                        if n >= 3:
                            ahead(f"B.yr{n}")
                        ins = dve.tensor_tensor_scan(ii[:, n, :], aa[:, n, :], rr[:, n, :], 0.0, ALU.mult, ALU.add)
                    ins.then_inc(lru_d, 1)
                    dve.wait_ge(lru_d, 4)
                    wait_free(dve, f"B.yr{NC-1}")
                    dve.tensor_tensor(aa, ii, fh, ALU.mult).then_inc(lru_d, 1)
                    dve.wait_ge(lru_a, 3)
                    dve.tensor_tensor(view(7168, NC, S, F32R), aa, view(2048, NC, S, F32R).bitcast(F32),
                                      ALU.subtract).then_inc(lru_d, 1)
                    mg = view(13312, NC, S)
                    for n in range(NC):
                        merge("B", n, S, view(15360, 2, S), view(15872, 2, S), mg, arena[:, 16384:16384 + S],
                              n == NC - 1)
                    merged_low(2, hH[:, :, S:2 * S], hL[:, :, S:2 * S], mg)
                    for n in range(NC):
                        evac(f"B.o{n}", lambda o: dve.tensor_copy(fh[:, n, :], o[:, 0:S]))
                rst, t32 = arena[:, 4096:4096 + S], view(2048, NC, S)
                variance(f"B.post{j}", D, S, rst)
                dve.wait_ge(std_ready, NORMS.index(f"B.post{j}") + 1)
                link(dve.reciprocal(rst, rst))
                for n in range(NC):
                    link(dve.scalar_tensor_tensor(out=t32[:, n, :], in0=fh[:, n, :], scalar=dv[:, 10 + j, n:n + 1],
                                                  in1=rst, op0=ALU.mult, op1=ALU.mult))
                    dve.tensor_tensor(xl(n), xl(n), t32[:, n, :], ALU.add).then_inc(norm_ready, 1)
            dve.wait_ge(norm_ready, norm_at("B.post2", NC))
            dve.tensor_copy(small[:, 92:93], small[:, 8:9]).then_inc(out_ready, 1)

        @block.gpsimd
        def _(pool):
            def hidden_low(name, T):
                L = plan.loops.get(name, dict(times=2, half=0))
                hid_h, hid_l = view(FF_AT, HALF, T, F32R).bitcast(F32), view(FF_AT + HALF * T, HALF, T, F32R)
                h32 = view(FF_AT + 2 * HALF * T + 2 * T, 2, T)
                with pool.Fori(0, L["times"]) as q:
                    for f in range(HALF):
                        pool.wait_ge(hidhi_ready, q * HALF + (L["half"] * HALF + f + 1))
                        pool.tensor_tensor(hid_l[:, f, :], h32[:, f % 2, :], hid_h[:, f, :], ALU.subtract)\
                            .then_inc(hidlo_ready, 1)

            for l in range(2):
                wait_free(pool, f"f{l}.K3")
                E = FILTER_AT[l]["E"]
                pool.dma_start(spectra[l], arena[:, E:E + 2048]).then_inc(spec_out, 16)
            pool.wait_ge(spec_out, 32)
            for l, q0, T in LAYERS:
                wait_free(pool, f"L{l}.O{len(attention_order('', T // P)) // 2 - 1}")
                pool.dma_start(arena[:, 6144:8192], spectra[l]).then_inc(spec_in, 16)
                if l == 0:
                    hidden_low("L0.ff", T)
            wait_free(pool, f"L1.bh{NC-1}")
            pool.dma_start(arena[:, 14592:14848], io["rt"]).then_inc(rt_in, 16)
            hidden_low("B.ff0", S)
            wait_free(pool, f"B.ff0.1.d{NC-1}")
            pool.dma_start(arena[:, 9216:13312], io["bias"]).then_inc(blk_in, 16)
            pool.dma_start(arena[:, 13312:15360], io["lru"]).then_inc(blk_in, 16)
            hidden_low("B.ff2", S)


def _tiles(w):
    k, n = w.shape
    return w.reshape(k // P, P, n // P, P).transpose(2, 0, 1, 3).reshape(-1, P, P)


def _rows(w):
    k, n = w.shape
    return w.reshape(k // P, P, n // P, P).transpose(0, 2, 1, 3).reshape(-1, P, P)


def _cols(v):
    return v.reshape(-1, P).T


def _constants():
    c = np.zeros((P, NCST), np.float32)

    def put(name, a, rows=slice(0, P)):
        at, w = CST[name]
        c[rows, at:at + w] = a
    put("ident", np.eye(P))
    put("ones", 1.0)
    t = np.arange(S)
    f = np.arange(S)
    ang = 2 * np.pi * ((t[:, None] * f[None, :]) % (2 * S)) / (2 * S)
    Fr, Fi = np.cos(ang), -np.sin(ang)
    Fi[:, 0] = (-1.0) ** t
    F = np.concatenate([Fr, Fi], 1)
    put("F", F.reshape(2, P, 2 * S).transpose(1, 0, 2).reshape(P, -1))
    Gr, Gi = 2 * np.cos(ang).T / (2 * S), -2 * np.sin(ang).T / (2 * S)
    Gr[0] = 1 / (2 * S)
    Gi[0] = (-1.0) ** t / (2 * S)
    G = np.concatenate([Gr, Gi], 0)
    put("G", G.reshape(4, P, S).transpose(1, 0, 2).reshape(P, -1))
    alt = np.zeros((P, P))
    alt[:, 0] = 2 * (-1.0) ** np.arange(P)
    put("alt2", alt)
    nf = ROPE // 4
    inv = (np.float32(10000.0) ** (-np.arange(nf, dtype=np.float32) / np.float32(nf))).astype(np.float32)
    r = np.repeat(np.arange(S // 64, dtype=np.float32), 64)
    col = np.tile(np.arange(64, dtype=np.float32), S // 64)
    a = np.concatenate([r[:, None] * inv, col[:, None] * inv], -1)
    cos, sin = np.cos(a).T, np.sin(a).T
    put("cos", np.concatenate([np.ones((ROPE, S)), np.concatenate([cos, cos], 0)], 1), slice(64, 96))
    put("sin", np.concatenate([np.zeros((ROPE, S)), np.concatenate([-sin, sin], 0)], 1), slice(96, 128))
    put("iota", np.arange(NE)[None, :])
    lin = np.linspace(0.0, 1.0, S, dtype=np.float32)
    put("negt", -lin.reshape(2, P).T)
    m = np.ones((P, 2))
    m[0, 0] = 0
    put("mask", m)
    put("negm", -m)
    put("h1m", m)
    bands = (EMB - 1) // 2
    phase = np.float32(2.0 * math.pi / S) * np.arange(S, dtype=np.float32)[:, None] * \
        np.linspace(1e-4, bands - 1, bands, dtype=np.float32)
    emb = np.concatenate([lin[:, None], np.cos(phase), -np.sin(phase)], -1).T
    return c, np.ascontiguousarray(emb, np.float32)


def _lay_out(i):
    f = lambda n: np.asarray(i[n], np.float32)
    tiles = []
    z = lambda k, n: np.zeros((k, n), np.float32)
    half = ROPE // 2

    def swap(w):
        return np.concatenate([w[:, half:], w[:, :half]], 1)

    def ffn(g, u, d):
        out = []
        for h in range(2):
            cs = slice(h * HALF * P, (h + 1) * HALF * P)
            gt, ut = (_tiles(w[:, cs]).reshape(HALF, NC, P, P) for w in (g, u))
            out += [np.stack([gt, ut], 1).reshape(-1, P, P), _tiles(d[cs])]
        return out

    for l in range(2):
        w = f("w_in")[l]
        tiles.append(_tiles(w[:, KV_START:KV_START + KV_LORA]))
        kr = w[:, KV_START + KV_LORA:HY_START]
        tiles.append(_tiles(np.concatenate([z(D, 64), kr, swap(kr)], 1)))
        tiles.append(_tiles(w[:, :Q_LORA]))
        tiles.append(_tiles(f("w_uk")[l]))
        tiles.append(_rows(f("w_uv")[l]))
        uq = f("w_uq")[l].reshape(Q_LORA, NH, QD)
        for h in range(NH):
            tiles.append(_tiles(np.concatenate([uq[:, h], swap(uq[:, h, NOPE:])], 1)))
        hy = _tiles(w[:, HY_START:GATE_START]).reshape(3, HYC, NC, P, P)
        tiles.append(hy.transpose(1, 0, 2, 3, 4).reshape(-1, P, P))
        ga = _tiles(w[:, GATE_START:GATE_START + D]).reshape(NC, NC, P, P)
        gh = _tiles(w[:, GATE_START + D:]).reshape(NC, NC, P, P)
        ba, bh = (_tiles(f(n)[l]).reshape(NC, 4, P, P) for n in ("w_br_attn", "w_br_hy"))
        tiles.append(np.concatenate([ga, ba, gh, bh], 1).reshape(-1, P, P))
        tiles.append(_tiles(f("w_out")[l]))
        if l == 0:
            tiles += ffn(f("ffn_w_gate")[0], f("ffn_w_up")[0], f("ffn_w_down")[0])
        else:
            for e in range(NE):
                g, u = (f(n)[0, e].reshape(NC, P, GB, 2, P).transpose(2, 0, 3, 1, 4)
                        for n in ("moe_w_gate", "moe_w_up"))
                tiles.append(np.concatenate([g, u], 2).reshape(-1, P, P))
                tiles.append(_rows(f("moe_w_down")[0, e]))
    gu = f("ffn1_w_gu_2")[0]
    tiles += ffn(gu[:, :DFF], gu[:, DFF:], f("ffn1_w_down_2")[0])
    w = f("w_in_2")[0]
    tiles.append(_tiles(w[:, :2 * AW]))
    tiles.append(_rows(w[:, 2 * AW:3 * AW]))
    tiles.append(_tiles(w[:, 3 * AW:3 * AW + 2 * D]))
    w = w[:, 3 * AW + 2 * D:]
    ga, gh, bh = (_tiles(m).reshape(NC, NC, P, P) for m in (w[:, :D], w[:, D:], f("w_rec_o_2")[0]))
    ba = _tiles(f("w_att_o_2")[0]).reshape(NC, 4, P, P)
    tiles.append(np.concatenate([ga, ba, gh, bh], 1).reshape(-1, P, P))
    tiles.append(_tiles(f("w_out_2")[0]))
    gu = f("ffn2_w_gu_2")[0]
    tiles += ffn(gu[:, :DFF], gu[:, DFF:], f("ffn2_w_down_2")[0])
    total = sum(t.shape[0] for t in tiles)
    wsplit = np.empty((total // TPS, P, TPS, P), np.float32)
    at = 0
    for t in tiles:
        for s in range(t.shape[0]):
            wsplit[(at + s) // TPS, :, (at + s) % TPS] = t[s]
        at += t.shape[0]

    wm = np.concatenate([f("w_mod")[0], f("w_mod")[1], f("w_ada_2")[0]], 1)
    wmod = np.ascontiguousarray(wm.reshape(NC // 2, 2, P, NMODB, 512).transpose(3, 0, 2, 1, 4)).reshape(NMOD, P, SLOT)

    v = np.zeros((P, NVEC), np.float32)

    def put(name, a, rows=P):
        at, w = VEC[name]
        v[0:rows, at:at + w] = a
    for l in range(2):
        put(f"n1{l}", _cols(f("norm1_g")[l]))
        put(f"n2{l}", _cols(f("norm2_g")[l]))
        put(f"qn{l}", _cols(f("q_norm_g")[l]))
        put(f"kvn{l}", _cols(f("kv_norm_g")[l]))
        put(f"sw{l}", _cols(f("hy_short_w")[l].reshape(-1)))
        put(f"sb{l}", _cols(f("hy_short_b")[l]))
        put(f"hb{l}", _cols(f("hy_bias")[l]))
        put(f"bm{l}", _cols(f("b_mod")[l]))
        put(f"fb1{l}", f("hy_b1")[l][:, None], FH)
        put(f"fb2{l}", f("hy_b2")[l][:, None], FH)
        put(f"freq{l}", f("hy_freq")[l][:, None], FH)
    put("fg", _cols(f("final_g")))
    put("bm2", _cols(f("b_ada_2")[0]))
    put("pre", _cols(f("norm_pre_2")[0].reshape(-1)))
    put("post", _cols(f("norm_post_2")[0].reshape(-1)))
    put("cw", _cols(f("conv_w_2")[0].reshape(-1)))
    put("cb", _cols(f("conv_b_2")[0]))
    put("ba", _cols(f("lru_ba_2")[0]))
    put("bx", _cols(f("lru_bx_2")[0]))
    put("lam", _cols(f("lru_lambda_2")[0]))
    put("router", f("moe_router")[0].reshape(NC, P, NE).transpose(1, 0, 2).reshape(P, -1))
    c3 = np.zeros((P, NC, 32), np.float32)
    for r, n in enumerate(("c_ctx", "c", "c_2")):
        c3[:, :, r] = _cols(f(n).reshape(-1))
    put("c3", c3.reshape(P, -1))
    cst, emb = _constants()
    q = np.arange(S)[:, None] - np.arange(S)[None, :]
    bias = f("rel_bias_2")[0][:, np.clip(q, -MAXREL, MAXREL) + MAXREL]
    bias = bias.reshape(NH, 2, P, S).transpose(2, 1, 0, 3).reshape(P, -1)
    lru = np.zeros((P, NC, 2, P), np.float32)
    for j, n in enumerate(("lru_wa_2", "lru_wx_2")):
        w = f(n)[0]
        for b in range(2 * NC):
            r = slice(64 * (b % 2), 64 * (b % 2) + 64)
            lru[r, b // 2, j, r] = w[b]
    return {
        "wsplit": wsplit.reshape(total // TPS, P, SLOT), "wmod": wmod, "vec": v, "cst": cst, "emb": emb,
        "xT": np.ascontiguousarray(f("x")[0].T), "ctxT": np.ascontiguousarray(f("ctx")[0].T),
        "fw1": f("hy_w1"), "fw2": f("hy_w2"), "fw3": f("hy_w3"), "decay": f("hy_decay").reshape(2, 2 * HY),
        "rt": np.concatenate([np.triu(np.ones((P, P), np.float32), 1),
                              np.tile(np.arange(P, dtype=np.float32), (P, 1))], 1),
        "bias": np.ascontiguousarray(bias), "lru": lru.reshape(P, -1),
    }


def kernel(**inputs):
    import concourse.bacc as _bacc
    from concourse.bass_utils import run_bass_kernel_spmd as _run

    nc = _bacc.Bacc("TRN2", target_bir_lowering=False, num_devices=1)
    arrays = {f"in_{k}": np.ascontiguousarray(v) for k, v in _lay_out(inputs).items()}
    io = {k[3:]: nc.dram_tensor(k, a.shape, F32, kind="ExternalInput").ap() for k, a in arrays.items()}
    io["out"] = nc.dram_tensor("out_xT", (D, S), F32, kind="ExternalOutput").ap()
    build(nc, io)
    r = _run(nc, [arrays], core_ids=[0])
    return np.ascontiguousarray(r.results[0]["out_xT"].T)[None]
```
